# Optimizing a Trainium2 kernel written in Bass

```python
import jax, jax.numpy as jnp
from jax import lax
import numpy as np

D_MODEL = 1024
BATCH = 1
SEQ = 1024
DEPTH = 2

GRID_W = 64
CTX_LEN = 256
HEAD_DIM = 64
Q_BLOCK = 128
WINDOW = 128
ROPE_THETA = 10000.0
RMS_EPS = 1e-6
GN_EPS = 64e-5
N_EVEN = (DEPTH + 1) // 2
N_ODD = DEPTH // 2
A_HEADS = D_MODEL // (2 * HEAD_DIM)
A_KV_HEADS = A_HEADS // 4
B_HEADS = D_MODEL // (2 * HEAD_DIM)
B_LORA = 64
A_WIDTH = A_HEADS * HEAD_DIM
A_KV_WIDTH = A_KV_HEADS * HEAD_DIM
B_WIDTH = B_HEADS * HEAD_DIM
B_PROJ = 3 * B_WIDTH + 4 * B_LORA
EVEN_IN = A_WIDTH + 2 * A_KV_WIDTH + B_PROJ + A_WIDTH + B_WIDTH
EVEN_MIX = A_WIDTH + B_WIDTH
C_HEADS = D_MODEL // HEAD_DIM
C_KV_HEADS = C_HEADS // 4
C_WIDTH = C_HEADS * HEAD_DIM
C_KV_WIDTH = C_KV_HEADS * HEAD_DIM
ODD_IN = C_WIDTH + 2 * C_KV_WIDTH + C_WIDTH

kernel_name = 'hybrid_dit_gqa_rwkv7_swa_prefix'

def _rms(x, gain):
    xf = x.astype(jnp.float32)
    xf = xf * lax.rsqrt(jnp.mean(xf * xf, axis=-1, keepdims=True) + RMS_EPS)
    return xf.astype(x.dtype) * gain

def _heads(x, n):
    return x.reshape(x.shape[:-1] + (n, HEAD_DIM))

def _axial_rope(n_tokens, dtype):
    n_rows = n_tokens // GRID_W
    t = jnp.arange(n_rows * GRID_W)
    row = (t // GRID_W).astype(jnp.float32)
    col = (t % GRID_W).astype(jnp.float32)
    axis_dim = HEAD_DIM // 2
    inv = ROPE_THETA ** (-jnp.arange(0, axis_dim, 2, dtype=jnp.float32) / axis_dim)
    ang = jnp.concatenate([row[:, None] * inv, col[:, None] * inv], axis=-1)
    return jnp.cos(ang).astype(dtype), jnp.sin(ang).astype(dtype)

def _rope(x, cos, sin):
    x1, x2 = x[..., 0::2], x[..., 1::2]
    c, s = cos[None, :, None, :], sin[None, :, None, :]
    return jnp.stack([x1 * c - x2 * s, x1 * s + x2 * c], axis=-1).reshape(x.shape)

def _dense_attention(q, k, v):
    B, T, Hq, D = q.shape
    G = k.shape[2]
    R = Hq // G
    nb = T // Q_BLOCK
    scale = HEAD_DIM ** -0.5
    qb = jnp.moveaxis(q.reshape(B, nb, Q_BLOCK, G, R, D), 1, 0)

    def block(qi):
        s = jnp.einsum('bqgrd,bsgd->bgrqs', qi, k).astype(jnp.float32) * scale
        p = jax.nn.softmax(s, axis=-1).astype(v.dtype)
        return jnp.einsum('bgrqs,bsgd->bqgrd', p, v)

    o = lax.map(block, qb)
    return jnp.moveaxis(o, 0, 1).reshape(B, T, Hq * D)

def _window_attention(q, k, v, kc, vc, sink):
    B, T, Hq, D = q.shape
    G = k.shape[2]
    R = Hq // G
    L = kc.shape[1]
    nb = T // Q_BLOCK
    band = 3 * Q_BLOCK
    scale = HEAD_DIM ** -0.5
    pad = ((0, 0), (Q_BLOCK, Q_BLOCK), (0, 0), (0, 0))
    kp, vp = jnp.pad(k, pad), jnp.pad(v, pad)
    sink_b = jnp.broadcast_to(sink.reshape(G, R, 1, 1).astype(jnp.float32), (B, G, R, Q_BLOCK, 1))

    def block(i):
        start = i * Q_BLOCK
        qi = lax.dynamic_slice_in_dim(q, start, Q_BLOCK, axis=1).reshape(B, Q_BLOCK, G, R, D)
        ki = lax.dynamic_slice_in_dim(kp, start, band, axis=1)
        vi = lax.dynamic_slice_in_dim(vp, start, band, axis=1)
        qpos = start + jnp.arange(Q_BLOCK)
        kpos = start - Q_BLOCK + jnp.arange(band)
        mask = (kpos[None, :] >= 0) & (kpos[None, :] < T) & (jnp.abs(kpos[None, :] - qpos[:, None]) <= WINDOW)
        s_loc = jnp.einsum('bqgrd,bkgd->bgrqk', qi, ki).astype(jnp.float32) * scale
        s_loc = jnp.where(mask, s_loc, -jnp.inf)
        s_ctx = jnp.einsum('bqgrd,bmgd->bgrqm', qi, kc).astype(jnp.float32) * scale
        p = jax.nn.softmax(jnp.concatenate([s_loc, s_ctx, sink_b], axis=-1), axis=-1).astype(v.dtype)
        return (jnp.einsum('bgrqk,bkgd->bqgrd', p[..., :band], vi)
                + jnp.einsum('bgrqm,bmgd->bqgrd', p[..., band:band + L], vc))

    o = lax.map(block, jnp.arange(nb))
    return jnp.moveaxis(o, 0, 1).reshape(B, T, Hq * D)

def _context_attention(q, k, v, sink):
    B, L, Hq, D = q.shape
    G = k.shape[2]
    R = Hq // G
    scale = HEAD_DIM ** -0.5
    s = jnp.einsum('blgrd,bmgd->bgrlm', q.reshape(B, L, G, R, D), k).astype(jnp.float32) * scale
    if sink is not None:
        s = jnp.concatenate([s, jnp.broadcast_to(sink.reshape(G, R, 1, 1).astype(jnp.float32), (B, G, R, L, 1))], axis=-1)
    p = jax.nn.softmax(s, axis=-1)[..., :L].astype(v.dtype)
    return jnp.einsum('bgrlm,bmgd->blgrd', p, v).reshape(B, L, Hq * D)

def _rwkv_streams(p, mu, w0, w2, a0, a2, k_k, k_a):
    B, T = p.shape[:2]
    pp = jnp.pad(p, ((0, 0), (1, 1), (0, 0)))
    p = p + mu * (0.5 * (pp[:, :-2] + pp[:, 2:]) - p)
    r, k, v, zw, za = jnp.split(p, [B_WIDTH, 2 * B_WIDTH, 3 * B_WIDTH, 3 * B_WIDTH + 2 * B_LORA], axis=-1)
    zw = zw.reshape(B, T, 2, B_LORA)
    za = za.reshape(B, T, 2, B_LORA)
    w_log = -jax.nn.softplus(-(w0[:, None, None, :] + jnp.einsum('btdr,drc->dbtc', jnp.tanh(zw), w2))) - 0.5
    decay = jnp.exp(-jnp.exp(w_log.astype(jnp.float32))).astype(p.dtype)
    a = _heads(jax.nn.sigmoid(a0[:, None, None, :] + jnp.einsum('btdr,drc->dbtc', za, a2)), B_HEADS)
    kkf = _heads(k * k_k, B_HEADS).astype(jnp.float32)
    kk = (kkf / jnp.maximum(jnp.sqrt(jnp.sum(kkf * kkf, axis=-1, keepdims=True)), 1e-12)).astype(p.dtype)
    kmod = _heads(k, B_HEADS)[None] * (1 + (a - 1) * _heads(k_a, B_HEADS))
    return _heads(r, B_HEADS), _heads(decay, B_HEADS), kk, kk[None] * a, kmod, _heads(v, B_HEADS)

def _rwkv_bidir_scan(r, decay, kk, b, kmod, v, state0):
    def time_major(x):
        return jnp.moveaxis(jnp.stack([x[0], jnp.flip(x[1], axis=1)], axis=0), 2, 0)

    def both(x):
        return jnp.broadcast_to(x[None], (2,) + x.shape)

    xs = (time_major(both(r)), time_major(decay), time_major(both(kk)),
          time_major(b), time_major(kmod), time_major(both(v)))

    def step(S, inp):
        r_t, w_t, kk_t, b_t, k_t, v_t = inp
        S = (S * w_t[..., None, :]
             - jnp.einsum('dbhvk,dbhk->dbhv', S, kk_t)[..., None] * b_t[..., None, :]
             + v_t[..., None] * k_t[..., None, :])
        return S, jnp.einsum('dbhvk,dbhk->dbhv', S, r_t)

    S, y = lax.scan(step, state0, xs)
    y = jnp.moveaxis(y, 0, 2)
    return jnp.stack([y[0], jnp.flip(y[1], axis=1)], axis=0), S

def _rwkv_readout(y, r, kmod, v, rk, gn_w, gn_b):
    yf = y.astype(jnp.float32)
    mean = jnp.mean(yf, axis=-1, keepdims=True)
    var = jnp.mean(jnp.square(yf - mean), axis=-1, keepdims=True)
    yn = ((yf - mean) * lax.rsqrt(var + GN_EPS)).astype(y.dtype) * gn_w + gn_b
    bonus = jnp.sum(r[None] * kmod * rk, axis=-1, keepdims=True) * v[None]
    o = jnp.sum(yn + bonus, axis=0)
    return o.reshape(o.shape[:2] + (B_WIDTH,))

def _even_mixer(hx, hc, cos, sin, need_ctx, w_in, w_out, qn, kn, mu, w0, w2, a0, a2, k_k, k_a, rk, gn_w, gn_b):
    cuts = np.cumsum([A_WIDTH, A_KV_WIDTH, A_KV_WIDTH, B_PROJ, A_WIDTH]).tolist()
    qx, kx, vx, bx, gax, gbx = jnp.split(hx @ w_in, cuts, axis=-1)
    qc, kc, vc, bc, gac, gbc = jnp.split(hc @ w_in, cuts, axis=-1)
    qx = _rope(_rms(_heads(qx, A_HEADS), qn), cos, sin)
    kx = _rope(_rms(_heads(kx, A_KV_HEADS), kn), cos, sin)
    kc = _rms(_heads(kc, A_KV_HEADS), kn)
    vx, vc = _heads(vx, A_KV_HEADS), _heads(vc, A_KV_HEADS)
    oa_x = _dense_attention(qx, jnp.concatenate([kx, kc], axis=1), jnp.concatenate([vx, vc], axis=1))
    gn_w, gn_b = gn_w.reshape(B_HEADS, HEAD_DIM), gn_b.reshape(B_HEADS, HEAD_DIM)
    r_c, d_c, kk_c, b_c, km_c, v_c = _rwkv_streams(bc, mu, w0, w2, a0, a2, k_k, k_a)
    r_x, d_x, kk_x, b_x, km_x, v_x = _rwkv_streams(bx, mu, w0, w2, a0, a2, k_k, k_a)
    state0 = jnp.zeros((2, hx.shape[0], B_HEADS, HEAD_DIM, HEAD_DIM), hx.dtype)
    y_c, state_c = _rwkv_bidir_scan(r_c, d_c, kk_c, b_c, km_c, v_c, state0)
    y_x, _ = _rwkv_bidir_scan(r_x, d_x, kk_x, b_x, km_x, v_x, state_c)
    ob_x = _rwkv_readout(y_x, r_x, km_x, v_x, rk, gn_w, gn_b)
    out_x = jnp.concatenate([oa_x * jax.nn.silu(gax), ob_x * jax.nn.silu(gbx)], axis=-1) @ w_out
    if not need_ctx:
        return out_x, None
    oa_c = _context_attention(_rms(_heads(qc, A_HEADS), qn), kc, vc, None)
    ob_c = _rwkv_readout(y_c, r_c, km_c, v_c, rk, gn_w, gn_b)
    out_c = jnp.concatenate([oa_c * jax.nn.silu(gac), ob_c * jax.nn.silu(gbc)], axis=-1) @ w_out
    return out_x, out_c

def _odd_mixer(hx, hc, cos, sin, need_ctx, w_in, w_out, qn, kn, sink):
    cuts = np.cumsum([C_WIDTH, C_KV_WIDTH, C_KV_WIDTH]).tolist()
    qx, kx, vx, gx = jnp.split(hx @ w_in, cuts, axis=-1)
    if need_ctx:
        qc, kc, vc, gc = jnp.split(hc @ w_in, cuts, axis=-1)
    else:
        kc, vc = jnp.split(hc @ w_in[:, C_WIDTH:C_WIDTH + 2 * C_KV_WIDTH], 2, axis=-1)
    qx = _rope(_rms(_heads(qx, C_HEADS), qn), cos, sin)
    kx = _rope(_rms(_heads(kx, C_KV_HEADS), kn), cos, sin)
    kc = _rms(_heads(kc, C_KV_HEADS), kn)
    vc = _heads(vc, C_KV_HEADS)
    ox = _window_attention(qx, kx, _heads(vx, C_KV_HEADS), kc, vc, sink)
    out_x = (ox * jax.nn.silu(gx)) @ w_out
    if not need_ctx:
        return out_x, None
    oc = _context_attention(_rms(_heads(qc, C_HEADS), qn), kc, vc, sink)
    return out_x, (oc * jax.nn.silu(gc)) @ w_out

def setup_inputs(seed: int = 0) -> dict:
    key = jax.random.key(seed)
    ks = jax.random.split(key, 27)
    f32 = jnp.float32
    D = D_MODEL

    def nrm(k, shape, s):
        return jax.random.normal(k, shape, f32) * s

    return {
        'x': nrm(ks[0], (BATCH, SEQ, D), 1.0),
        'c': nrm(ks[1], (BATCH, D), 1.0),
        'ctx': nrm(ks[2], (BATCH, CTX_LEN, D), 1.0),
        'c_ctx': nrm(ks[3], (D,), 1.0),
        'w_mod': nrm(ks[4], (DEPTH, D, 3 * D), 0.5 * D ** -0.5),
        'b_mod': nrm(ks[5], (DEPTH, 3 * D), 0.01),
        'g_pre': 1.0 + nrm(ks[6], (DEPTH, D), 0.05),
        'g_post': 1.0 + nrm(ks[7], (DEPTH, D), 0.05),
        'w_in_even': nrm(ks[8], (N_EVEN, D, EVEN_IN), D ** -0.5),
        'w_out_even': nrm(ks[9], (N_EVEN, EVEN_MIX, D), EVEN_MIX ** -0.5),
        'qn_a': 1.0 + nrm(ks[10], (N_EVEN, HEAD_DIM), 0.05),
        'kn_a': 1.0 + nrm(ks[11], (N_EVEN, HEAD_DIM), 0.05),
        'mu_b': jax.random.uniform(ks[12], (N_EVEN, B_PROJ), f32, 0.1, 0.9),
        'w0_b': nrm(ks[13], (N_EVEN, 2, B_WIDTH), 0.5),
        'w2_b': nrm(ks[14], (N_EVEN, 2, B_LORA, B_WIDTH), B_LORA ** -0.5),
        'a0_b': nrm(ks[15], (N_EVEN, 2, B_WIDTH), 0.5),
        'a2_b': nrm(ks[16], (N_EVEN, 2, B_LORA, B_WIDTH), B_LORA ** -0.5),
        'kk_b': 0.85 + nrm(ks[17], (N_EVEN, B_WIDTH), 0.05),
        'ka_b': 1.0 + nrm(ks[18], (N_EVEN, B_WIDTH), 0.05),
        'rk_b': nrm(ks[19], (N_EVEN, B_HEADS, HEAD_DIM), 0.1),
        'gn_w_b': 1.0 + nrm(ks[20], (N_EVEN, B_WIDTH), 0.05),
        'gn_b_b': nrm(ks[21], (N_EVEN, B_WIDTH), 0.01),
        'w_in_odd': nrm(ks[22], (N_ODD, D, ODD_IN), D ** -0.5),
        'w_out_odd': nrm(ks[23], (N_ODD, C_WIDTH, D), C_WIDTH ** -0.5),
        'qn_c': 1.0 + nrm(ks[24], (N_ODD, HEAD_DIM), 0.05),
        'kn_c': 1.0 + nrm(ks[25], (N_ODD, HEAD_DIM), 0.05),
        'sink_c': nrm(ks[26], (N_ODD, C_HEADS), 0.5),
    }

def reference(x, c, ctx, c_ctx, w_mod, b_mod, g_pre, g_post, w_in_even, w_out_even, qn_a, kn_a,
              mu_b, w0_b, w2_b, a0_b, a2_b, kk_b, ka_b, rk_b, gn_w_b, gn_b_b,
              w_in_odd, w_out_odd, qn_c, kn_c, sink_c):
    cos, sin = _axial_rope(x.shape[1], x.dtype)
    for l in range(DEPTH):
        need_ctx = l < DEPTH - 1
        mod_x = jax.nn.silu(c) @ w_mod[l] + b_mod[l]
        mod_c = jax.nn.silu(c_ctx) @ w_mod[l] + b_mod[l]
        sh_x, sc_x, gt_x = jnp.split(mod_x[:, None, :], 3, axis=-1)
        sh_c, sc_c, gt_c = jnp.split(mod_c, 3, axis=-1)
        hx = _rms(x, g_pre[l]) * (1 + sc_x) + sh_x
        hc = _rms(ctx, g_pre[l]) * (1 + sc_c) + sh_c
        if l % 2 == 0:
            i = l // 2
            yx, yc = _even_mixer(hx, hc, cos, sin, need_ctx, w_in_even[i], w_out_even[i], qn_a[i], kn_a[i],
                                 mu_b[i], w0_b[i], w2_b[i], a0_b[i], a2_b[i], kk_b[i], ka_b[i], rk_b[i],
                                 gn_w_b[i], gn_b_b[i])
        else:
            j = l // 2
            yx, yc = _odd_mixer(hx, hc, cos, sin, need_ctx, w_in_odd[j], w_out_odd[j], qn_c[j], kn_c[j], sink_c[j])
        x = x + gt_x * _rms(yx, g_post[l])
        if need_ctx:
            ctx = ctx + gt_c * _rms(yc, g_post[l])
    return x


_drawn_inputs = setup_inputs


def setup_inputs(seed=0):
    import zlib

    import numpy as np

    out = dict(_drawn_inputs(seed))
    spreads = {}
    factors = {'g_post': 2.842,
     'qn_a': 8.0,
     'kn_a': 8.0,
     'kk_b': 6.764,
     'ka_b': 2.721,
     'gn_w_b': 4.337,
     'gn_b_b': 8.0,
     'qn_c': 8.0,
     'kn_c': 8.0,
     'sink_c': 8.0}
    for name, (base, spread) in spreads.items():
        noise = np.random.default_rng([zlib.crc32(name.encode()), seed]).standard_normal(out[name].shape)
        drawn = base * np.exp(spread * noise) if base else spread * noise
        out[name] = __import__('jax').numpy.asarray(drawn.astype(out[name].dtype))
    for name, factor in factors.items():
        out[name] = (out[name] * factor).astype(out[name].dtype)
    return out
```

```python
from contextlib import ExitStack

import numpy as np
import concourse.bass as bass
from concourse import mybir

F32 = mybir.dt.float32
F32R = mybir.dt.float32r
ALU = mybir.AluOpType
ACT = mybir.ActivationFunctionType
AX = mybir.AxisListType.X

P = 128
D = 1024
SEQ = 1024
CTX = 256
TOK = SEQ + CTX
NT = TOK // P
NTX = SEQ // P
NTC = CTX // P
KC = D // P
HD = 64
GRID_W = 64
WINDOW = 128
EPS = 1e-6
GN_EPS = 64e-5
AH, AKV = 8, 2
CH, CKV = 16, 4
BW = 512
PAIRS = BW // P
CHUNK = 64
NCH = TOK // CHUNK
BPROJ = 1792
NFC = BPROJ // P
LEVELS = 5
R = 4
SCALE = HD ** -0.5
DECAY = float(np.exp(-0.5))
NEG = -1e30
BLK = 256

C_ID = 0
C_ONES = C_ID + P
C_GRAM = C_ONES + P
C_LEV = C_GRAM + 2 * 2 * P
C_SUM = C_LEV + (LEVELS + 1) * P
C_SEL = C_SUM + HD
C_END = C_SEL + PAIRS * 8


def constant_tables():
    p = np.arange(P)
    s, t = p[:, None], p[None, :]
    same = (s // CHUNK) == (t // CHUNK)
    parts = [np.eye(P), ((s // HD) == (t // HD)) * 1.0]
    for fwd in (True, False):
        parts += [same * ((s <= t) if fwd else (s >= t)), same * ((s < t) if fwd else (s > t))]
    for k in range(LEVELS + 1):
        m = 1 << k
        parts.append(((s // (2 * m)) == (t // (2 * m))) & ((s // m) != (t // m)))
    parts.append(np.vstack([np.eye(HD)] * 2))
    sel = np.zeros((P, PAIRS, 8))
    for i in range(PAIRS):
        for h in range(2):
            sel[h * HD:(h + 1) * HD, i, 2 * i + h] = 1.0
    parts.append(sel.reshape(P, -1))
    table = np.concatenate([np.asarray(x, np.float32) for x in parts], axis=1)
    q, k = p[:, None], np.arange(3 * P)[None, :] - P
    win = np.zeros((NTX, P, 3 * P), np.float32)
    for i in range(NTX):
        pos = k + i * P
        ok = (pos >= 0) & (pos < SEQ) & (np.abs(k - q) <= WINDOW)
        win[i] = np.where(ok, 0.0, NEG)
    tok = np.arange(SEQ)
    inv = (10000.0 ** (-np.arange(0, 32, 2, dtype=np.float32) / np.float32(32))).astype(np.float32)
    ang = np.concatenate([(tok // GRID_W).astype(np.float32)[:, None] * inv,
                          (tok % GRID_W).astype(np.float32)[:, None] * inv], axis=1)
    rope = np.zeros((TOK, 2, 32), np.float32)
    rope[:SEQ, 0], rope[:SEQ, 1] = np.cos(ang), np.sin(ang)
    rope[SEQ:, 0] = 1.0
    return table, win, rope


class Stage:

    def __init__(self, nc, name):
        self.nc, self.name, self.stack, self.signals = nc, name, ExitStack(), []

    def sb(self, name, shape, dt=F32):
        return self.stack.enter_context(self.nc.sbuf_tensor(f"{self.name}_{name}", shape, dt))

    def ps(self, name, shape):
        return self.stack.enter_context(self.nc.psum_tensor(f"{self.name}_{name}", shape, F32))

    def sem(self, name):
        self.signals.append(self.nc.alloc_semaphore(f"{self.name}_{name}"))
        return self.signals[-1]

    def sems(self, *names):
        return [self.sem(n) for n in names]

    def __enter__(self):
        return self

    def __exit__(self, *a):
        self.nc.clear_and_free_semaphores(self.signals)
        self.nc.all_engine_barrier()
        return self.stack.__exit__(*a)


def loop(eng, n, body):
    if n == 1:
        body(0)
    else:
        with eng.Fori(0, n) as i:
            body(i)


def two_slots(eng, n, body):
    def pair(i):
        for s in range(2):
            body(i, s, i * 2 + s)
    if n >= 2:
        loop(eng, n // 2, pair)
    if n % 2:
        body(n // 2, 0, n - 1)


def at(i):
    return bass.ds(i, 1)


def rows(ap, i, n=P):
    return ap[bass.ds(i * n, n)]


def modulation(nc, l, c, c_ctx, w_mod, b_mod, mod):
    NB = 3 * D // 512
    with Stage(nc, f"mod{l}") as st:
        cc = st.sb("cc", [P, 2, KC])
        sg = st.sb("sg", [P, 2, KC])
        sl = st.sb("sl", [P, KC, 2])
        w = st.sb("w", [P, 2, KC, 512])
        bias = st.sb("bias", [2, 3 * D])
        res = st.sb("res", [2, 3 * D])
        acc = [st.ps(f"acc{s}", [P, 512]) for s in range(2)]
        loaded, sig, silu, stored = st.sems("loaded", "sig", "silu", "stored")
        w_in, summed, added = (st.sems(f"{n}0", f"{n}1") for n in ("w_in", "summed", "added"))
        with nc.Block() as block:
            @block.sync
            def _(sp):
                with nc.allow_non_contiguous_dma(reason="one column of 1024 values"):
                    sp.dma_start(cc[:, 0, :], c.rearrange("a (k p) -> p (a k)", p=P)).then_inc(loaded, 16)
                    sp.dma_start(cc[:, 1, :], c_ctx.rearrange("(k p) -> p k", p=P)).then_inc(loaded, 16)
                for r in range(2):
                    sp.dma_start(bias[r:r + 1, :], b_mod[l:l + 1, :]).then_inc(loaded, 16)
                wv = w_mod[l].rearrange("(k p) n -> p k n", p=P)

                def load(i, s, b):
                    sp.wait_ge(summed[s], i)
                    sp.dma_start(w[:, s], wv[:, :, bass.ds(b * 512, 512)]).then_inc(w_in[s], 16)
                two_slots(sp, NB, load)
                for s in range(2):
                    sp.wait_ge(added[s], NB // 2)
                sp.dma_start(mod[l], res[:]).then_inc(stored, 16)
                sp.wait_ge(stored, 16)

            @block.scalar
            def _(act):
                act.wait_ge(loaded, 64)
                act.activation(sg[:], cc[:], ACT.Sigmoid).then_inc(sig, 1)

            @block.vector
            def _(dve):
                dve.wait_ge(loaded, 64)
                dve.wait_ge(sig, 1)
                dve.tensor_tensor(sl[:].rearrange("p k a -> p a k"), cc[:], sg[:], ALU.mult).then_inc(silu, 1)

                def add(i, s, b):
                    dve.wait_ge(summed[s], i + 1)
                    cols = bass.ds(b * 512, 512)
                    dve.tensor_tensor(res[:, cols], acc[s][0:2, :], bias[:, cols], ALU.add).then_inc(added[s], 1)
                two_slots(dve, NB, add)

            @block.tensor
            def _(pe):
                pe.wait_ge(silu, 1)

                def product(i, s, b):
                    pe.wait_ge(w_in[s], i * 16 + 16)
                    pe.wait_ge(added[s], i)
                    for k in range(KC):
                        last = pe.matmul(acc[s][0:2, :], sl[:, k, :], w[:, s, k, :], start=(k == 0), stop=(k == KC - 1))
                    last.then_inc(summed[s], 1)
                two_slots(pe, NB, product)


def normed_input(nc, l, src_x, src_ctx, g_pre, mod, consts, hi, lo):
    with Stage(nc, f"norm{l}") as st:
        ident = st.sb("ident", [P, P])
        gp = st.sb("gp", [P, KC])
        shift = st.sb("shift", [P, 2, KC])
        scale = st.sb("scale", [P, 2, KC])
        gain = st.sb("gain", [P, 2, KC])
        x = st.sb("x", [P, 2, D])
        sq = st.sb("sq", [P, D])
        ss = st.sb("ss", [P, 2, 1])
        ms = st.sb("ms", [P, 2, 1])
        rt = st.sb("rt", [P, 2, 1])
        rstd = st.sb("rstd", [P, 2, 1])
        xn = st.sb("xn", [P, 2, D])
        h = st.sb("h", [P, 2, KC, P])
        tr = [[st.ps(f"tr{s}{b}", [P, 4, P]) for b in range(2)] for s in range(2)]
        loaded, gained = st.sems("loaded", "gained")
        x_in, squared, meaned, rooted, inverted, normed, turned, moved, high, low = (
            st.sems(f"{n}0", f"{n}1") for n in (
                "x_in", "squared", "meaned", "rooted", "inverted", "normed", "turned", "moved", "high", "low"))
        with nc.Block() as block:
            @block.sync
            def _(sp):
                sp.dma_start(ident[:], consts[:, C_ID:C_ID + P]).then_inc(loaded, 16)
                with nc.allow_non_contiguous_dma(reason="columns of 1024 values"):
                    sp.dma_start(gp[:], g_pre[l].rearrange("(k p) -> p k", p=P)).then_inc(loaded, 16)
                    for r in range(2):
                        sp.dma_start(shift[:, r, :], mod[l, r, 0:D].rearrange("(k p) -> p k", p=P)).then_inc(loaded, 16)
                        sp.dma_start(scale[:, r, :], mod[l, r, D:2 * D].rearrange("(k p) -> p k", p=P)).then_inc(loaded, 16)

                def part(src, n, done):
                    def load(i, s, t):
                        sp.wait_ge(normed[s], i + done)
                        sp.dma_start(x[:, s], rows(src, t)).then_inc(x_in[s], 16)
                    two_slots(sp, n, load)
                part(src_x, NTX, 0)
                part(src_ctx, NTC, NTX // 2)

            def tiles(eng, step):
                two_slots(eng, NTX, lambda i, s, t: step(i, s, t * P, 0))
                two_slots(eng, NTC, lambda i, s, t: step(i + NTX // 2, s, SEQ + t * P, 1))

            @block.scalar
            def _(act):
                act.wait_ge(gained, 1)

                def step(i, s, col, which):
                    act.wait_ge(x_in[s], i * 16 + 16)
                    act.wait_ge(inverted[s], i)
                    act.activation(sq[:], x[:, s], ACT.Square, accum_out=ss[:, s]).then_inc(squared[s], 1)
                    act.wait_ge(meaned[s], i + 1)
                    act.activation(rt[:, s], ms[:, s], ACT.Sqrt).then_inc(rooted[s], 1)
                    act.wait_ge(turned[s], i + 1)
                    act.wait_ge(low[s], i)
                    for k in range(KC):
                        last = act.activation(h[:, s, k, :], tr[s][k // 4][:, k % 4, :], ACT.Identity,
                                              scale=gain[:, which, k:k + 1], bias=shift[:, which, k:k + 1])
                    last.then_inc(moved[s], 1)
                    act.wait_ge(moved[s], i + 1)
                    act.activation(hi[:, :, bass.ds(col, P)], h[:, s], ACT.Copy).then_inc(high[s], 1)
                tiles(act, step)

            @block.vector
            def _(dve):
                dve.wait_ge(loaded, 96)
                dve.tensor_scalar(gain[:], scale[:], 1.0, None, ALU.add).then_inc(gained, 1)
                dve.wait_ge(gained, 1)
                for r in range(2):
                    dve.tensor_tensor(gain[:, r, :], gain[:, r, :], gp[:], ALU.mult).then_inc(gained, 1)

                def step(i, s, col, which):
                    dve.wait_ge(squared[s], i + 1)
                    dve.tensor_scalar(ms[:, s], ss[:, s], 1.0 / D, EPS, ALU.mult, ALU.add).then_inc(meaned[s], 1)
                    dve.wait_ge(rooted[s], i + 1)
                    dve.reciprocal(rstd[:, s], rt[:, s]).then_inc(inverted[s], 1)
                    dve.wait_ge(inverted[s], i + 1)
                    dve.wait_ge(turned[s], i)
                    dve.tensor_scalar(xn[:, s], x[:, s], rstd[:, s], None, ALU.mult).then_inc(normed[s], 1)
                    dve.wait_ge(high[s], i + 1)
                    dve.tensor_tensor(lo[:, :, bass.ds(col, P)], h[:, s],
                                      hi[:, :, bass.ds(col, P)].bitcast(F32), ALU.subtract).then_inc(low[s], 1)
                tiles(dve, step)

            @block.tensor
            def _(pe):
                pe.wait_ge(loaded, 96)

                def step(i, s, col, which):
                    pe.wait_ge(normed[s], i + 1)
                    pe.wait_ge(moved[s], i)
                    for k in range(KC):
                        last = pe.transpose(tr[s][k // 4][:, k % 4, :], xn[:, s, k * P:(k + 1) * P], ident[:])
                    last.then_inc(turned[s], 1)
                tiles(pe, step)


def split_products(pe, out, lhs_hi, lhs_lo, rhs_hi, rhs_lo, n=KC):
    for k in range(n):
        for x, (a, b) in enumerate(((lhs_hi, rhs_hi), (lhs_hi, rhs_lo), (lhs_lo, rhs_hi))):
            last = pe.matmul(out, a(k), b(k), start=(k == 0 and x == 0), stop=(k == n - 1 and x == 2))
    return last


def project(nc, name, w, first, blocks, tiles, tile0, hi, lo, out):
    NBK = 4
    with Stage(nc, name) as st:
        raw = st.sb("raw", [P, 2, KC, BLK])
        whi = st.sb("whi", [P, 2, KC, BLK], F32R)
        wlo = st.sb("wlo", [P, 2, KC, BLK], F32R)
        res = st.sb("res", [P, 2, tiles, BLK])
        acc = [st.ps(f"acc{b}", [P, BLK * 2]) for b in range(NBK)]
        w_in, high, low, summed, moved, stored = (
            st.sems(f"{n}0", f"{n}1") for n in ("w_in", "high", "low", "summed", "moved", "stored"))
        wv = w.rearrange("(k p) n -> p k n", p=P)
        ov = out.rearrange("(t p) n -> p t n", p=P)
        with nc.Block() as block:
            @block.sync
            def _(sp):
                def load(i, s, b):
                    sp.wait_ge(low[s], i)
                    sp.dma_start(raw[:, s], wv[:, :, bass.ds(b * BLK + first, BLK)]).then_inc(w_in[s], 16)
                two_slots(sp, blocks, load)

            @block.scalar
            def _(act):
                def step(i, s, b):
                    act.wait_ge(stored[s], i * 16)
                    for t in range(tiles):
                        act.wait_ge(summed[s], i * tiles + t + 1)
                        act.activation(res[:, s, t, :], acc[t % NBK][:, 0:BLK], ACT.Copy).then_inc(moved[s], 1)
                    act.wait_ge(moved[s], i * tiles + tiles)
                    act.dma_start(ov[:, tile0:tile0 + tiles, bass.ds(b * BLK, BLK)], res[:, s]).then_inc(stored[s], 16)
                two_slots(act, blocks, step)
                for s in range(2):
                    if (blocks + 1 - s) // 2:
                        act.wait_ge(stored[s], (blocks + 1 - s) // 2 * 16)

            @block.vector
            def _(dve):
                def step(i, s, b):
                    dve.wait_ge(w_in[s], i * 16 + 16)
                    dve.wait_ge(summed[s], i * tiles)
                    dve.tensor_copy(whi[:, s], raw[:, s]).then_inc(high[s], 1)
                    dve.wait_ge(high[s], i + 1)
                    dve.tensor_tensor(wlo[:, s], raw[:, s], whi[:, s].bitcast(F32), ALU.subtract).then_inc(low[s], 1)
                two_slots(dve, blocks, step)

            @block.tensor
            def _(pe):
                def step(i, s, b):
                    pe.wait_ge(low[s], i + 1)
                    for t in range(tiles):
                        if t >= NBK:
                            pe.wait_ge(moved[s], i * tiles + t - NBK + 1)
                        elif s == 0:
                            pe.wait_ge(moved[1], i * tiles)
                        else:
                            pe.wait_ge(moved[0], i * tiles + (tiles - 1 - t) // NBK * NBK + t + 1)
                        tok = slice((tile0 + t) * P, (tile0 + t + 1) * P)
                        split_products(
                            pe, acc[t % NBK][:, 0:BLK], lambda k: hi[:, k, tok], lambda k: lo[:, k, tok],
                            lambda k: whi[:, s, k, :], lambda k: wlo[:, s, k, :]).then_inc(summed[s], 1)
                two_slots(pe, blocks, step)


def shifted_streams(nc, w, mu, hi, lo, rkvz):
    FIRST = 768
    SEGS = ((0, 512, 1), (512, 512, 513), (SEQ, CTX, SEQ + 3))
    PW = TOK + 4
    with Stage(nc, "streams") as st:
        raw = st.sb("raw", [P, 2, KC, P])
        whi = st.sb("whi", [P, 2, KC, P], F32R)
        wlo = st.sb("wlo", [P, 2, KC, P], F32R)
        pad = st.sb("pad", [P, 2, PW])
        near = st.sb("near", [P, 2, PW - 2])
        mix = st.sb("mix", [P, 2, PW - 2])
        mus = st.sb("mus", [P, NFC])
        keep = st.sb("keep", [P, NFC])
        half = st.sb("half", [P, NFC])
        acc = [[st.ps(f"acc{s}{b}", [P, 512]) for b in range(3)] for s in range(2)]
        loaded, prepared = st.sems("loaded", "prepared")
        w_in, high, low, summed, moved, summed2, scaled, mixed, stored = (
            st.sems(f"{n}0", f"{n}1") for n in (
                "w_in", "high", "low", "summed", "moved", "near", "scaled", "mixed", "stored"))
        wv = w.rearrange("(k p) n -> p k n", p=P)
        with nc.Block() as block:
            @block.sync
            def _(sp):
                with nc.allow_non_contiguous_dma(reason="one column of 1792 values"):
                    sp.dma_start(mus[:], mu.rearrange("(c p) -> p c", p=P)).then_inc(loaded, 16)

                def load(i, s, b):
                    sp.wait_ge(low[s], i)
                    sp.dma_start(raw[:, s], wv[:, :, bass.ds(b * P + FIRST, P)]).then_inc(w_in[s], 16)
                two_slots(sp, NFC, load)

            @block.scalar
            def _(act):
                act.wait_ge(prepared, 2)

                def step(i, s, b):
                    act.wait_ge(mixed[s], i)
                    act.wait_ge(summed2[s], i)
                    for n, (t0, n_t, col) in enumerate(SEGS):
                        act.wait_ge(summed[s], i * 3 + n + 1)
                        act.activation(pad[:, s, col:col + n_t], acc[s][n][:, 0:n_t], ACT.Copy).then_inc(moved[s], 1)
                two_slots(act, NFC, step)
                for s in range(2):
                    act.wait_ge(stored[s], NFC // 2 * 32)

            @block.gpsimd
            def _(pool):
                pool.memset(pad[:], 0.0).then_inc(prepared, 1)

                def step(i, s, b):
                    pool.wait_ge(moved[s], i * 3 + 3)
                    pool.wait_ge(mixed[s], i)
                    pool.tensor_tensor(near[:, s], pad[:, s, 0:PW - 2], pad[:, s, 2:PW], ALU.add).then_inc(summed2[s], 1)
                    pool.wait_ge(mixed[s], i + 1)
                    pool.dma_start(rkvz[at(b), :, 0:SEQ].rearrange("a p n -> (a p) n"),
                                   mix[:, s, 0:SEQ]).then_inc(stored[s], 16)
                    pool.dma_start(rkvz[at(b), :, SEQ:TOK].rearrange("a p n -> (a p) n"),
                                   mix[:, s, SEQ + 2:TOK + 2]).then_inc(stored[s], 16)
                two_slots(pool, NFC, step)

            @block.vector
            def _(dve):
                dve.wait_ge(loaded, 16)
                dve.tensor_scalar(keep[:], mus[:], -1.0, 1.0, ALU.mult, ALU.add)
                dve.tensor_scalar(half[:], mus[:], 0.5, None, ALU.mult).then_inc(prepared, 1)
                dve.wait_ge(prepared, 2)

                def split(i, s, b):
                    dve.wait_ge(w_in[s], i * 16 + 16)
                    dve.wait_ge(summed[s], i * 3)
                    dve.tensor_copy(whi[:, s], raw[:, s]).then_inc(high[s], 1)
                    dve.wait_ge(high[s], i + 1)
                    dve.tensor_tensor(wlo[:, s], raw[:, s], whi[:, s].bitcast(F32), ALU.subtract).then_inc(low[s], 1)

                def step(i, s, b):
                    dve.wait_ge(moved[s], i * 3 + 3)
                    dve.wait_ge(stored[s], i * 32)
                    dve.tensor_scalar(mix[:, s], pad[:, s, 1:PW - 1], keep[:, at(b)], None, ALU.mult).then_inc(scaled[s], 1)
                    dve.wait_ge(scaled[s], i + 1)
                    dve.wait_ge(summed2[s], i + 1)
                    dve.scalar_tensor_tensor(mix[:, s], near[:, s], half[:, at(b)], mix[:, s],
                                             ALU.mult, ALU.add).then_inc(mixed[s], 1)

                def pair(i):
                    for s in range(2):
                        split(i, s, i * 2 + s)
                    for s in range(2):
                        step(i, s, i * 2 + s)
                loop(dve, NFC // 2, pair)

            @block.tensor
            def _(pe):
                def step(i, s, b):
                    pe.wait_ge(low[s], i + 1)
                    pe.wait_ge(moved[s], i * 3)
                    for n, (t0, n_t, col) in enumerate(SEGS):
                        split_products(
                            pe, acc[s][n][:, 0:n_t], lambda k: whi[:, s, k, :], lambda k: wlo[:, s, k, :],
                            lambda k: hi[:, k, t0:t0 + n_t], lambda k: lo[:, k, t0:t0 + n_t]).then_inc(summed[s], 1)
                two_slots(pe, NFC, step)


def decayed_streams(nc, rkvz, w0, w2, a0, a2, k_k, k_a, r_k, consts, streams, wcs, vtok, bonus):
    SPANS = ((0, 512), (512, 512), (1024, 256))
    with Stage(nc, "decay") as st:
        ones = st.sb("ones", [P, P])
        ident = st.sb("ident", [P, P])
        carry = st.sb("carry", [P, 2, TOK])
        tz = st.sb("tz", [P, TOK])
        za = st.sb("za", [P, TOK])
        w0c = st.sb("w0c", [P, 2, PAIRS])
        a0c = st.sb("a0c", [P, 2, PAIRS])
        kkc, kac, rkc, kan = (st.sb(n, [P, PAIRS]) for n in ("kkc", "kac", "rkc", "kan"))
        rkv = st.sb("rkv", [P, 2, 3, TOK])
        w2s = st.sb("w2s", [P, 2, P])
        a2s = st.sb("a2s", [P, 2, P])
        sq = st.sb("sq", [P, TOK])
        norm = st.sb("norm", [P, TOK])
        kk = st.sb("kk", [P, TOK])
        sig, rate, cum, before, e_in, e_to, e_from = (
            st.sb(n, [P, TOK]) for n in ("sig", "rate", "cum", "before", "e_in", "e_to", "e_from"))
        b_, km = st.sb("b", [P, TOK]), st.sb("km", [P, 2, TOK])
        out = st.sb("out", [P, 4, TOK])
        tot = st.sb("tot", [P, 2, NT])
        vt = st.sb("vt", [P, NT, P])
        bon = st.sb("bon", [P, TOK])
        even = st.ps("even", [P, 3 * 512])
        odd = st.ps("odd", [P, 3 * 512])
        loaded, ready, zin, tanhed = st.sems("loaded", "ready", "zin", "tanhed")
        rkv_in = st.sems("rkv_in0", "rkv_in1")
        names = ("squared", "even_in", "odd_in", "even_read", "odd_read", "clamped", "inverted", "unit",
                 "rated", "summed", "shifted", "exp_in", "exp_to", "exp_from", "r_done", "a_done", "mixed", "km_done",
                 "k_done", "b_made", "b_done", "totals", "out_stored", "bon_sum", "bon_done", "bon_stored",
                 "sig_used", "v_stored", "tot_stored")
        S = {n: st.sem(n) for n in names}
        with nc.Block() as block:
            @block.sync
            def _(sp):
                sp.dma_start(ones[:], consts[:, C_ONES:C_ONES + P]).then_inc(loaded, 16)
                sp.dma_start(ident[:], consts[:, C_ID:C_ID + P]).then_inc(loaded, 16)
                sp.dma_start(tz[:], rkvz[12]).then_inc(zin, 16)
                sp.dma_start(za[:], rkvz[13]).then_inc(loaded, 16)
                with nc.allow_non_contiguous_dma(reason="columns of 512 values"):
                    for d in range(2):
                        sp.dma_start(w0c[:, d], w0[d].rearrange("(c p) -> p c", p=P)).then_inc(loaded, 16)
                        sp.dma_start(a0c[:, d], a0[d].rearrange("(c p) -> p c", p=P)).then_inc(loaded, 16)
                    for dst, src in ((kkc, k_k), (kac, k_a), (rkc, r_k)):
                        sp.dma_start(dst[:], src.rearrange("(c p) -> p c", p=P)).then_inc(loaded, 16)

                def load(i, s, b):
                    sp.wait_ge(S["bon_done"], i * 2)
                    cols = bass.ds(b * P, P)
                    sp.dma_start(w2s[:, s], w2.rearrange("d r n -> (d r) n")[:, cols]).then_inc(rkv_in[s], 16)
                    sp.dma_start(a2s[:, s], a2.rearrange("d r n -> (d r) n")[:, cols]).then_inc(rkv_in[s], 16)
                    for n in range(3):
                        sp.dma_start(rkv[:, s, n], rkvz[at(b + n * PAIRS)].rearrange("a p n -> (a p) n")
                                     ).then_inc(rkv_in[s], 16)
                two_slots(sp, PAIRS, load)

            @block.scalar
            def _(act):
                act.wait_ge(zin, 16)
                act.activation(tz[:], tz[:], ACT.Tanh).then_inc(tanhed, 1)
                act.wait_ge(ready, 4)

                def step(i, s, b):
                    act.wait_ge(rkv_in[s], i * 80 + 80)
                    act.wait_ge(S["even_in"], b * 3)
                    act.activation(sq[:], rkv[:, s, 1], ACT.Square, scale=kkc[:, at(b)]).then_inc(S["squared"], 1)
                    act.wait_ge(S["even_in"], b * 3 + 1)
                    act.wait_ge(S["unit"], b)
                    act.activation(norm[:], even[:, 0:TOK], ACT.Sqrt).then_inc(S["even_read"], 1)
                    for d in range(2):
                        n = b * 2 + d
                        act.wait_ge(S["odd_in"], b * 3 + d + 1)
                        act.wait_ge(S["b_made"], n)
                        act.activation(rate[:], odd[:, 0:TOK], ACT.Sigmoid, bias=w0c[:, d, at(b)]).then_inc(S["odd_read"], 1)
                        act.wait_ge(S["even_in"], b * 3 + d + 2)
                        act.wait_ge(S["mixed"], n)
                        act.activation(sig[:], even[:, 0:TOK], ACT.Sigmoid, bias=a0c[:, d, at(b)]).then_inc(S["even_read"], 1)
                        act.wait_ge(S["summed"], n + 1)
                        act.wait_ge(S["r_done"], n)
                        act.activation(e_to[:], cum[:], ACT.Exp).then_inc(S["exp_to"], 1)
                        act.wait_ge(S["b_done"], n)
                        act.activation(e_from[:], cum[:], ACT.Exp, scale=-1.0).then_inc(S["exp_from"], 1)
                        act.wait_ge(S["shifted"], n + 1)
                        act.wait_ge(S["a_done"], n)
                        act.activation(e_in[:], before[:], ACT.Exp).then_inc(S["exp_in"], 1)
                        act.wait_ge(S["exp_to"], n + 1)
                        act.wait_ge(S["tot_stored"], n * 16)
                        first = CHUNK - 1 if d == 0 else 0
                        act.activation(tot[:].rearrange("p c t -> p t c"), e_to[:, first::CHUNK].rearrange("p (t c) -> p t c", c=2),
                                       ACT.Copy).then_inc(S["totals"], 1)
                        act.wait_ge(S["totals"], n + 1)
                        act.dma_start(wcs[d][at(b)].rearrange("a p c t -> (a p) c t"), tot[:]).then_inc(S["tot_stored"], 16)
                    act.wait_ge(S["odd_in"], b * 3 + 3)
                    act.wait_ge(S["v_stored"], b * 16)
                    act.activation(vt[:].rearrange("p t n -> p (t n)"), odd[:, 0:TOK], ACT.Copy).then_inc(S["odd_read"], 1)
                    act.wait_ge(S["odd_read"], b * 3 + 3)
                    act.dma_start(vtok.rearrange("(t p) n -> p t n", p=P)[:, :, bass.ds(b * P, P)], vt[:]
                                  ).then_inc(S["v_stored"], 16)
                two_slots(act, PAIRS, step)
                act.wait_ge(S["v_stored"], PAIRS * 16)
                act.wait_ge(S["tot_stored"], PAIRS * 32)

            @block.gpsimd
            def _(pool):
                pool.memset(carry[:], 1.0).then_inc(ready, 1)
                pool.wait_ge(ready, 2)
                pool.memset(carry[:, 0, ::CHUNK], 0.0).then_inc(ready, 1)
                pool.memset(carry[:, 1, CHUNK - 1::CHUNK], 0.0).then_inc(ready, 1)

                def step(i, s, b):
                    for d in range(2):
                        n = b * 2 + d
                        pool.wait_ge(rkv_in[s], i * 80 + 80)
                        pool.wait_ge(S["exp_to"], n + 1)
                        pool.wait_ge(S["out_stored"], n * 16)
                        pool.tensor_tensor(out[:, 0], rkv[:, s, 0], e_to[:], ALU.mult).then_inc(S["r_done"], 1)
                        pool.wait_ge(S["r_done"], n + 1)
                        pool.wait_ge(S["a_done"], n + 1)
                        pool.wait_ge(S["k_done"], n + 1)
                        pool.wait_ge(S["b_done"], n + 1)
                        pool.dma_start(streams[d][at(b)].rearrange("a p f n -> (a p) f n"), out[:]
                                       ).then_inc(S["out_stored"], 16)
                    pool.wait_ge(S["bon_done"], b + 1)
                    pool.dma_start(bonus[at(b)].rearrange("a p n -> (a p) n"), bon[:]).then_inc(S["bon_stored"], 16)
                two_slots(pool, PAIRS, step)
                pool.wait_ge(S["out_stored"], PAIRS * 32)
                pool.wait_ge(S["bon_stored"], PAIRS * 16)

            @block.vector
            def _(dve):
                dve.wait_ge(loaded, 16 * 10)
                dve.tensor_scalar(kan[:], kac[:], -1.0, 1.0, ALU.mult, ALU.add).then_inc(ready, 1)
                dve.wait_ge(ready, 4)

                def step(i, s, b):
                    k = rkv[:, s, 1]
                    dve.wait_ge(rkv_in[s], i * 80 + 80)
                    dve.wait_ge(S["even_read"], b * 3 + 1)
                    dve.tensor_scalar(norm[:], norm[:], 1e-12, None, ALU.max).then_inc(S["clamped"], 1)
                    dve.wait_ge(S["clamped"], b + 1)
                    dve.reciprocal(norm[:], norm[:]).then_inc(S["inverted"], 1)
                    dve.wait_ge(S["inverted"], b + 1)
                    dve.scalar_tensor_tensor(kk[:], k, kkc[:, at(b)], norm[:], ALU.mult, ALU.mult).then_inc(S["unit"], 1)
                    for d in range(2):
                        n = b * 2 + d
                        back = slice(None, None, 1 if d == 0 else -1)
                        dve.wait_ge(S["odd_read"], b * 3 + d + 1)
                        dve.tensor_scalar(rate[:], rate[:], -DECAY, None, ALU.mult).then_inc(S["rated"], 1)
                        dve.wait_ge(S["rated"], n + 1)
                        dve.wait_ge(S["exp_from"], n)
                        dve.tensor_tensor_scan(cum[:, back], carry[:, d, back], rate[:, back], 0.0,
                                               ALU.mult, ALU.add).then_inc(S["summed"], 1)
                        dve.wait_ge(S["summed"], n + 1)
                        dve.wait_ge(S["exp_in"], n)
                        dve.tensor_tensor(before[:], cum[:], rate[:], ALU.subtract).then_inc(S["shifted"], 1)
                        dve.wait_ge(S["even_read"], b * 3 + d + 2)
                        if d == 0:
                            dve.wait_ge(S["bon_sum"], b)
                        dve.tensor_scalar(km[:, d], sig[:], kac[:, at(b)], kan[:, at(b)],
                                          ALU.mult, ALU.add).then_inc(S["mixed"], 1)
                        dve.wait_ge(S["mixed"], n + 1)
                        dve.wait_ge(S["unit"], b + 1)
                        dve.tensor_tensor(b_[:], kk[:], sig[:], ALU.mult).then_inc(S["b_made"], 1)
                        dve.tensor_tensor(km[:, d], km[:, d], k, ALU.mult).then_inc(S["km_done"], 1)
                        dve.wait_ge(S["exp_in"], n + 1)
                        dve.wait_ge(S["out_stored"], n * 16)
                        dve.tensor_tensor(out[:, 1], kk[:], e_in[:], ALU.mult).then_inc(S["a_done"], 1)
                        dve.wait_ge(S["km_done"], n + 1)
                        dve.wait_ge(S["exp_from"], n + 1)
                        dve.tensor_tensor(out[:, 3], km[:, d], e_from[:], ALU.mult).then_inc(S["k_done"], 1)
                        dve.wait_ge(S["b_made"], n + 1)
                        dve.tensor_tensor(out[:, 2], b_[:], e_from[:], ALU.mult).then_inc(S["b_done"], 1)
                    dve.wait_ge(S["bon_stored"], b * 16)
                    dve.wait_ge(S["km_done"], b * 2 + 2)
                    dve.tensor_tensor(bon[:], km[:, 0], km[:, 1], ALU.add).then_inc(S["bon_sum"], 1)
                    dve.wait_ge(S["bon_sum"], b + 1)
                    dve.wait_ge(S["r_done"], b * 2 + 2)
                    dve.wait_ge(S["odd_in"], b * 3 + 3)
                    dve.scalar_tensor_tensor(bon[:], rkv[:, s, 0], rkc[:, at(b)], bon[:], ALU.mult, ALU.mult
                                             ).then_inc(S["bon_done"], 1)
                two_slots(dve, PAIRS, step)

            @block.tensor
            def _(pe):
                pe.wait_ge(loaded, 16 * 10)
                pe.wait_ge(tanhed, 1)

                def spans(out_, lhs, rhs):
                    for t0, n in SPANS:
                        last = pe.matmul(out_[:, t0:t0 + n], lhs, rhs[:, t0:t0 + n], start=True, stop=True)
                    return last

                def step(i, s, b):
                    pe.wait_ge(S["squared"], b + 1)
                    pe.wait_ge(S["even_read"], b * 3)
                    spans(even, ones[:], sq).then_inc(S["even_in"], 1)
                    pe.wait_ge(rkv_in[s], i * 80 + 80)
                    for d in range(2):
                        half = slice(d * HD, (d + 1) * HD)
                        pe.wait_ge(S["odd_read"], b * 3 + d)
                        spans(odd, w2s[half, s], tz[half]).then_inc(S["odd_in"], 1)
                        pe.wait_ge(S["even_read"], b * 3 + d + 1)
                        spans(even, a2s[half, s], za[half]).then_inc(S["even_in"], 1)
                    pe.wait_ge(S["odd_read"], b * 3 + 2)
                    for t in range(NT):
                        last = pe.transpose(odd[:, t * P:(t + 1) * P], rkv[:, s, 2, t * P:(t + 1) * P], ident[:])
                    last.then_inc(S["odd_in"], 1)
                two_slots(pe, PAIRS, step)



def chunked_scan(nc, streams, wcs, vtok, consts, ydir):
    STEPS = 20
    with Stage(nc, "scan") as st:
        ident = st.sb("ident", [P, P])
        gmask = st.sb("gmask", [P, 2, 2, P])
        lmask = st.sb("lmask", [P, LEVELS + 1, P])
        state = st.sb("state", [P, 2, PAIRS, 2, HD])
        wend = st.sb("wend", [P, 2, PAIRS, 2, NT])
        G = range(2)
        L = [st.sb(f"L{g}", [P, 2, 4, P]) for g in G]
        V = [st.sb(f"V{g}", [P, 2, P]) for g in G]
        RI = [st.sb(f"RI{g}", [P, 4, P]) for g in G]
        U = [st.sb(f"U{g}", [P, 4, 2, P]) for g in G]
        LL = [st.sb(f"LL{g}", [P, 4, 2, P]) for g in G]
        AV = [st.sb(f"AV{g}", [P, 4, P]) for g in G]
        off = [st.sb(f"off{g}", [P, 4, LEVELS, P]) for g in G]
        X = [st.sb(f"X{g}", [P, 4, P]) for g in G]
        XT = [st.sb(f"XT{g}", [P, 4, P]) for g in G]
        X1 = [st.sb(f"X1{g}", [P, 4, P]) for g in G]
        P1 = [st.sb(f"P1{g}", [P, 4, P]) for g in G]
        P2 = [st.sb(f"P2{g}", [P, 4, HD]) for g in G]
        EQ = [st.sb(f"EQ{g}", [P, 4, P]) for g in G]
        Y = [st.sb(f"Y{g}", [P, 4, HD]) for g in G]
        gram = [[st.ps(f"gram{g}{h}", [P, 2, 2 * P]) for h in range(2)] for g in G]
        work = [st.ps(f"work{g}", [P, 4, P]) for g in G]
        step0 = [st.ps(f"step{g}", [P, 4, P]) for g in G]
        def zbank(g, d, n):
            bank = step0[g] if d == 0 else gram[g][1]
            return bank[:].rearrange("p a b -> p (a b)")[:, n * P:(n + 1) * P]

        loaded, ready = st.sems("loaded", "ready")
        (l_in, v_in, r_in, gram_in, gram_read, work_in, work_read, masked, first_x, z_in, state_new, y_read, stored) = (
            st.sems(f"{n}0", f"{n}1") for n in (
                "l_in", "v_in", "r_in", "gram_in", "gram_read", "work_in", "work_read", "masked", "first_x",
                "z_in", "state_new", "y_read", "stored"))

        def bodies(eng, body):
            for count, base, t0, t1 in ((NTC, 0, NTX, NTX + NTC - 1), (NTX, 2 * NTC, 0, NTX - 1)):
                with eng.Fori(0, count) as j:
                    for r in range(2):
                        body(j * 2 + (base + r), (j + t0, (j * -1) + t1), (2 * r, 2 * r + 1))

        with nc.Block() as block:
            @block.sync
            def _(sp):
                sp.dma_start(ident[:], consts[:, C_ID:C_ID + P]).then_inc(loaded, 16)
                sp.dma_start(gmask[:].rearrange("p a b n -> p (a b n)"), consts[:, C_GRAM:C_GRAM + 4 * P]).then_inc(loaded, 16)
                sp.dma_start(lmask[:].rearrange("p a n -> p (a n)"), consts[:, C_LEV:C_LEV + (LEVELS + 1) * P]).then_inc(loaded, 16)
                with nc.allow_non_contiguous_dma(reason="one decay per chunk and feature"):
                    for c in range(2):
                        half = slice((1 - c) * HD, (2 - c) * HD)
                        for d in range(2):
                            for h in range(2):
                                sp.dma_start(wend[half, d, :, h, :],
                                             wcs[d].rearrange("q (h k) c t -> h c k q t", h=2)[h, c]
                                             ).then_inc(loaded, 16)
                for g in G:
                    for c in range(2):
                        for u in range(4):
                            sp.dma_start(RI[g][c * HD:(c + 1) * HD, u, (1 - c) * HD:(2 - c) * HD],
                                         consts[0:HD, C_ID:C_ID + HD]).then_inc(loaded, 16)

                def body(n, tiles, pairs):
                    for g in G:
                        sp.wait_ge(gram_in[g], n * 4)
                        for d in range(2):
                            tok = bass.ds(tiles[d] * P, P)
                            sp.dma_start(L[g][:, d], streams[d, pairs[g], :, :, tok]).then_inc(l_in[g], 16)
                        sp.wait_ge(work_read[g], n * STEPS)
                        for d in range(2):
                            for c in range(2):
                                sp.dma_start(
                                    RI[g][c * HD:(c + 1) * HD, 2 * d:2 * d + 2, c * HD:(c + 1) * HD],
                                    streams[d, pairs[g]].rearrange("(h k) f n -> f k h n", h=2)[
                                        0, :, :, bass.ds(tiles[d] * P + c * CHUNK, CHUNK)]).then_inc(r_in[g], 16)
                        sp.wait_ge(z_in[g], n * 2)
                        for d in range(2):
                            sp.dma_start(V[g][:, d], vtok[bass.ds(tiles[d] * P, P), pairs[g] * P:(pairs[g] + 1) * P]
                                         ).then_inc(v_in[g], 16)
                bodies(sp, body)

            @block.gpsimd
            def _(pool):
                pool.memset(state[:], 0.0).then_inc(ready, 1)
                for g in G:
                    pool.memset(P1[g][:], 0.0).then_inc(ready, 1)
                pool.wait_ge(loaded, 16 * (3 + 8 + 16))

                def body(n, tiles, pairs):
                    for g in G:
                        pool.wait_ge(work_in[g], n * STEPS)
                        for u in range(4):
                            pool.wait_ge(gram_read[g], n * 4 + u + 1)
                            pool.tensor_tensor(off[g][:, u], LL[g][:, u, 0:1, :].to_broadcast([P, LEVELS, P]),
                                               lmask[:, 1:], ALU.mult).then_inc(masked[g], 1)
                bodies(pool, body)

            @block.scalar
            def _(act):
                act.wait_ge(ready, 3)

                def work_step(n, g, m):
                    act.wait_ge(work_in[g], n * STEPS + m + 1)

                def body(n, tiles, pairs):
                    for d in range(2):
                        us = slice(2 * d, 2 * d + 2)
                        for g in G:
                            work_step(n, g, d)
                            w = work[g][:].rearrange("p f (h k) -> p f h k", h=2)
                            act.activation(AV[g][:, us, 0:HD], w[:, 0], ACT.Copy)
                            for c in range(2):
                                rows_ = slice(c * HD, (c + 1) * HD)
                                last = act.activation(
                                    U[g][rows_, us, :, (1 - c) * HD:(2 - c) * HD].rearrange("p h f k -> p f h k"),
                                    w[rows_, 1:3], ACT.Copy)
                            last.then_inc(work_read[g], 1)
                    for g in G:
                        work_step(n, g, 2)
                        act.activation(AV[g][:, :, HD:P], work[g][:, 0:2, :].rearrange("p a (b k) -> p (a b) k", b=2),
                                       ACT.Copy).then_inc(work_read[g], 1)
                    for g in G:
                        work_step(n, g, 3)
                        act.activation(X[g][:], work[g][:], ACT.Copy).then_inc(work_read[g], 1)
                    for k in range(LEVELS):
                        for g in G:
                            work_step(n, g, 4 + 3 * k)
                            act.activation(X1[g][:], work[g][:], ACT.Copy).then_inc(work_read[g], 1)
                        if k < LEVELS - 1:
                            for g in G:
                                work_step(n, g, 6 + 3 * k)
                                act.activation(XT[g][:], work[g][:], ACT.Copy).then_inc(work_read[g], 1)
                    for g in G:
                        work_step(n, g, 18)
                        for c in range(2):
                            half = slice(c * HD, (c + 1) * HD)
                            act.activation(P1[g][half, :, half], work[g][half, :, 0:HD], ACT.Copy, scale=-1.0)
                        act.activation(P2[g][:], work[g][:, :, HD:P], ACT.Copy, scale=-1.0).then_inc(work_read[g], 1)
                    for x in range(2):
                        for g in G:
                            if x == 0:
                                act.wait_ge(stored[g], n * 32)
                            act.wait_ge(z_in[g], n * 2 + x + 1)
                            for d in range(2):
                                c = x ^ d
                                rows_ = slice(c * HD, (c + 1) * HD)
                                last = act.activation(
                                    Y[g][rows_, 2 * d:2 * d + 2, :],
                                    zbank(g, d, x)[rows_, :].rearrange("p (h v) -> p h v", h=2), ACT.Copy)
                            last.then_inc(y_read[g], 1)
                    for g in G:
                        act.wait_ge(y_read[g], n * 2 + 2)
                        for d in range(2):
                            act.dma_start(
                                ydir[d, bass.ds(tiles[d] * P, P), pairs[g] * P:(pairs[g] + 1) * P],
                                Y[g][:, 2 * d:2 * d + 2, :].rearrange("p h v -> p (h v)")).then_inc(stored[g], 16)
                bodies(act, body)
                for g in G:
                    act.wait_ge(stored[g], 2 * NT * 32)

            @block.vector
            def _(dve):
                dve.wait_ge(loaded, 16 * (3 + 8 + 16))

                def body(n, tiles, pairs):
                    for u in range(4):
                        d, h = u // 2, u % 2
                        for g in G:
                            dve.wait_ge(gram_in[g], n * 4 + u + 1)
                            dve.wait_ge(masked[g], n * 4)
                            src = gram[g][h]
                            for c in range(2):
                                half = slice(c * HD, (c + 1) * HD)
                                dve.tensor_tensor(U[g][half, u, :, half], src[half, :, half],
                                                  gmask[half, d, 0:1, half].to_broadcast([HD, 2, HD]), ALU.mult)
                            dve.tensor_tensor(LL[g][:, u], src[:, :, P:2 * P],
                                              gmask[:, d, 1:2, :].to_broadcast([P, 2, P]), ALU.mult
                                              ).then_inc(gram_read[g], 1)
                    for g in G:
                        dve.wait_ge(gram_read[g], n * 4 + 4)
                        dve.tensor_tensor(XT[g][:], LL[g][:, :, 0, :], lmask[:, 0:1, :].to_broadcast([P, 4, P]),
                                          ALU.mult).then_inc(first_x[g], 1)
                        dve.wait_ge(first_x[g], n * 2 + 1)
                        dve.tensor_tensor(XT[g][:], ident[:, None, :].to_broadcast([P, 4, P]), XT[g][:],
                                          ALU.subtract).then_inc(first_x[g], 1)
                    for k in range(LEVELS):
                        for g in G:
                            dve.wait_ge(work_in[g], n * STEPS + 4 + 3 * k + 2)
                            x = X[g] if k < LEVELS - 1 else XT[g]
                            dve.tensor_tensor(x[:], x[:], work[g][:], ALU.subtract).then_inc(work_read[g], 1)
                    for g in G:
                        dve.wait_ge(r_in[g], n * 64 + 64)
                        dve.wait_ge(work_in[g], n * STEPS + 20)
                        dve.tensor_tensor(EQ[g][:], work[g][:], RI[g][:], ALU.add).then_inc(work_read[g], 1)
                    for x in range(2):
                        for g in G:
                            dve.wait_ge(z_in[g], n * 2 + x + 1)
                            for d in range(2):
                                c = x ^ d
                                half = slice((1 - c) * HD, (2 - c) * HD)
                                last = dve.tensor_tensor(
                                    state[half, d, pairs[g]], zbank(g, d, x)[half, :].rearrange("p (h v) -> p h v", h=2),
                                    wend[half, d, pairs[g], :, bass.ds(tiles[d], 1)].to_broadcast([HD, 2, HD]), ALU.mult)
                            last.then_inc(state_new[g], 1)
                bodies(dve, body)

            @block.tensor
            def _(pe):
                pe.wait_ge(loaded, 16 * (3 + 8 + 16))
                pe.wait_ge(ready, 3)

                def body(n, tiles, pairs):
                    def work_free(g, m):
                        pe.wait_ge(work_read[g], n * STEPS + m)

                    for d in range(2):
                        for g in G:
                            if d == 0:
                                pe.wait_ge(l_in[g], n * 32 + 32)
                            work_free(g, d)
                            for f in range(3):
                                last = pe.transpose(work[g][:, f, :], L[g][:, d, f + 1, :], ident[:])
                            last.then_inc(work_in[g], 1)
                    for u in range(4):
                        d, h = u // 2, u % 2
                        half = slice(h * HD, (h + 1) * HD)
                        for g in G:
                            if u < 2:
                                pe.wait_ge(gram_read[g], n * 4)
                                pe.wait_ge(state_new[g], n * 2)
                                pe.wait_ge(y_read[g], n * 2)
                            else:
                                pe.wait_ge(gram_read[g], n * 4 + u - 1)
                            for f in range(2):
                                last = pe.matmul(gram[g][h][:, f, :], L[g][half, d, 2 + f, :],
                                                 L[g][half, d, 0:2, :].rearrange("p a n -> p (a n)"), start=True, stop=True)
                            last.then_inc(gram_in[g], 1)
                    for g in G:
                        work_free(g, 2)
                        pe.wait_ge(v_in[g], n * 32 + 32)
                        pe.wait_ge(gram_read[g], n * 4 + 4)
                        for u in range(4):
                            last = pe.matmul(work[g][:, u // 2, (u % 2) * HD:(u % 2 + 1) * HD], LL[g][:, u, 1, :],
                                             V[g][:, u // 2, (u % 2) * HD:(u % 2 + 1) * HD], start=True, stop=True)
                        last.then_inc(work_in[g], 1)
                    for g in G:
                        work_free(g, 3)
                        pe.wait_ge(first_x[g], n * 2 + 2)
                        for u in range(4):
                            last = pe.transpose(work[g][:, u, :], XT[g][:, u, :], ident[:])
                        last.then_inc(work_in[g], 1)
                    for k in range(LEVELS):
                        for g in G:
                            work_free(g, 4 + 3 * k)
                            pe.wait_ge(masked[g], n * 4 + 4)
                            for u in range(4):
                                last = pe.matmul(work[g][:, u, :], off[g][:, u, k, :], X[g][:, u, :], start=True, stop=True)
                            last.then_inc(work_in[g], 1)
                        for g in G:
                            work_free(g, 5 + 3 * k)
                            for u in range(4):
                                if k < LEVELS - 1:
                                    last = pe.matmul(work[g][:, u, :], XT[g][:, u, :], X1[g][:, u, :], start=True, stop=True)
                                else:
                                    last = pe.matmul(work[g][:, u, :], X1[g][:, u, :], XT[g][:, u, :], start=True, stop=True)
                            last.then_inc(work_in[g], 1)
                        if k < LEVELS - 1:
                            for g in G:
                                work_free(g, 6 + 3 * k)
                                for u in range(4):
                                    last = pe.transpose(work[g][:, u, :], X[g][:, u, :], ident[:])
                                last.then_inc(work_in[g], 1)
                    for g in G:
                        work_free(g, 18)
                        for u in range(4):
                            last = pe.matmul(work[g][:, u, :], XT[g][:, u, :], AV[g][:, u, :], start=True, stop=True)
                        last.then_inc(work_in[g], 1)
                    for g in G:
                        work_free(g, 19)
                        for u in range(4):
                            last = pe.matmul(work[g][:, u, :], P1[g][:, u, :], U[g][:, u, 0, :], start=True, stop=True)
                        last.then_inc(work_in[g], 1)
                    for x in range(2):
                        for g in G:
                            if x == 0:
                                work_free(g, 20)
                            pe.wait_ge(state_new[g], n * 2 + x)
                            pe.wait_ge(y_read[g], n * 2 + x)
                            for u in range(4):
                                d, h = u // 2, u % 2
                                c = x ^ d
                                half = slice(c * HD, (c + 1) * HD)
                                out = zbank(g, d, x)[:, h * HD:(h + 1) * HD]
                                pe.matmul(out, U[g][half, u, 0, :], P2[g][half, u, :], start=True, stop=False)
                                pe.matmul(out, U[g][half, u, 1, :], V[g][half, d, h * HD:(h + 1) * HD],
                                          start=False, stop=False)
                                last = pe.matmul(out, EQ[g][half, u, :], state[half, d, pairs[g], h, :],
                                                 start=False, stop=True)
                            last.then_inc(z_in[g], 1)
                bodies(pe, body)



def heads(nc, name, src, nh, gain, rope, consts, parts, qst=None, kst=None, vst=None, pad=0):
    keys = kst is not None
    W = nh * HD
    NG = 1 if keys else nh // R
    with Stage(nc, name) as st:
        ident = st.sb("ident", [P, P])
        gains = st.sb("gains", [P, HD])
        x = st.sb("x", [P, 2, W * (2 if keys else 1)])
        cs = st.sb("cs", [P, 2, 2, 32])
        sq = st.sb("sq", [P, W])
        ss, ms, rt, r0, t0, t1, rstd = (st.sb(n, [P, 2, nh]) for n in ("ss", "ms", "rt", "r0", "t0", "t1", "rstd"))
        xn = st.sb("xn", [P, 2, W])
        xc = st.sb("xc", [P, 2, W])
        xs = st.sb("xs", [P, 2, W])
        xr = st.sb("xr", [P, 2, nh, 2, HD])
        bank = [st.ps(f"bank{s}", [P, 4, P]) for s in range(2)]
        hl = [st.sb(f"hl{s}", [P, 2, 4, P], F32R) for s in range(2)]
        vs = st.sb("vs", [P, 2, nh, 2, HD], F32R) if keys else None
        loaded = st.sem("loaded")
        (x_in, squared, summed, meaned, rooted, inv, nwt, scaled, gained, cosd, sind, rotated, v_hi, v_lo) = (
            st.sems(f"{n}0", f"{n}1") for n in (
                "x_in", "squared", "summed", "meaned", "rooted", "inverted", "newton", "scaled", "gained", "cosined",
                "sined", "rotated", "v_hi", "v_lo"))
        turned, high, low, stored, v_stored, twice = (
            st.sems(f"{n}0", f"{n}1") for n in ("turned", "high", "low", "stored", "v_stored", "twice"))

        def tiles(eng, step):
            done = 0
            for first, count in parts:
                base = done // 2
                two_slots(eng, count, lambda i, s, t: step(i + base, s, t + first))
                done += count

        total = sum(c for _, c in parts)

        def uses(i, s, g):
            if NG == 1:
                return i, s
            return (i * 2 + s) * (NG // 2) + g // 2, g % 2

        with nc.Block() as block:
            @block.sync
            def _(sp):
                sp.dma_start(ident[:], consts[:, C_ID:C_ID + P]).then_inc(loaded, 16)
                sp.dma_start(gains[:], gain.rearrange("(a n) -> a n", a=1).to_broadcast([P, HD])).then_inc(loaded, 16)

                def load(i, s, t):
                    sp.wait_ge(rotated[s], i * 2)
                    sp.wait_ge(sind[s], i)
                    sp.wait_ge(cosd[s], i)
                    if keys:
                        sp.wait_ge(v_lo[s], i)
                    sp.dma_start(x[:, s], rows(src, t)).then_inc(x_in[s], 16)
                    sp.dma_start(cs[:, s], rows(rope, t)).then_inc(x_in[s], 16)
                tiles(sp, load)

            @block.scalar
            def _(act):
                def step(i, s, t):
                    act.wait_ge(x_in[s], i * 32 + 32)
                    act.wait_ge(summed[1 - s], i + s)
                    act.activation(sq[:], x[:, s, 0:W], ACT.Square).then_inc(squared[s], 1)
                    act.wait_ge(meaned[s], i + 1)
                    act.activation(rt[:, s], ms[:, s], ACT.Sqrt).then_inc(rooted[s], 1)
                    act.wait_ge(rotated[s], i * 2 + 2)
                    act.activation(xr[:, s, :, 1, :], xr[:, s, :, 0, :], ACT.Copy).then_inc(twice[s], 1)
                    for g in range(NG):
                        n, b = uses(i, s, g)
                        act.wait_ge(turned[b], n + 1)
                        act.wait_ge(stored[b], n * (32 if keys else 16))
                        if keys:
                            act.activation(hl[b][:, 0, 0:nh], bank[b][:, 0:nh, :], ACT.Copy).then_inc(high[b], 1)
                        else:
                            act.activation(hl[b][:, 0], bank[b][:], ACT.Copy).then_inc(high[b], 1)
                tiles(act, step)

            @block.gpsimd
            def _(pool):
                def step(i, s, t):
                    pool.wait_ge(gained[s], i + 1)
                    pool.wait_ge(rotated[s], i * 2)
                    pool.tensor_tensor(xs[:, s].rearrange("p (h a b) -> p h a b", h=nh, b=2),
                                       xn[:, s].rearrange("p (h a b) -> p h a b", h=nh, b=2),
                                       cs[:, s, 1][:, None, :, None].to_broadcast([P, nh, 32, 2]), ALU.mult).then_inc(sind[s], 1)
                    if keys:
                        pool.wait_ge(v_lo[s], i + 1)
                        pool.dma_start(vst[bass.ds(t * P + (pad if t_is_latent[0] else 2 * pad), P)], vs[:, s].rearrange("p h a d -> p h (a d)").bitcast(F32)).then_inc(v_stored[s], 16)
                    for g in range(NG):
                        n, b = uses(i, s, g)
                        pool.wait_ge(low[b], n + 1)
                        if keys:
                            col = t * P + pad if t_is_latent[0] else t * P + 2 * pad
                            for part in range(2):
                                pool.dma_start(kst[part, :, :, bass.ds(col, P)].rearrange("h p n -> p h n"),
                                               hl[b][:, part, 0:nh, :].bitcast(F32)).then_inc(stored[b], 16)
                        else:
                            pool.dma_start(qst[at(t), g].rearrange("a p n -> (a p) n"),
                                           hl[b][:, 0].rearrange("p r n -> p (r n)").bitcast(F32)).then_inc(stored[b], 16)
                t_is_latent = [True]
                done = 0
                for first, count in parts:
                    t_is_latent[0] = first < NTX
                    base = done // 2
                    two_slots(pool, count, lambda i, s, t: step(i + base, s, t + first))
                    done += count
                for s in range(2):
                    n = total // 2 if NG == 1 else total * NG // 2
                    pool.wait_ge(stored[s], n * (32 if keys else 16))
                    if keys:
                        pool.wait_ge(v_stored[s], total // 2 * 16)

            @block.vector
            def _(dve):
                dve.wait_ge(loaded, 32)

                def step(i, s, t):
                    xh = x[:, s, 0:W].rearrange("p (h d) -> p h d", h=nh)
                    xnh = xn[:, s].rearrange("p (h d) -> p h d", h=nh)
                    dve.wait_ge(squared[s], i + 1)
                    dve.tensor_reduce(ss[:, s], sq[:].rearrange("p (h d) -> p h d", h=nh), AX, ALU.add).then_inc(summed[s], 1)
                    dve.wait_ge(summed[s], i + 1)
                    dve.tensor_scalar(ms[:, s], ss[:, s], 1.0 / HD, EPS, ALU.mult, ALU.add).then_inc(meaned[s], 1)
                    if keys:
                        v = x[:, s, W:2 * W].rearrange("p (h d) -> p h d", h=nh)
                        dve.wait_ge(v_stored[s], i * 16)
                        dve.tensor_copy(vs[:, s, :, 0], v).then_inc(v_hi[s], 1)
                        dve.wait_ge(v_hi[s], i + 1)
                        dve.tensor_tensor(vs[:, s, :, 1], v, vs[:, s, :, 0].bitcast(F32), ALU.subtract).then_inc(v_lo[s], 1)
                    dve.wait_ge(rooted[s], i + 1)
                    dve.reciprocal(r0[:, s], rt[:, s]).then_inc(inv[s], 1)
                    dve.wait_ge(inv[s], i + 1)
                    dve.tensor_tensor(t0[:, s], r0[:, s], r0[:, s], ALU.mult).then_inc(nwt[s], 1)
                    dve.wait_ge(nwt[s], i * 4 + 1)
                    dve.tensor_tensor(t1[:, s], t0[:, s], ms[:, s], ALU.mult).then_inc(nwt[s], 1)
                    dve.wait_ge(nwt[s], i * 4 + 2)
                    dve.tensor_scalar(t1[:, s], t1[:, s], -0.5, 1.5, ALU.mult, ALU.add).then_inc(nwt[s], 1)
                    dve.wait_ge(nwt[s], i * 4 + 3)
                    dve.tensor_tensor(rstd[:, s], r0[:, s], t1[:, s], ALU.mult).then_inc(nwt[s], 1)
                    dve.wait_ge(nwt[s], i * 4 + 4)
                    dve.wait_ge(sind[s], i)
                    dve.tensor_tensor(xnh, xh, rstd[:, s, :, None].to_broadcast([P, nh, HD]), ALU.mult).then_inc(scaled[s], 1)
                    dve.wait_ge(scaled[s], i + 1)
                    dve.tensor_tensor(xnh, xnh, gains[:, None, :].to_broadcast([P, nh, HD]), ALU.mult).then_inc(gained[s], 1)
                    dve.wait_ge(gained[s], i + 1)
                    dve.tensor_tensor(xc[:, s].rearrange("p (h a b) -> p h a b", h=nh, b=2),
                                      xn[:, s].rearrange("p (h a b) -> p h a b", h=nh, b=2),
                                      cs[:, s, 0][:, None, :, None].to_broadcast([P, nh, 32, 2]), ALU.mult).then_inc(cosd[s], 1)
                    dve.wait_ge(cosd[s], i + 1)
                    dve.wait_ge(sind[s], i + 1)
                    if NG == 1:
                        dve.wait_ge(turned[s], i)
                    else:
                        dve.wait_ge(turned[1], i * NG)
                    c2, s2 = (z[:, s].rearrange("p (h a b) -> p b h a", h=nh, b=2) for z in (xc, xs))
                    dve.tensor_tensor(xr[:, s, :, 0, 0::2], c2[:, 0], s2[:, 1], ALU.subtract).then_inc(rotated[s], 1)
                    dve.tensor_tensor(xr[:, s, :, 0, 1::2], s2[:, 0], c2[:, 1], ALU.add).then_inc(rotated[s], 1)
                    for g in range(NG):
                        n, b = uses(i, s, g)
                        dve.wait_ge(high[b], n + 1)
                        if keys:
                            dve.tensor_tensor(hl[b][:, 1, 0:nh], bank[b][:, 0:nh, :], hl[b][:, 0, 0:nh].bitcast(F32),
                                              ALU.subtract).then_inc(low[b], 1)
                        else:
                            dve.tensor_tensor(hl[b][HD:P, 0], bank[b][HD:P], hl[b][HD:P, 0].bitcast(F32),
                                              ALU.subtract).then_inc(low[b], 1)
                tiles(dve, step)

            @block.tensor
            def _(pe):
                pe.wait_ge(loaded, 32)

                def step(i, s, t):
                    pe.wait_ge(twice[s], i + 1)
                    for g in range(NG):
                        n, b = uses(i, s, g)
                        pe.wait_ge(low[b], n)
                        for r in range(nh if keys else R):
                            h = g * R + r
                            last = pe.transpose(bank[b][:, r, :],
                                                xr[:, s, h].rearrange("p a d -> p (a d)"), ident[:])
                        last.then_inc(turned[b], 1)
                tiles(pe, step)



def attention(nc, name, qst, kst, vst, consts, orows, ngroups, tile0, count, spans, mask=None, sink=None):
    window = mask is not None
    nk = 5 * P if window else sum(n for _, n in spans)
    nkt = nk // P
    nbank = 2 if window else (nk + 511) // 512
    piece = nk // 2 if window else min(nk, 512)
    pieces = [(b * piece, min(piece, nk - b * piece), b) for b in range(nbank)]
    NTB = 2 if nbank <= 2 else 1
    half = ngroups // 2
    ctx_col = 2 * P + SEQ
    with Stage(nc, name) as st:
        ident = st.sb("ident", [P, P])
        summer = st.sb("summer", [P, HD])
        nkv = 2 if window else ngroups
        K = st.sb("K", [P, nkv, 2, nk], F32R)
        V = st.sb("V", [P, nkv, nkt, P], F32R)
        Q = st.sb("Q", [P, 2, R * P], F32R)
        prob = st.sb("prob", [P, 2, R, nk])
        ph = st.sb("ph", [P, 2, R * P], F32R)
        pl = st.sb("pl", [P, 2, R * P], F32R)
        osum = st.sb("osum", [P, R * P])
        top = st.sb("top", [P, 2, R])
        ntop = st.sb("ntop", [P, 2, R])
        rsum = st.sb("rsum", [P, 2, R])
        rinv = st.sb("rinv", [P, 2, R])
        res = st.sb("res", [P, 2, R, HD])
        if window:
            masks = st.sb("masks", [P, NTX, 3 * P], F32R)
            masks_raw = st.sb("masks_raw", [P, NTX, 3 * P])
            eye = st.sb("eye", [P, P], F32R)
            rounded = st.sem("rounded")
            sinks = st.sb("sinks", [P, ngroups * R])
            nsinks = st.sb("nsinks", [P, ngroups * R])
            sd = st.sb("sd", [P, 2, R])
            se = st.sb("se", [P, 2, R])
            den = st.sb("den", [P, 2, R])
        score = [st.ps(f"score{b}", [P, nbank, 512]) for b in range(2)]
        tb = [st.ps(f"tb{b}", [P, R, P]) for b in range(NTB)]
        osc = st.ps("osc", [P, R * P])
        loaded, sinked, topped, ntopped, high, pv_done, o_read, fin = st.sems(
            "loaded", "sinked", "topped", "ntopped", "high", "pv_done", "o_read", "fin")
        q_in, k_in, v_in, score_in, score_read, expd, tb_in, low, inverted, out_done, stored, sink_d, sink_e, denned = (
            st.sems(f"{n}0", f"{n}1") for n in (
                "q_in", "k_in", "v_in", "score_in", "score_read", "expd", "tb_in", "low", "inverted", "out_done",
                "stored", "sink_d", "sink_e", "denned"))

        def uses(b):
            return (nkt - b + NTB - 1) // NTB

        def before(eng, s, t, r):
            if r >= 2:
                eng.wait_ge(expd[s], t * R + r - 1)
            elif s:
                eng.wait_ge(expd[0], t * R + R)
            else:
                eng.wait_ge(expd[1], t * R)

        def scores(b, g):
            v = score[b][:]
            return v[:, :, 0:piece] if window else v.rearrange("p b n -> p (b n)")[:, 0:nk]

        def schedule(eng, first, start, turn, value, finish, own):
            def after(i, g):
                return (i, g + 1) if g + 1 < ngroups else (i + 1, 0)

            def body(i, last):
                for g in range(ngroups):
                    ahead = not (last and g == ngroups - 1)
                    ni, ng = after(i, g)
                    if ahead:
                        first(ni, ng)
                    todo = list(range(R)) if ahead else []
                    for kt in range(nkt):
                        value(i, g, kt)
                        while todo and (R - len(todo)) * nkt < (kt + 1) * R:
                            start(ni, ng, todo.pop(0))
                    if ahead:
                        turn(ni, ng)
                    finish(i, g)

            first(0, 0)
            for r in range(R):
                start(0, 0, r)
            turn(0, 0)
            if count > 1:
                if count > 2:
                    with eng.Fori(0, count - 1) as i:
                        body(i, False)
                else:
                    body(0, False)
            body(count - 1, True)

        def nothing(*a):
            pass

        def unit(i, g):
            return i * ngroups + g, g % 2, i * half + g // 2

        with nc.Block() as block:
            @block.sync
            def _(sp):
                sp.dma_start(ident[:], consts[:, C_ID:C_ID + P]).then_inc(loaded, 16)
                sp.dma_start(summer[:], consts[:, C_SUM:C_SUM + HD]).then_inc(loaded, 16)
                if window:
                    sp.dma_start(masks_raw[:], mask.rearrange("i p n -> p i n")).then_inc(loaded, 16)
                    sp.dma_start(sinks[:], sink.rearrange("(a n) -> a n", a=1).to_broadcast([P, ngroups * R])
                                 ).then_inc(loaded, 16)
                else:
                    for g in range(ngroups):
                        to = 0
                        for col, n in spans:
                            for part in range(2):
                                sp.dma_start(K[:, g, part, to:to + n].bitcast(F32), kst[part, g, :, col:col + n]).then_inc(k_in[g], 16)
                            sp.dma_start(V[:, g, to // P:(to + n) // P, :].bitcast(F32),
                                         vst[col:col + n, g, :].rearrange("(t p) n -> p t n", p=P)).then_inc(v_in[g], 16)
                            to += n

                def first(i, g):
                    n, s, t = unit(i, g)
                    sp.wait_ge(out_done[s], t)
                    sp.dma_start(Q[:, s].bitcast(F32), qst[bass.ds(i + tile0, 1), g].rearrange("a p n -> (a p) n")).then_inc(q_in[s], 16)
                    if window:
                        sp.dma_start(K[:, s, :, 0:3 * P].bitcast(F32), kst[:, g, :, bass.ds(i * P, 3 * P)].rearrange("a p n -> p a n")
                                     ).then_inc(k_in[s], 16)
                        sp.dma_start(K[:, s, :, 3 * P:].bitcast(F32), kst[:, g, :, ctx_col:ctx_col + CTX].rearrange("a p n -> p a n")
                                     ).then_inc(k_in[s], 16)
                        sp.dma_start(V[:, s, 0:3].bitcast(F32), vst[bass.ds(i * P, 3 * P), g, :].rearrange("(t p) n -> p t n", p=P)
                                     ).then_inc(v_in[s], 16)
                        sp.dma_start(V[:, s, 3:5].bitcast(F32), vst[ctx_col:ctx_col + CTX, g, :].rearrange("(t p) n -> p t n", p=P)
                                     ).then_inc(v_in[s], 16)

                schedule(sp, first, nothing, nothing, nothing, nothing, None)

            @block.gpsimd
            def _(pool):
                if window:
                    pool.wait_ge(loaded, 64)
                    pool.tensor_copy(eye[:], ident[:]).then_inc(rounded, 1)
                    pool.tensor_copy(masks[:], masks_raw[:]).then_inc(rounded, 1)

                def finish(i, g):
                    n, s, t = unit(i, g)
                    pool.wait_ge(out_done[s], t + 1)
                    pool.dma_start(orows[bass.ds((i + tile0) * P, P), g * R * HD:(g + 1) * R * HD],
                                   res[:, s].rearrange("p r d -> p (r d)")).then_inc(stored[s], 16)
                schedule(pool, nothing, nothing, nothing, nothing, finish, None)
                for s in range(2):
                    pool.wait_ge(stored[s], count * half * 16)

            @block.scalar
            def _(act):
                def start(i, g, r):
                    n, s, t = unit(i, g)
                    act.wait_ge(ntopped, n * R + r + 1)
                    if r == 0:
                        act.wait_ge(out_done[s], t)
                    dst = prob[:, s, r].rearrange("p (b n) -> p b n", b=2) if window else prob[:, s, r]
                    act.activation(dst, scores(r % 2, g), ACT.Exp, bias=ntop[:, s, r:r + 1], scale=SCALE,
                                   accum_out=rsum[:, s, r:r + 1]).then_inc(expd[s], 1)

                def turn(i, g):
                    n, s, t = unit(i, g)
                    if window:
                        act.wait_ge(sink_d[s], t + 1)
                        act.activation(se[:, s], sd[:, s], ACT.Exp).then_inc(sink_e[s], 1)

                def value(i, g, kt):
                    n, s, t = unit(i, g)
                    b = kt % NTB
                    act.wait_ge(tb_in[b], n * uses(b) + kt // NTB + 1)
                    act.wait_ge(pv_done, n * nkt + max(kt - 1, 0))
                    act.activation(ph[:, kt % 2], tb[b][:].rearrange("p r n -> p (r n)"), ACT.Copy).then_inc(high, 1)

                def finish(i, g):
                    n, s, t = unit(i, g)
                    act.wait_ge(pv_done, n * nkt + nkt)
                    act.wait_ge(fin, n)
                    act.activation(osum[:], osc[:], ACT.Copy).then_inc(o_read, 1)
                schedule(act, nothing, start, turn, value, finish, None)

            @block.vector
            def _(dve):
                if window:
                    dve.wait_ge(loaded, 64)
                    dve.tensor_scalar(nsinks[:], sinks[:], -1.0, None, ALU.mult).then_inc(sinked, 1)
                    dve.wait_ge(sinked, 1)

                def start(i, g, r):
                    n, s, t = unit(i, g)
                    dve.wait_ge(score_in[r % 2], n * 2 + r // 2 + 1)
                    dve.wait_ge(expd[s], t * R)
                    dve.tensor_reduce(top[:, s, r:r + 1], scores(r % 2, g), mybir.AxisListType.XY if window else AX, ALU.max
                                      ).then_inc(topped, 1)
                    dve.wait_ge(topped, n * R + r + 1)
                    if window:
                        dve.tensor_scalar(ntop[:, s, r:r + 1], top[:, s, r:r + 1], -SCALE, nsinks[:, g * R + r:g * R + r + 1],
                                          ALU.mult, ALU.min).then_inc(ntopped, 1)
                    else:
                        dve.tensor_scalar(ntop[:, s, r:r + 1], top[:, s, r:r + 1], -SCALE, None, ALU.mult).then_inc(ntopped, 1)

                def turn(i, g):
                    n, s, t = unit(i, g)
                    if window:
                        dve.wait_ge(ntopped, n * R + R)
                        dve.wait_ge(sink_e[s], t)
                        dve.tensor_tensor(sd[:, s], ntop[:, s], sinks[:, g * R:g * R + R], ALU.add).then_inc(sink_d[s], 1)

                def value(i, g, kt):
                    n, s, t = unit(i, g)
                    b = kt % NTB
                    dve.wait_ge(high, n * nkt + kt + 1)
                    dve.tensor_tensor(pl[:, kt % 2], tb[b][:].rearrange("p r n -> p (r n)"), ph[:, kt % 2].bitcast(F32),
                                      ALU.subtract).then_inc(low[b], 1)

                def finish(i, g):
                    n, s, t = unit(i, g)
                    b = nkt % NTB
                    dve.wait_ge(expd[s], t * R + R)
                    if window:
                        dve.wait_ge(sink_e[s], t + 1)
                        dve.tensor_tensor(den[:, s], rsum[:, s], se[:, s], ALU.add).then_inc(denned[s], 1)
                        dve.wait_ge(denned[s], t + 1)
                    dve.reciprocal(rinv[:, s], den[:, s] if window else rsum[:, s]).then_inc(inverted[s], 1)
                    dve.wait_ge(inverted[s], t + 1)
                    dve.wait_ge(stored[s], t * 16)
                    dve.wait_ge(fin, n + 1)
                    dve.tensor_tensor(res[:, s], tb[b][:].rearrange("p r n -> p (r n)")[:, 0:R * HD].rearrange("p (r d) -> p r d", r=R),
                                      rinv[:, s, :, None].to_broadcast([P, R, HD]), ALU.mult).then_inc(out_done[s], 1)
                schedule(dve, nothing, start, turn, value, finish, None)

            @block.tensor
            def _(pe):
                pe.wait_ge(loaded, 64 if window else 32)
                if window:
                    pe.wait_ge(rounded, 2)

                def start(i, g, r):
                    n, s, t = unit(i, g)
                    kv = s if window else g
                    b = r % 2
                    m = n * 2 + r // 2
                    if r == 0:
                        pe.wait_ge(q_in[s], t * 16 + 16)
                        pe.wait_ge(k_in[s], t * 32 + 32 if window else 32 * len(spans))
                    before(pe, s, t, r)
                    for off, w, bk in pieces:
                        masked = min(w, 3 * P - off) if window else 0
                        for part in range(2):
                            last = pe.matmul(score[b][:, bk, 0:w], Q[:, s, r * P:(r + 1) * P], K[:, kv, part, off:off + w],
                                             start=(part == 0), stop=(part == 1))
                            if masked > 0 and part == 0:
                                pe.matmul(score[b][:, bk, 0:masked], eye[:], masks[:, at(i), off:off + masked].rearrange("p a n -> p (a n)"),
                                          start=False, stop=False)
                    last.then_inc(score_in[b], 1)

                def value(i, g, kt):
                    n, s, t = unit(i, g)
                    kv = s if window else g
                    b = kt % NTB
                    if kt == 0:
                        pe.wait_ge(expd[s], t * R + R)
                        pe.wait_ge(v_in[s], t * 32 + 32 if window else 16 * len(spans))
                        for x in range(NTB):
                            pe.wait_ge(low[x], n * uses(x))
                        pe.wait_ge(out_done[0], i * half + (g + 1) // 2)
                        pe.wait_ge(out_done[1], i * half + g // 2)
                    if kt >= NTB:
                        pe.wait_ge(low[b], n * uses(b) + kt // NTB)
                    for r in range(R):
                        last = pe.transpose(tb[b][:, r, :], prob[:, s, r, kt * P:(kt + 1) * P], ident[:])
                    last.then_inc(tb_in[b], 1)
                    if kt:
                        meet(i, g, kt - 1)
                    if kt == nkt - 1:
                        meet(i, g, kt)

                def meet(i, g, kt):
                    n, s, t = unit(i, g)
                    kv = s if window else g
                    b = kt % NTB
                    if kt == 0:
                        pe.wait_ge(o_read, n)
                    pe.wait_ge(high, n * nkt + kt + 1)
                    pe.matmul(osc[:], V[:, kv, kt, :], ph[:, kt % 2], start=(kt == 0), stop=False)
                    pe.wait_ge(low[b], n * uses(b) + kt // NTB + 1)
                    pe.matmul(osc[:], V[:, kv, kt, :], pl[:, kt % 2], start=False, stop=(kt == nkt - 1)).then_inc(pv_done, 1)

                def finish(i, g):
                    n, s, t = unit(i, g)
                    b = nkt % NTB
                    pe.wait_ge(o_read, n + 1)
                    out = tb[b][:].rearrange("p r n -> p (r n)")
                    pe.wait_ge(low[b], (n + 1) * uses(b))
                    for r in range(R):
                        last = pe.matmul(out[:, r * HD:(r + 1) * HD], osum[:, r * P:(r + 1) * P], summer[:], start=True, stop=True)
                    last.then_inc(fin, 1)
                schedule(pe, nothing, start, nothing, value, finish, None)



def gated(nc, name, orows, gates, parts, consts, hi, lo, rwkv=None):
    nh = 2 * BW // HD
    OW = BW if rwkv else D
    with Stage(nc, name) as st:
        ident = st.sb("ident", [P, P])
        o = st.sb("o", [P, 2, D])
        ga = st.sb("ga", [P, 2, D])
        sg = st.sb("sg", [P, D])
        prod = st.sb("prod", [P, 2, D])
        if rwkv:
            ydir, vtok, bonus, gn_w, gn_b = rwkv
            sel = st.sb("sel", [P, PAIRS, 8])
            gw = st.sb("gw", [P, BW])
            gb = st.sb("gb", [P, BW])
            y = st.sb("y", [P, 2, 2 * BW])
            v = st.sb("v", [P, 2, BW])
            bo = st.sb("bo", [P, 2, PAIRS, P])
            sq = st.sb("sq", [P, 2 * BW])
            mean, var, rt, rstd = (st.sb(n, [P, nh]) for n in ("mean", "var", "rt", "rstd"))
            bsum = st.sb("bsum", [P, 8])
            bank_b = st.ps("bank_b", [P, 512])
        tr = [[st.ps(f"tr{s}{b}", [P, 4, P]) for b in range(2)] for s in range(2)]
        loaded = st.sem("loaded")
        names = ("o_in", "y_in", "sig", "silu", "gated", "turned", "high", "low", "bon_in", "meant", "centred",
                 "squared", "vared", "rooted", "inverted", "steps")
        S = {n: st.sems(f"{n}0", f"{n}1") for n in names}
        NCONST = 4 if rwkv else 1

        def tiles(eng, step):
            done = 0
            for first, count in parts:
                base = done // 2
                two_slots(eng, count, lambda i, s, t: step(i + base, s, t + first))
                done += count

        with nc.Block() as block:
            @block.sync
            def _(sp):
                sp.dma_start(ident[:], consts[:, C_ID:C_ID + P]).then_inc(loaded, 16)
                if rwkv:
                    sp.dma_start(sel[:].rearrange("p a b -> p (a b)"), consts[:, C_SEL:C_END]).then_inc(loaded, 16)
                    sp.dma_start(gw[:], gn_w.rearrange("(a n) -> a n", a=1).to_broadcast([P, BW])).then_inc(loaded, 16)
                    sp.dma_start(gb[:], gn_b.rearrange("(a n) -> a n", a=1).to_broadcast([P, BW])).then_inc(loaded, 16)

                def load(i, s, t):
                    sp.wait_ge(S["gated"][s], i)
                    sp.dma_start(ga[:, s], rows(gates, t)).then_inc(S["o_in"][s], 16)
                    sp.dma_start(o[:, s, 0:OW], rows(orows, t)).then_inc(S["o_in"][s], 16)
                    if rwkv:
                        sp.wait_ge(S["bon_in"][s], i)
                        for d in range(2):
                            sp.dma_start(y[:, s, d * BW:(d + 1) * BW], rows(ydir[d], t)).then_inc(S["y_in"][s], 16)
                        sp.dma_start(v[:, s], rows(vtok, t)).then_inc(S["y_in"][s], 16)
                        sp.dma_start(bo[:, s], bonus[:, :, bass.ds(t * P, P)].rearrange("q p n -> p q n")
                                     ).then_inc(S["y_in"][s], 16)
                tiles(sp, load)

            @block.scalar
            def _(act):
                def step(i, s, t):
                    if rwkv:
                        act.wait_ge(S["centred"][s], i + 1)
                        act.wait_ge(S["vared"][1 - s], i + s)
                        act.activation(sq[:], y[:, s], ACT.Square).then_inc(S["squared"][s], 1)
                        act.wait_ge(S["vared"][s], i + 1)
                        act.activation(rt[:], var[:], ACT.Sqrt).then_inc(S["rooted"][s], 1)
                    act.wait_ge(S["o_in"][s], i * 32 + 32)
                    act.wait_ge(S["silu"][1 - s], i + s)
                    act.activation(sg[:], ga[:, s], ACT.Sigmoid).then_inc(S["sig"][s], 1)
                    act.wait_ge(S["turned"][s], i + 1)
                    for b in range(2):
                        last = act.activation(hi[:, 4 * b:4 * b + 4, bass.ds(t * P, P)], tr[s][b][:], ACT.Copy)
                    last.then_inc(S["high"][s], 1)
                tiles(act, step)

            @block.vector
            def _(dve):
                dve.wait_ge(loaded, 16 * NCONST)

                def step(i, s, t):
                    if rwkv:
                        yh = y[:, s].rearrange("p (h d) -> p h d", h=nh)
                        vh = v[:, s].rearrange("p (h d) -> p h d", h=nh // 2)
                        k = [0]

                        def chain(ins):
                            k[0] += 1
                            ins.then_inc(S["steps"][s], 1)
                            dve.wait_ge(S["steps"][s], i * 11 + k[0])

                        dve.wait_ge(S["y_in"][s], i * 64 + 64)
                        chain(dve.tensor_reduce(mean[:], yh, AX, ALU.add))
                        chain(dve.tensor_scalar(mean[:], mean[:], 1.0 / HD, None, ALU.mult))
                        dve.tensor_tensor(yh, yh, mean[:, :, None].to_broadcast([P, nh, HD]), ALU.subtract
                                          ).then_inc(S["centred"][s], 1)
                        dve.wait_ge(S["squared"][s], i + 1)
                        chain(dve.tensor_reduce(var[:], sq[:].rearrange("p (h d) -> p h d", h=nh), AX, ALU.add))
                        dve.tensor_scalar(var[:], var[:], 1.0 / HD, GN_EPS, ALU.mult, ALU.add).then_inc(S["vared"][s], 1)
                        dve.wait_ge(S["rooted"][s], i + 1)
                        chain(dve.reciprocal(rstd[:], rt[:]))
                        dve.wait_ge(S["centred"][s], i + 1)
                        chain(dve.tensor_tensor(yh, yh, rstd[:, :, None].to_broadcast([P, nh, HD]), ALU.mult))
                        chain(dve.tensor_tensor(y[:, s, 0:BW], y[:, s, 0:BW], y[:, s, BW:], ALU.add))
                        chain(dve.tensor_tensor(y[:, s, 0:BW], y[:, s, 0:BW], gw[:], ALU.mult))
                        chain(dve.scalar_tensor_tensor(y[:, s, 0:BW], gb[:], 2.0, y[:, s, 0:BW], ALU.mult, ALU.add))
                        dve.wait_ge(S["bon_in"][s], i + 1)
                        chain(dve.tensor_copy(bsum[:], bank_b[:, 0:8]))
                        chain(dve.tensor_tensor(vh, vh, bsum[:, :, None].to_broadcast([P, 8, HD]), ALU.mult))
                        dve.wait_ge(S["o_in"][s], i * 32 + 32)
                        chain(dve.tensor_tensor(o[:, s, BW:], y[:, s, 0:BW], v[:, s], ALU.add))
                    dve.wait_ge(S["sig"][s], i + 1)
                    dve.wait_ge(S["turned"][s], i)
                    dve.tensor_tensor(prod[:, s], ga[:, s], sg[:], ALU.mult).then_inc(S["silu"][s], 1)
                    dve.wait_ge(S["silu"][s], i + 1)
                    if rwkv:
                        dve.wait_ge(S["steps"][s], i * 11 + 11)
                    dve.tensor_tensor(prod[:, s], prod[:, s], o[:, s], ALU.mult).then_inc(S["gated"][s], 1)
                    dve.wait_ge(S["high"][s], i + 1)
                    for b in range(2):
                        at_ = (slice(None), slice(4 * b, 4 * b + 4), bass.ds(t * P, P))
                        last = dve.tensor_tensor(lo[at_], tr[s][b][:], hi[at_].bitcast(F32), ALU.subtract)
                    last.then_inc(S["low"][s], 1)
                tiles(dve, step)

            @block.tensor
            def _(pe):
                pe.wait_ge(loaded, 16 * NCONST)

                def step(i, s, t):
                    if rwkv:
                        pe.wait_ge(S["y_in"][s], i * 64 + 64)
                        pe.wait_ge(S["gated"][1 - s], i + s)
                        for q in range(PAIRS):
                            last = pe.matmul(bank_b[:, 0:8], bo[:, s, q, :], sel[:, q, :], start=(q == 0), stop=(q == PAIRS - 1))
                        last.then_inc(S["bon_in"][s], 1)
                    pe.wait_ge(S["gated"][s], i + 1)
                    pe.wait_ge(S["low"][s], i)
                    for k in range(KC):
                        last = pe.transpose(tr[s][k // 4][:, k % 4, :], prod[:, s, k * P:(k + 1) * P], ident[:])
                    last.then_inc(S["turned"][s], 1)
                tiles(pe, step)


def residual(nc, name, l, yrows, src_x, src_ctx, g_post, mod, dst_x, dst_ctx):
    with Stage(nc, name) as st:
        gt = st.sb("gt", [P, 2, D])
        gp = st.sb("gp", [P, D])
        y = st.sb("y", [P, 2, D])
        x = st.sb("x", [P, 2, D])
        sq = st.sb("sq", [P, D])
        ss, ms, rt, rstd = (st.sb(n, [P, 2, 1]) for n in ("ss", "ms", "rt", "rstd"))
        res = st.sb("res", [P, 2, D])
        loaded, gained = st.sems("loaded", "gained")
        y_in, squared, meaned, rooted, inverted, scaled, added, stored = (
            st.sems(f"{n}0", f"{n}1") for n in (
                "y_in", "squared", "meaned", "rooted", "inverted", "scaled", "added", "stored"))
        parts = [(src_x, dst_x, NTX, 0, 0)]
        if dst_ctx is not None:
            parts.append((src_ctx, dst_ctx, NTC, NTX, 1))

        def tiles(eng, step):
            for src, dst, n, first, which in parts:
                two_slots(eng, n, lambda i, s, t: step(i + first // 2, s, t, src, dst, first, which))

        with nc.Block() as block:
            @block.sync
            def _(sp):
                for r in range(2):
                    sp.dma_start(gt[:, r], mod[l, r:r + 1, 2 * D:3 * D].to_broadcast([P, D])).then_inc(loaded, 16)
                sp.dma_start(gp[:], g_post[l:l + 1, :].to_broadcast([P, D])).then_inc(loaded, 16)

                def load(i, s, t, src, dst, first, which):
                    sp.wait_ge(added[s], i)
                    sp.dma_start(y[:, s], rows(yrows, t + first)).then_inc(y_in[s], 16)
                    sp.dma_start(x[:, s], rows(src, t)).then_inc(y_in[s], 16)
                tiles(sp, load)

            @block.scalar
            def _(act):
                def step(i, s, t, src, dst, first, which):
                    act.wait_ge(y_in[s], i * 32 + 32)
                    act.wait_ge(meaned[s], i)
                    act.activation(sq[:], y[:, s], ACT.Square, accum_out=ss[:, s]).then_inc(squared[s], 1)
                    act.wait_ge(meaned[s], i + 1)
                    act.activation(rt[:, s], ms[:, s], ACT.Sqrt).then_inc(rooted[s], 1)
                    act.wait_ge(added[s], i + 1)
                    act.dma_start(rows(dst, t), res[:, s]).then_inc(stored[s], 16)
                tiles(act, step)
                for s in range(2):
                    act.wait_ge(stored[s], sum(p[2] for p in parts) // 2 * 16)

            @block.vector
            def _(dve):
                dve.wait_ge(loaded, 48)
                for r in range(2):
                    dve.tensor_tensor(gt[:, r], gt[:, r], gp[:], ALU.mult).then_inc(gained, 1)
                dve.wait_ge(gained, 2)

                def step(i, s, t, src, dst, first, which):
                    dve.wait_ge(squared[s], i + 1)
                    dve.tensor_scalar(ms[:, s], ss[:, s], 1.0 / D, EPS, ALU.mult, ALU.add).then_inc(meaned[s], 1)
                    dve.wait_ge(rooted[s], i + 1)
                    dve.reciprocal(rstd[:, s], rt[:, s]).then_inc(inverted[s], 1)
                    dve.wait_ge(inverted[s], i + 1)
                    dve.wait_ge(stored[s], i * 16)
                    dve.scalar_tensor_tensor(res[:, s], y[:, s], rstd[:, s], gt[:, which], ALU.mult, ALU.mult
                                             ).then_inc(scaled[s], 1)
                    dve.wait_ge(scaled[s], i + 1)
                    dve.tensor_tensor(res[:, s], res[:, s], x[:, s], ALU.add).then_inc(added[s], 1)
                tiles(dve, step)


def zero_pads(nc, kst, vst):
    with Stage(nc, "pads") as st:
        z = st.sb("z", [P, 2 * CKV * P])
        zeroed, stored = st.sems("zeroed", "stored")
        with nc.Block() as block:
            @block.gpsimd
            def _(pool):
                pool.memset(z[:], 0.0).then_inc(zeroed, 1)

            @block.sync
            def _(sp):
                sp.wait_ge(zeroed, 1)
                for col in (0, P + SEQ):
                    sp.dma_start(kst[:, :, :, col:col + P].rearrange("a g p n -> p (a g) n"),
                                 z[:].rearrange("p (b n) -> p b n", n=P)).then_inc(stored, 16)
                    sp.dma_start(vst[col:col + P].rearrange("p g n -> p (g n)"), z[:, 0:CKV * P]).then_inc(stored, 16)
                sp.wait_ge(stored, 64)


def hybrid_layers(nc, a, out):
    def scratch(name, *shape):
        return nc.dram_tensor(name, shape, F32).ap()

    mod = scratch("mod", 2, 2, 3 * D)
    q0, kv0, gates0 = scratch("q0", TOK, AH * HD), scratch("kv0", TOK, 2 * AKV * HD), scratch("gates0", TOK, D)
    rkvz = scratch("rkvz", NFC, P, TOK)
    streams = scratch("streams", 2, PAIRS, P, 4, TOK)
    wcs, vtok = scratch("wcs", 2, PAIRS, P, 2, NT), scratch("vtok", TOK, BW)
    bonus, ydir = scratch("bonus", PAIRS, P, TOK), scratch("ydir", 2, TOK, BW)
    qst0, kst0, vst0 = scratch("qst0", NT, AKV, P, R * P), scratch("kst0", 2, AKV, P, TOK), scratch("vst0", TOK, AKV, P)
    oa, y0 = scratch("oa", TOK, BW), scratch("y0", TOK, D)
    x1, ctx1 = scratch("x1", SEQ, D), scratch("ctx1", CTX, D)
    q1, kv1, gates1 = scratch("q1", SEQ, CH * HD), scratch("kv1", TOK, 2 * CKV * HD), scratch("gates1", SEQ, D)
    PT = TOK + 2 * P
    qst1, kst1, vst1 = scratch("qst1", NTX, CKV, P, R * P), scratch("kst1", 2, CKV, P, PT), scratch("vst1", PT, CKV, P)
    oc, y1 = scratch("oc", SEQ, D), scratch("y1", SEQ, D)
    x, ctx, consts = a["x"][0], a["ctx"][0], a["consts"]
    w0, w1 = a["w_in_even"][0], a["w_in_odd"][0]
    QC, GA = AH * HD, 768 + BPROJ

    for l in range(2):
        modulation(nc, l, a["c"], a["c_ctx"], a["w_mod"], a["b_mod"], mod)
    zero_pads(nc, kst1, vst1)

    def halves():
        return (nc.sbuf_tensor(f"{n}{nc.next_id()}", [P, KC, TOK], F32R) for n in ("hi", "lo"))

    h, lw = halves()
    with h as hi, lw as lo:
        normed_input(nc, 0, x, ctx, a["g_pre"], mod, consts, hi, lo)
        shifted_streams(nc, w0, a["mu_b"][0], hi, lo, rkvz)
        project(nc, "q0p", w0, 0, QC // BLK, NT, 0, hi, lo, q0)
        project(nc, "kv0p", w0, QC, 1, NT, 0, hi, lo, kv0)
        project(nc, "g0p", w0, GA, D // BLK, NT, 0, hi, lo, gates0)
    decayed_streams(nc, rkvz, a["w0_b"][0], a["w2_b"][0], a["a0_b"][0], a["a2_b"][0], a["kk_b"][0], a["ka_b"][0],
                    a["rk_b"][0].rearrange("h d -> (h d)"), consts, streams, wcs, vtok, bonus)
    chunked_scan(nc, streams, wcs, vtok, consts, ydir)
    both = ((0, NTX), (NTX, NTC))
    heads(nc, "qh0", q0, AH, a["qn_a"][0], a["rope"], consts, both, qst=qst0)
    heads(nc, "kh0", kv0, AKV, a["kn_a"][0], a["rope"], consts, both, kst=kst0, vst=vst0)
    attention(nc, "dense", qst0, kst0, vst0, consts, oa, AKV, 0, NTX, ((0, TOK),))
    attention(nc, "context", qst0, kst0, vst0, consts, oa, AKV, NTX, NTC, ((SEQ, CTX),))
    h, lw = halves()
    with h as hi, lw as lo:
        gated(nc, "gate0", oa, gates0, both, consts, hi, lo,
              (ydir, vtok, bonus, a["gn_w_b"][0], a["gn_b_b"][0]))
        project(nc, "out0", a["w_out_even"][0], 0, D // BLK, NT, 0, hi, lo, y0)
    residual(nc, "res0", 0, y0, x, ctx, a["g_post"], mod, x1, ctx1)
    h, lw = halves()
    with h as hi, lw as lo:
        normed_input(nc, 1, x1, ctx1, a["g_pre"], mod, consts, hi, lo)
        project(nc, "q1p", w1, 0, D // BLK, NTX, 0, hi, lo, q1)
        project(nc, "kv1p", w1, D, 2 * CKV * HD // BLK, NT, 0, hi, lo, kv1)
        project(nc, "g1p", w1, D + 2 * CKV * HD, D // BLK, NTX, 0, hi, lo, gates1)
    heads(nc, "qh1", q1, CH, a["qn_c"][0], a["rope"], consts, ((0, NTX),), qst=qst1)
    heads(nc, "kh1", kv1, CKV, a["kn_c"][0], a["rope"], consts, both, kst=kst1, vst=vst1, pad=P)
    attention(nc, "window", qst1, kst1, vst1, consts, oc, CKV, 0, NTX, None, a["win"], a["sink_c"][0])
    h, lw = halves()
    with h as hi, lw as lo:
        gated(nc, "gate1", oc, gates1, ((0, NTX),), consts, hi, lo)
        project(nc, "out1", a["w_out_odd"][0], 0, D // BLK, NTX, 0, hi, lo, y1)
    residual(nc, "res1", 1, y1, x1, None, a["g_post"], mod, out[0], None)


INPUTS = ("x", "c", "ctx", "c_ctx", "w_mod", "b_mod", "g_pre", "g_post", "w_in_even", "w_out_even", "qn_a", "kn_a",
          "mu_b", "w0_b", "w2_b", "a0_b", "a2_b", "kk_b", "ka_b", "rk_b", "gn_w_b", "gn_b_b",
          "w_in_odd", "w_out_odd", "qn_c", "kn_c", "sink_c")


def kernel(**inputs):
    import numpy as _np
    import concourse.bacc as _bacc
    from concourse import mybir as _mybir
    from concourse.bass_utils import run_bass_kernel_spmd as _run

    nc = _bacc.Bacc("TRN2", target_bir_lowering=False, num_devices=1)
    arrays = {name: _np.ascontiguousarray(inputs[name]) for name in INPUTS}
    arrays["consts"], arrays["win"], arrays["rope"] = constant_tables()
    feeds, args = {}, {}
    for name, v in arrays.items():
        feeds[f"in_{name}"] = v
        args[name] = nc.dram_tensor(f"in_{name}", v.shape, _mybir.dt.from_np(v.dtype), kind="ExternalInput").ap()
    out = nc.dram_tensor("out", (1, SEQ, D), F32, kind="ExternalOutput").ap()
    hybrid_layers(nc, args, out)
    r = _run(nc, [feeds], core_ids=[0])
    return r.results[0]["out"]
```

```python
from contextlib import ExitStack

import numpy as np
import concourse.bass as bass
from concourse import mybir

F32 = mybir.dt.float32
F32R = mybir.dt.float32r
ALU = mybir.AluOpType
ACT = mybir.ActivationFunctionType
AX = mybir.AxisListType.X
AXS = mybir.AxisListType.XY

P = 128
D = 1024
SEQ = 1024
CTX = 256
TOK = SEQ + CTX
NT = TOK // P
NTX = SEQ // P
NTC = CTX // P
KC = D // P
HD = 64
GRID_W = 64
WINDOW = 128
EPS = 1e-6
GN_EPS = 64e-5
AH, AKV = 8, 2
CH, CKV = 16, 4
BW = 512
PAIRS = BW // P
CHUNK = 64
NCH = TOK // CHUNK
BPROJ = 1792
NFC = BPROJ // P
LEVELS = 5
R = 4
SCALE = HD ** -0.5
DECAY = float(np.exp(-0.5))
NEG = -1e30
BLK = 256

C_ID = 0
C_ONES = C_ID + P
C_GRAM = C_ONES + P
C_LEV = C_GRAM + 2 * 2 * CHUNK
C_SUM = C_LEV + (LEVELS + 1) * P
C_SEL = C_SUM + HD
C_ALL = C_SEL + PAIRS * 8


def constant_tables():
    p = np.arange(P)
    s, t = p[:, None], p[None, :]
    parts = [np.eye(P), ((s // HD) == (t // HD)) * 1.0]
    cs, ct = s % CHUNK, np.arange(CHUNK)[None, :]
    parts += [cs <= ct, cs < ct, cs >= ct, cs > ct]
    for k in range(LEVELS + 1):
        m = 1 << k
        parts.append(((s // (2 * m)) == (t // (2 * m))) & ((s // m) != (t // m)))
    parts.append(np.vstack([np.eye(HD)] * 2))
    sel = np.zeros((P, PAIRS, 8))
    for i in range(PAIRS):
        for h in range(2):
            sel[h * HD:(h + 1) * HD, i, 2 * i + h] = 1.0
    parts += [sel.reshape(P, -1), np.ones((P, P))]
    table = np.concatenate([np.asarray(x, np.float32) for x in parts], axis=1)
    q, k = p[:, None], np.arange(3 * P)[None, :] - P
    win = np.zeros((NTX, P, 5 * P), np.float32)
    for i in range(NTX):
        pos = k + i * P
        ok = (pos >= 0) & (pos < SEQ) & (np.abs(k - q) <= WINDOW)
        win[i, :, :3 * P] = np.where(ok, 0.0, NEG)
        win[i, :, 3 * P:4 * P], win[i, :, 4 * P:] = win[i, :, :P].T, win[i, :, 2 * P:3 * P].T
    tok = np.arange(SEQ)
    inv = (10000.0 ** (-np.arange(0, 32, 2, dtype=np.float32) / np.float32(32))).astype(np.float32)
    ang = np.concatenate([(tok // GRID_W).astype(np.float32)[:, None] * inv,
                          (tok % GRID_W).astype(np.float32)[:, None] * inv], axis=1)
    rope = np.zeros((TOK, 2, 32), np.float32)
    rope[:SEQ, 0], rope[:SEQ, 1] = np.cos(ang), np.sin(ang)
    rope[SEQ:, 0] = 1.0
    return table, win, rope


class Stage:

    def __init__(self, nc, name):
        self.nc, self.name, self.stack, self.signals = nc, name, ExitStack(), []

    def sb(self, name, shape, dt=F32):
        return self.stack.enter_context(self.nc.sbuf_tensor(f"{self.name}_{name}", shape, dt))

    def ps(self, name, shape):
        return self.stack.enter_context(self.nc.psum_tensor(f"{self.name}_{name}", shape, F32))

    def sem(self, name):
        self.signals.append(self.nc.alloc_semaphore(f"{self.name}_{name}"))
        return self.signals[-1]

    def sems(self, *names):
        return [self.sem(n) for n in names]

    def __enter__(self):
        return self

    def __exit__(self, *a):
        self.nc.clear_and_free_semaphores(self.signals)
        self.nc.all_engine_barrier()
        return self.stack.__exit__(*a)


def loop(eng, n, body, peel=True):
    start = 1 if peel or n == 1 else 0
    for i in range(start):
        body(i)
    if n - start == 1:
        body(start)
    elif n > start:
        with eng.Fori(start, n) as i:
            body(i)


def two_slots(eng, n, body):
    def pair(i):
        for s in range(2):
            body(i, s, i * 2 + s)
    if n >= 2:
        loop(eng, n // 2, pair)
    if n % 2:
        body(n // 2, 0, n - 1)


def skewed(eng, parts, *hooks):
    def both(ahead, now):
        for k in range(0, len(hooks), 2):
            for hook, step in ((hooks[k], ahead), (hooks[k + 1], now)):
                if hook and step:
                    hook(*step)

    both((0, 0, parts[0][0], 0), None)
    base = 0
    for k, (t0, count) in enumerate(parts):
        def pair(i, last):
            both((i + base, 1, i * 2 + (t0 + 1), k), (i + base, 0, i * 2 + t0, k))
            ahead = None
            if not last:
                ahead = (i + (base + 1), 0, i * 2 + (t0 + 2), k)
            elif k + 1 < len(parts):
                ahead = (base + count // 2, 0, parts[k + 1][0], k + 1)
            both(ahead, (i + base, 1, i * 2 + (t0 + 1), k))
        if count > 2:
            loop(eng, count // 2 - 1, lambda i: pair(i, False))
        pair(count // 2 - 1, True)
        base += count // 2


def at(i):
    return bass.ds(i, 1)


def rows(ap, i, n=P):
    return ap[bass.ds(i * n, n)]


def modulation(nc, c, c_ctx, w_mod, b_mod, mod, kst, vst):
    NB = 3 * D // 512
    with Stage(nc, "modulation") as st:
        cc = st.sb("cc", [P, 2, KC])
        sg = st.sb("sg", [P, 2, KC])
        sl = st.sb("sl", [P, KC, 2])
        w = st.sb("w", [P, 2, KC, 512])
        bias = st.sb("bias", [2, 2, 3 * D])
        res = st.sb("res", [2, 2, 3 * D])
        zeros = st.sb("zeros", [P, 2 * CKV * P])
        acc = [st.ps(f"acc{s}", [P, 512]) for s in range(2)]
        loaded, sig, silu, stored, zeroed, padded = st.sems("loaded", "sig", "silu", "stored", "zeroed", "padded")
        w_in, summed, added = (st.sems(f"{n}0", f"{n}1") for n in ("w_in", "summed", "added"))

        def blocks_of(eng, step):
            for l in range(2):
                two_slots(eng, NB, lambda i, s, b: step(i + l * (NB // 2), s, b, l))

        with nc.Block() as block:
            @block.sync
            def _(sp):
                with nc.allow_non_contiguous_dma(reason="one column of 1024 values"):
                    sp.dma_start(cc[:, 0, :], c.rearrange("a (k p) -> p (a k)", p=P)).then_inc(loaded, 16)
                    sp.dma_start(cc[:, 1, :], c_ctx.rearrange("(k p) -> p k", p=P)).then_inc(loaded, 16)
                for r in range(2):
                    for l in range(2):
                        sp.dma_start(bias[r:r + 1, l, :], b_mod[l:l + 1, :]).then_inc(loaded, 16)

                def load(i, s, b, l):
                    sp.wait_ge(summed[s], i)
                    sp.dma_start(w[:, s], w_mod[l].rearrange("(k p) n -> p k n", p=P)[:, :, bass.ds(b * 512, 512)]
                                 ).then_inc(w_in[s], 16)
                blocks_of(sp, load)
                for s in range(2):
                    sp.wait_ge(added[s], NB)
                for l in range(2):
                    sp.dma_start(mod[l], res[:, l]).then_inc(stored, 16)
                sp.wait_ge(stored, 32)

            @block.scalar
            def _(act):
                act.wait_ge(loaded, 96)
                act.activation(sg[:], cc[:], ACT.Sigmoid).then_inc(sig, 1)

            @block.gpsimd
            def _(pool):
                pool.memset(zeros[:], 0.0).then_inc(zeroed, 1)
                pool.wait_ge(zeroed, 1)
                for col in (0, P + SEQ):
                    pool.dma_start(kst[:, :, :, col:col + P].rearrange("p a g n -> p (a g) n"),
                                   zeros[:].rearrange("p (b n) -> p b n", n=P)).then_inc(padded, 16)
                    pool.dma_start(vst[col:col + P].rearrange("p g n -> p (g n)"), zeros[:, 0:CKV * P]).then_inc(padded, 16)
                pool.wait_ge(padded, 64)

            @block.vector
            def _(dve):
                dve.wait_ge(loaded, 96)
                dve.wait_ge(sig, 1)
                dve.tensor_tensor(sl[:].rearrange("p k a -> p a k"), cc[:], sg[:], ALU.mult).then_inc(silu, 1)

                def add(i, s, b, l):
                    dve.wait_ge(summed[s], i + 1)
                    cols = bass.ds(b * 512, 512)
                    dve.tensor_tensor(res[:, l, cols], acc[s][0:2, :], bias[:, l, cols], ALU.add).then_inc(added[s], 1)
                blocks_of(dve, add)

            @block.tensor
            def _(pe):
                pe.wait_ge(silu, 1)

                def product(i, s, b, l):
                    pe.wait_ge(w_in[s], i * 16 + 16)
                    pe.wait_ge(added[s], i)
                    for k in range(KC):
                        last = pe.matmul(acc[s][0:2, :], sl[:, k, :], w[:, s, k, :], start=(k == 0), stop=(k == KC - 1))
                    last.then_inc(summed[s], 1)
                blocks_of(pe, product)


def normed_input(nc, l, src_x, src_ctx, g_pre, mod, consts, hi, lo):
    PARTS = ((0, NTX), (NTX, NTC))
    with Stage(nc, f"norm{l}") as st:
        ident = st.sb("ident", [P, P])
        eps = st.sb("eps", [P, 1])
        gp = st.sb("gp", [P, D])
        shift = st.sb("shift", [P, 2, D])
        gain = st.sb("gain", [P, 2, D])
        x = st.sb("x", [P, 2, D])
        sq = st.sb("sq", [P, D])
        ss, rt, rstd = (st.sb(n, [P, 2, 1]) for n in ("ss", "rt", "rstd"))
        xn = st.sb("xn", [P, 2, D])
        tr = [[st.ps(f"tr{s}{b}", [P, 4, P]) for b in range(2)] for s in range(2)]
        loaded, gained, ready = st.sems("loaded", "gained", "ready")
        x_in, squared, rooted, inverted, scaled, shifted, turned, high, low = (
            st.sems(f"{n}0", f"{n}1") for n in (
                "x_in", "squared", "rooted", "inverted", "scaled", "shifted", "turned", "high", "low"))
        with nc.Block() as block:
            @block.sync
            def _(sp):
                def part(src, n, done):
                    def load(i, s, t):
                        sp.wait_ge(scaled[s], i + done)
                        sp.dma_start(x[:, s], rows(src, t)).then_inc(x_in[s], 16)
                    two_slots(sp, n, load)
                sp.dma_start(gp[:], g_pre[l:l + 1, :].to_broadcast([P, D])).then_inc(loaded, 16)
                for r in range(2):
                    sp.dma_start(gain[:, r], mod[l, r:r + 1, D:2 * D].to_broadcast([P, D])).then_inc(loaded, 16)
                    sp.dma_start(shift[:, r], mod[l, r:r + 1, 0:D].to_broadcast([P, D])).then_inc(loaded, 16)
                sp.dma_start(ident[:], consts[:, C_ID:C_ID + P]).then_inc(loaded, 16)
                part(src_x, NTX, 0)
                part(src_ctx, NTC, NTX // 2)

            @block.scalar
            def _(act):
                act.wait_ge(ready, 1)

                def first(i, s, t, which):
                    act.wait_ge(x_in[s], i * 16 + 16)
                    act.wait_ge(rooted[s], i)
                    act.activation(sq[:], x[:, s], ACT.Square, accum_out=ss[:, s]).then_inc(squared[s], 1)
                    act.wait_ge(squared[s], i + 1)
                    act.wait_ge(inverted[s], i)
                    act.activation(rt[:, s], ss[:, s], ACT.Sqrt, scale=1.0 / D, bias=eps[:]).then_inc(rooted[s], 1)

                def second(i, s, t, which):
                    act.wait_ge(turned[s], i + 1)
                    for b in range(2):
                        last = act.activation(hi[:, 4 * b:4 * b + 4, bass.ds(t * P, P)], tr[s][b][:], ACT.Copy)
                    last.then_inc(high[s], 1)
                skewed(act, PARTS, first, second)

            @block.gpsimd
            def _(pool):
                pool.memset(eps[:], EPS).then_inc(ready, 1)
                pool.wait_ge(loaded, 96)

                def first(i, s, t, which):
                    pool.wait_ge(scaled[s], i + 1)
                    pool.tensor_tensor(xn[:, s], xn[:, s], shift[:, which], ALU.add).then_inc(shifted[s], 1)
                skewed(pool, PARTS, first, None)

            @block.vector
            def _(dve):
                dve.wait_ge(loaded, 96)
                for r in range(2):
                    dve.scalar_tensor_tensor(gain[:, r], gain[:, r], 1.0, gp[:], ALU.add, ALU.mult).then_inc(gained, 1)
                dve.wait_ge(gained, 2)

                def first(i, s, t, which):
                    dve.wait_ge(rooted[s], i + 1)
                    dve.wait_ge(scaled[s], i)
                    dve.reciprocal(rstd[:, s], rt[:, s]).then_inc(inverted[s], 1)
                    dve.wait_ge(inverted[s], i + 1)
                    dve.wait_ge(turned[s], i)
                    dve.scalar_tensor_tensor(xn[:, s], x[:, s], rstd[:, s], gain[:, which], ALU.mult, ALU.mult
                                             ).then_inc(scaled[s], 1)

                def second(i, s, t, which):
                    dve.wait_ge(high[s], i + 1)
                    for b in range(2):
                        part = (slice(None), slice(4 * b, 4 * b + 4), bass.ds(t * P, P))
                        last = dve.tensor_tensor(lo[part], tr[s][b][:], hi[part].bitcast(F32), ALU.subtract)
                    last.then_inc(low[s], 1)
                skewed(dve, PARTS, first, second)

            @block.tensor
            def _(pe):
                pe.wait_ge(loaded, 96)

                def second(i, s, t, which):
                    pe.wait_ge(shifted[s], i + 1)
                    pe.wait_ge(low[s], i)
                    for k in range(KC):
                        last = pe.transpose(tr[s][k // 4][:, k % 4, :], xn[:, s, k * P:(k + 1) * P], ident[:])
                    last.then_inc(turned[s], 1)
                skewed(pe, PARTS, None, second)


def split_products(pe, out, lhs_hi, lhs_lo, rhs_hi, rhs_lo, n=KC):
    for k in range(n):
        for x, (a, b) in enumerate(((lhs_hi, rhs_hi), (lhs_hi, rhs_lo), (lhs_lo, rhs_hi))):
            last = pe.matmul(out, a(k), b(k), start=(k == 0 and x == 0), stop=(k == n - 1 and x == 2))
    return last


def project(nc, name, w, jobs, hi, lo):
    NBK = 4
    with Stage(nc, name) as st:
        raw = st.sb("raw", [P, 2, KC, BLK])
        whi = st.sb("whi", [P, 2, KC, BLK], F32R)
        wlo = st.sb("wlo", [P, 2, KC, BLK], F32R)
        res = st.sb("res", [P, 2, max(job[2] for job in jobs), BLK])
        acc = [st.ps(f"acc{b}", [P, BLK * 2]) for b in range(NBK)]
        w_in, high, low, summed, moved, stored = (
            st.sems(f"{n}0", f"{n}1") for n in ("w_in", "high", "low", "summed", "moved", "stored"))
        wv = w.rearrange("(k p) n -> p k n", p=P)

        def blocks_of(eng, step):
            turn, done = 0, 0
            for job in jobs:
                _, blocks, tiles, _ = job
                two_slots(eng, blocks, lambda i, s, b: step(i + turn, s, b, i * tiles + done, job))
                turn, done = turn + blocks // 2, done + blocks // 2 * tiles

        turns = [sum((job[1] + 1 - s) // 2 for job in jobs) for s in range(2)]
        with nc.Block() as block:
            @block.sync
            def _(sp):
                def load(i, s, b, done, job):
                    sp.wait_ge(low[s], i)
                    sp.dma_start(raw[:, s], wv[:, :, bass.ds(b * BLK + job[0], BLK)]).then_inc(w_in[s], 16)
                blocks_of(sp, load)

            @block.scalar
            def _(act):
                def step(i, s, b, done, job):
                    _, _, tiles, out = job
                    act.wait_ge(stored[s], i * 16)
                    for t in range(tiles):
                        act.wait_ge(summed[s], done + (t + 1))
                        act.activation(res[:, s, t, :], acc[t % NBK][:, 0:BLK], ACT.Copy).then_inc(moved[s], 1)
                    act.wait_ge(moved[s], done + tiles)
                    act.dma_start(out.rearrange("(t p) n -> p t n", p=P)[:, 0:tiles, bass.ds(b * BLK, BLK)], res[:, s, 0:tiles]
                                  ).then_inc(stored[s], 16)
                blocks_of(act, step)
                for s in range(2):
                    act.wait_ge(stored[s], turns[s] * 16)

            @block.vector
            def _(dve):
                def step(i, s, b, done, job):
                    dve.wait_ge(w_in[s], i * 16 + 16)
                    dve.wait_ge(summed[s], done)
                    dve.tensor_copy(whi[:, s], raw[:, s]).then_inc(high[s], 1)
                    dve.wait_ge(high[s], i + 1)
                    dve.tensor_tensor(wlo[:, s], raw[:, s], whi[:, s].bitcast(F32), ALU.subtract).then_inc(low[s], 1)
                blocks_of(dve, step)

            @block.tensor
            def _(pe):
                def step(i, s, b, done, job):
                    tiles = job[2]
                    pe.wait_ge(low[s], i + 1)
                    for t in range(tiles):
                        if t >= NBK:
                            pe.wait_ge(moved[s], done + (t - NBK + 1))
                        elif s == 0:
                            pe.wait_ge(moved[1], done)
                        else:
                            pe.wait_ge(moved[0], done + ((tiles - 1 - t) // NBK * NBK + t + 1))
                        tok = slice(t * P, (t + 1) * P)
                        split_products(
                            pe, acc[t % NBK][:, 0:BLK], lambda k: hi[:, k, tok], lambda k: lo[:, k, tok],
                            lambda k: whi[:, s, k, :], lambda k: wlo[:, s, k, :]).then_inc(summed[s], 1)
                blocks_of(pe, step)


def shifted_streams(nc, w, mu, hi, lo, rkvz):
    FIRST = 768
    SEGS = ((0, 512, 1), (512, 512, 513), (SEQ, CTX, SEQ + 3))
    PW = TOK + 4
    with Stage(nc, "streams") as st:
        raw = st.sb("raw", [P, 2, KC, P])
        whi = st.sb("whi", [P, 2, KC, P], F32R)
        wlo = st.sb("wlo", [P, 2, KC, P], F32R)
        pad = st.sb("pad", [P, 2, PW])
        near = st.sb("near", [P, 2, PW - 2])
        mix = st.sb("mix", [P, 2, PW - 2])
        mus = st.sb("mus", [P, NFC])
        keep = st.sb("keep", [P, NFC])
        half = st.sb("half", [P, NFC])
        acc = [[st.ps(f"acc{s}{b}", [P, 512]) for b in range(3)] for s in range(2)]
        loaded, prepared = st.sems("loaded", "prepared")
        w_in, high, low, summed, moved, summed2, scaled, mixed, stored = (
            st.sems(f"{n}0", f"{n}1") for n in (
                "w_in", "high", "low", "summed", "moved", "near", "scaled", "mixed", "stored"))
        wv = w.rearrange("(k p) n -> p k n", p=P)
        with nc.Block() as block:
            @block.sync
            def _(sp):
                with nc.allow_non_contiguous_dma(reason="one column of 1792 values"):
                    sp.dma_start(mus[:], mu.rearrange("(c p) -> p c", p=P)).then_inc(loaded, 16)

                def load(i, s, b):
                    sp.wait_ge(low[s], i)
                    sp.dma_start(raw[:, s], wv[:, :, bass.ds(b * P + FIRST, P)]).then_inc(w_in[s], 16)
                two_slots(sp, NFC, load)

            @block.scalar
            def _(act):
                act.wait_ge(prepared, 2)

                def step(i, s, b):
                    act.wait_ge(mixed[s], i)
                    act.wait_ge(summed2[s], i)
                    for n, (t0, n_t, col) in enumerate(SEGS):
                        act.wait_ge(summed[s], i * 3 + n + 1)
                        act.activation(pad[:, s, col:col + n_t], acc[s][n][:, 0:n_t], ACT.Copy).then_inc(moved[s], 1)
                two_slots(act, NFC, step)
                for s in range(2):
                    act.wait_ge(stored[s], NFC // 2 * 32)

            @block.gpsimd
            def _(pool):
                pool.memset(pad[:], 0.0).then_inc(prepared, 1)

                def step(i, s, b):
                    pool.wait_ge(moved[s], i * 3 + 3)
                    pool.wait_ge(mixed[s], i)
                    pool.tensor_tensor(near[:, s], pad[:, s, 0:PW - 2], pad[:, s, 2:PW], ALU.add).then_inc(summed2[s], 1)
                    pool.wait_ge(mixed[s], i + 1)
                    pool.dma_start(rkvz[at(b), :, 0:SEQ].rearrange("a p n -> (a p) n"),
                                   mix[:, s, 0:SEQ]).then_inc(stored[s], 16)
                    pool.dma_start(rkvz[at(b), :, SEQ:TOK].rearrange("a p n -> (a p) n"),
                                   mix[:, s, SEQ + 2:TOK + 2]).then_inc(stored[s], 16)
                two_slots(pool, NFC, step)

            @block.vector
            def _(dve):
                dve.wait_ge(loaded, 16)
                dve.tensor_scalar(keep[:], mus[:], -1.0, 1.0, ALU.mult, ALU.add)
                dve.tensor_scalar(half[:], mus[:], 0.5, None, ALU.mult).then_inc(prepared, 1)
                dve.wait_ge(prepared, 2)

                def split(i, s, b, k):
                    dve.wait_ge(w_in[s], i * 16 + 16)
                    dve.wait_ge(summed[s], i * 3)
                    dve.tensor_copy(whi[:, s], raw[:, s]).then_inc(high[s], 1)
                    dve.wait_ge(high[s], i + 1)
                    dve.tensor_tensor(wlo[:, s], raw[:, s], whi[:, s].bitcast(F32), ALU.subtract).then_inc(low[s], 1)

                def step(i, s, b, k):
                    dve.wait_ge(moved[s], i * 3 + 3)
                    dve.wait_ge(stored[s], i * 32)
                    dve.tensor_scalar(mix[:, s], pad[:, s, 1:PW - 1], keep[:, at(b)], None, ALU.mult).then_inc(scaled[s], 1)
                    dve.wait_ge(scaled[s], i + 1)
                    dve.wait_ge(summed2[s], i + 1)
                    dve.scalar_tensor_tensor(mix[:, s], near[:, s], half[:, at(b)], mix[:, s],
                                             ALU.mult, ALU.add).then_inc(mixed[s], 1)

                skewed(dve, ((0, NFC),), split, step)

            @block.tensor
            def _(pe):
                def step(i, s, b):
                    pe.wait_ge(low[s], i + 1)
                    pe.wait_ge(moved[s], i * 3)
                    for n, (t0, n_t, _) in enumerate(SEGS):
                        split_products(
                            pe, acc[s][n][:, 0:n_t], lambda k: whi[:, s, k, :], lambda k: wlo[:, s, k, :],
                            lambda k: hi[:, k, t0:t0 + n_t], lambda k: lo[:, k, t0:t0 + n_t]).then_inc(summed[s], 1)
                two_slots(pe, NFC, step)


def decayed_streams(nc, rkvz, w0, w2, a0, a2, k_k, k_a, r_k, consts, streams, wcs, vtok, bonus):
    SPANS = ((0, 512), (512, 512), (1024, 256))
    with Stage(nc, "decay") as st:
        ones = st.sb("ones", [P, P])
        ident = st.sb("ident", [P, P])
        carry = st.sb("carry", [P, 2, TOK])
        tz = st.sb("tz", [P, TOK])
        za = st.sb("za", [P, TOK])
        w0c = st.sb("w0c", [P, 2, PAIRS])
        a0c = st.sb("a0c", [P, 2, PAIRS])
        kkc, kac, rkc, kan = (st.sb(n, [P, PAIRS]) for n in ("kkc", "kac", "rkc", "kan"))
        rkv = st.sb("rkv", [P, 2, 3, TOK])
        w2s = st.sb("w2s", [P, 2, P])
        a2s = st.sb("a2s", [P, 2, P])
        sq = st.sb("sq", [P, TOK])
        norm = st.sb("norm", [P, TOK])
        kk = st.sb("kk", [P, TOK])
        sig, rate, cum, before, e_in, e_to, e_from = (
            st.sb(n, [P, TOK]) for n in ("sig", "rate", "cum", "before", "e_in", "e_to", "e_from"))
        b_, km = st.sb("b", [P, TOK]), st.sb("km", [P, 2, TOK])
        out = st.sb("out", [P, NT, 4 * P])
        tot = st.sb("tot", [P, 2, NT])
        vt = st.sb("vt", [P, NT, P])
        bon = st.sb("bon", [P, TOK])
        even = st.ps("even", [P, 3 * 512])
        odd = st.ps("odd", [P, 3 * 512])
        loaded, ready, zin, tanhed = st.sems("loaded", "ready", "zin", "tanhed")
        rkv_in = st.sems("rkv_in0", "rkv_in1")
        def by_tile(ap):
            return ap.rearrange("p (t n) -> p t n", n=P)

        names = ("squared", "even_in", "odd_in", "even_read", "odd_read", "clamped", "inverted", "unit",
                 "rated", "summed", "shifted", "exp_in", "exp_to", "exp_from", "r_done", "a_done", "mixed", "km_done",
                 "k_done", "b_made", "b_done", "totals", "out_stored", "bon_sum", "bon_done", "bon_stored",
                 "sig_used", "v_stored", "tot_stored")
        S = {n: st.sem(n) for n in names}
        with nc.Block() as block:
            @block.sync
            def _(sp):
                sp.dma_start(ones[:], consts[:, C_ONES:C_ONES + P]).then_inc(loaded, 16)
                sp.dma_start(ident[:], consts[:, C_ID:C_ID + P]).then_inc(loaded, 16)
                sp.dma_start(tz[:], rkvz[12]).then_inc(zin, 16)
                sp.dma_start(za[:], rkvz[13]).then_inc(loaded, 16)
                with nc.allow_non_contiguous_dma(reason="columns of 512 values"):
                    for d in range(2):
                        sp.dma_start(w0c[:, d], w0[d].rearrange("(c p) -> p c", p=P)).then_inc(loaded, 16)
                        sp.dma_start(a0c[:, d], a0[d].rearrange("(c p) -> p c", p=P)).then_inc(loaded, 16)
                    for dst, src in ((kkc, k_k), (kac, k_a), (rkc, r_k)):
                        sp.dma_start(dst[:], src.rearrange("(c p) -> p c", p=P)).then_inc(loaded, 16)

                def load(i, s, b):
                    sp.wait_ge(S["bon_done"], i * 2)
                    cols = bass.ds(b * P, P)
                    sp.dma_start(w2s[:, s], w2.rearrange("d r n -> (d r) n")[:, cols]).then_inc(rkv_in[s], 16)
                    sp.dma_start(a2s[:, s], a2.rearrange("d r n -> (d r) n")[:, cols]).then_inc(rkv_in[s], 16)
                    for n in range(3):
                        sp.dma_start(rkv[:, s, n], rkvz[at(b + n * PAIRS)].rearrange("a p n -> (a p) n")
                                     ).then_inc(rkv_in[s], 16)
                two_slots(sp, PAIRS, load)

            @block.scalar
            def _(act):
                act.wait_ge(zin, 16)
                act.activation(tz[:], tz[:], ACT.Tanh).then_inc(tanhed, 1)
                act.wait_ge(ready, 4)

                def step(i, s, b):
                    act.wait_ge(rkv_in[s], i * 80 + 80)
                    act.wait_ge(S["even_in"], b * 3)
                    act.activation(sq[:], rkv[:, s, 1], ACT.Square, scale=kkc[:, at(b)]).then_inc(S["squared"], 1)
                    act.wait_ge(S["even_in"], b * 3 + 1)
                    act.wait_ge(S["unit"], b)
                    act.activation(norm[:], even[:, 0:TOK], ACT.Sqrt).then_inc(S["even_read"], 1)
                    for d in range(2):
                        n = b * 2 + d
                        act.wait_ge(S["odd_in"], b * 3 + d + 1)
                        act.wait_ge(S["b_made"], n)
                        act.activation(rate[:], odd[:, 0:TOK], ACT.Sigmoid, bias=w0c[:, d, at(b)]).then_inc(S["odd_read"], 1)
                        act.wait_ge(S["even_in"], b * 3 + d + 2)
                        act.wait_ge(S["mixed"], n)
                        act.activation(sig[:], even[:, 0:TOK], ACT.Sigmoid, bias=a0c[:, d, at(b)]).then_inc(S["even_read"], 1)
                        act.wait_ge(S["summed"], n + 1)
                        act.wait_ge(S["r_done"], n)
                        act.activation(e_to[:], cum[:], ACT.Exp).then_inc(S["exp_to"], 1)
                        act.wait_ge(S["b_done"], n)
                        act.activation(e_from[:], cum[:], ACT.Exp, scale=-1.0).then_inc(S["exp_from"], 1)
                        act.wait_ge(S["shifted"], n + 1)
                        act.wait_ge(S["a_done"], n)
                        act.activation(e_in[:], before[:], ACT.Exp).then_inc(S["exp_in"], 1)
                        act.wait_ge(S["exp_to"], n + 1)
                        act.wait_ge(S["tot_stored"], n * 16)
                        first = CHUNK - 1 if d == 0 else 0
                        act.activation(tot[:].rearrange("p c t -> p t c"), e_to[:, first::CHUNK].rearrange("p (t c) -> p t c", c=2),
                                       ACT.Copy).then_inc(S["totals"], 1)
                        act.wait_ge(S["totals"], n + 1)
                        act.dma_start(wcs[d][at(b)].rearrange("a p c t -> (a p) c t"), tot[:]).then_inc(S["tot_stored"], 16)
                    act.wait_ge(S["odd_in"], b * 3 + 3)
                    act.wait_ge(S["v_stored"], b * 16)
                    act.activation(vt[:].rearrange("p t n -> p (t n)"), odd[:, 0:TOK], ACT.Copy).then_inc(S["odd_read"], 1)
                    act.wait_ge(S["odd_read"], b * 3 + 3)
                    act.dma_start(vtok.rearrange("(t p) n -> p t n", p=P)[:, :, bass.ds(b * P, P)], vt[:]
                                  ).then_inc(S["v_stored"], 16)
                two_slots(act, PAIRS, step)
                act.wait_ge(S["v_stored"], PAIRS * 16)
                act.wait_ge(S["tot_stored"], PAIRS * 32)

            @block.gpsimd
            def _(pool):
                pool.memset(carry[:], 1.0).then_inc(ready, 1)
                pool.wait_ge(ready, 2)
                pool.memset(carry[:, 0, ::CHUNK], 0.0).then_inc(ready, 1)
                pool.memset(carry[:, 1, CHUNK - 1::CHUNK], 0.0).then_inc(ready, 1)

                def step(i, s, b):
                    for d in range(2):
                        n = b * 2 + d
                        pool.wait_ge(rkv_in[s], i * 80 + 80)
                        pool.wait_ge(S["exp_to"], n + 1)
                        pool.wait_ge(S["out_stored"], n * 16)
                        pool.tensor_tensor(out[:, :, 0:P], by_tile(rkv[:, s, 0]), by_tile(e_to[:]), ALU.mult).then_inc(S["r_done"], 1)
                        pool.wait_ge(S["r_done"], n + 1)
                        pool.wait_ge(S["a_done"], n + 1)
                        pool.wait_ge(S["k_done"], n + 1)
                        pool.wait_ge(S["b_done"], n + 1)
                        pool.dma_start(streams[d][at(b)].rearrange("a p t n -> (a p) t n"), out[:]
                                       ).then_inc(S["out_stored"], 16)
                    pool.wait_ge(S["bon_done"], b + 1)
                    pool.dma_start(bonus[at(b)].rearrange("a p n -> (a p) n"), bon[:]).then_inc(S["bon_stored"], 16)
                two_slots(pool, PAIRS, step)
                pool.wait_ge(S["out_stored"], PAIRS * 32)
                pool.wait_ge(S["bon_stored"], PAIRS * 16)

            @block.vector
            def _(dve):
                dve.wait_ge(loaded, 16 * 10)
                dve.tensor_scalar(kan[:], kac[:], -1.0, 1.0, ALU.mult, ALU.add).then_inc(ready, 1)
                dve.wait_ge(ready, 4)

                def step(i, s, b):
                    k = rkv[:, s, 1]
                    dve.wait_ge(rkv_in[s], i * 80 + 80)
                    dve.wait_ge(S["even_read"], b * 3 + 1)
                    dve.tensor_scalar(norm[:], norm[:], 1e-12, None, ALU.max).then_inc(S["clamped"], 1)
                    dve.wait_ge(S["clamped"], b + 1)
                    dve.reciprocal(norm[:], norm[:]).then_inc(S["inverted"], 1)
                    dve.wait_ge(S["inverted"], b + 1)
                    dve.scalar_tensor_tensor(kk[:], k, kkc[:, at(b)], norm[:], ALU.mult, ALU.mult).then_inc(S["unit"], 1)
                    for d in range(2):
                        n = b * 2 + d
                        back = slice(None, None, 1 if d == 0 else -1)
                        dve.wait_ge(S["odd_read"], b * 3 + d + 1)
                        dve.tensor_scalar(rate[:], rate[:], -DECAY, None, ALU.mult).then_inc(S["rated"], 1)
                        dve.wait_ge(S["rated"], n + 1)
                        dve.wait_ge(S["exp_from"], n)
                        dve.tensor_tensor_scan(cum[:, back], carry[:, d, back], rate[:, back], 0.0,
                                               ALU.mult, ALU.add).then_inc(S["summed"], 1)
                        dve.wait_ge(S["summed"], n + 1)
                        dve.wait_ge(S["exp_in"], n)
                        dve.tensor_tensor(before[:], cum[:], rate[:], ALU.subtract).then_inc(S["shifted"], 1)
                        dve.wait_ge(S["even_read"], b * 3 + d + 2)
                        if d == 0:
                            dve.wait_ge(S["bon_sum"], b)
                        dve.tensor_scalar(km[:, d], sig[:], kac[:, at(b)], kan[:, at(b)],
                                          ALU.mult, ALU.add).then_inc(S["mixed"], 1)
                        dve.wait_ge(S["mixed"], n + 1)
                        dve.wait_ge(S["unit"], b + 1)
                        dve.tensor_tensor(b_[:], kk[:], sig[:], ALU.mult).then_inc(S["b_made"], 1)
                        dve.tensor_tensor(km[:, d], km[:, d], k, ALU.mult).then_inc(S["km_done"], 1)
                        dve.wait_ge(S["exp_in"], n + 1)
                        dve.wait_ge(S["out_stored"], n * 16)
                        dve.tensor_tensor(out[:, :, P:2 * P], by_tile(kk[:]), by_tile(e_in[:]), ALU.mult).then_inc(S["a_done"], 1)
                        dve.wait_ge(S["km_done"], n + 1)
                        dve.wait_ge(S["exp_from"], n + 1)
                        dve.tensor_tensor(out[:, :, 2 * P + HD:3 * P + HD], by_tile(km[:, d]), by_tile(e_from[:]), ALU.mult).then_inc(S["k_done"], 1)
                        dve.wait_ge(S["b_made"], n + 1)
                        for c, to in ((0, 2 * P), (1, 3 * P + HD)):
                            half = slice(c * CHUNK, (c + 1) * CHUNK)
                            last = dve.tensor_tensor(out[:, :, to:to + CHUNK], by_tile(b_[:])[:, :, half],
                                                     by_tile(e_from[:])[:, :, half], ALU.mult)
                        last.then_inc(S["b_done"], 1)
                    dve.wait_ge(S["bon_stored"], b * 16)
                    dve.wait_ge(S["km_done"], b * 2 + 2)
                    dve.tensor_tensor(bon[:], km[:, 0], km[:, 1], ALU.add).then_inc(S["bon_sum"], 1)
                    dve.wait_ge(S["bon_sum"], b + 1)
                    dve.wait_ge(S["r_done"], b * 2 + 2)
                    dve.wait_ge(S["odd_in"], b * 3 + 3)
                    dve.scalar_tensor_tensor(bon[:], rkv[:, s, 0], rkc[:, at(b)], bon[:], ALU.mult, ALU.mult
                                             ).then_inc(S["bon_done"], 1)
                two_slots(dve, PAIRS, step)

            @block.tensor
            def _(pe):
                pe.wait_ge(loaded, 16 * 10)
                pe.wait_ge(tanhed, 1)

                def spans(out_, lhs, rhs):
                    for t0, n in SPANS:
                        last = pe.matmul(out_[:, t0:t0 + n], lhs, rhs[:, t0:t0 + n], start=True, stop=True)
                    return last

                def step(i, s, b):
                    pe.wait_ge(S["squared"], b + 1)
                    pe.wait_ge(S["even_read"], b * 3)
                    spans(even, ones[:], sq).then_inc(S["even_in"], 1)
                    pe.wait_ge(rkv_in[s], i * 80 + 80)
                    for d in range(2):
                        half = slice(d * HD, (d + 1) * HD)
                        pe.wait_ge(S["odd_read"], b * 3 + d)
                        spans(odd, w2s[half, s], tz[half]).then_inc(S["odd_in"], 1)
                        pe.wait_ge(S["even_read"], b * 3 + d + 1)
                        spans(even, a2s[half, s], za[half]).then_inc(S["even_in"], 1)
                    pe.wait_ge(S["odd_read"], b * 3 + 2)
                    for t in range(NT):
                        last = pe.transpose(odd[:, t * P:(t + 1) * P], rkv[:, s, 2, t * P:(t + 1) * P], ident[:])
                    last.then_inc(S["odd_in"], 1)
                two_slots(pe, PAIRS, step)



def chunked_scan(nc, streams, wcs, vtok, consts, ydir):
    with Stage(nc, "scan") as st:
        ident = st.sb("ident", [P, P])
        stacked = st.sb("stacked", [P, 2, HD])
        gmask = st.sb("gmask", [P, 2, 2, CHUNK])
        lmask = st.sb("lmask", [P, LEVELS + 1, P])
        state = st.sb("state", [P, 2, PAIRS, 2, HD])
        wend = st.sb("wend", [P, 2, PAIRS, 2, NT])
        G = range(2)
        L = [st.sb(f"L{g}", [P, 2, 4 * P]) for g in G]
        RI = [st.sb(f"RI{g}", [P, 4, P]) for g in G]
        LT = [st.sb(f"LT{g}", [P, 4, P]) for g in G]
        AK = [st.sb(f"AK{g}", [P, 4, P]) for g in G]
        AV = [st.sb(f"AV{g}", [P, 4, P]) for g in G]
        off = [st.sb(f"off{g}", [P, 4, LEVELS, P]) for g in G]
        X = [st.sb(f"X{g}", [P, 4, P]) for g in G]
        XT = [st.sb(f"XT{g}", [P, 4, P]) for g in G]
        Y = [st.sb(f"Y{g}", [P, 4, P]) for g in G]
        P1 = [st.sb(f"P1{g}", [P, 4, P]) for g in G]
        YO = [st.sb(f"YO{g}", [P, 4, HD]) for g in G]
        V = [st.sb(f"V{g}", [P, 2, P]) for g in G]
        U = [[st.sb(f"U{r}{g}", [P, 4, 2, P]) for g in G] for r in range(2)]
        PV = [[st.sb(f"PV{r}{g}", [P, 4, 2, HD]) for g in G] for r in range(2)]
        EQ = [[st.sb(f"EQ{r}{g}", [P, 4, P]) for g in G] for r in range(2)]
        banks = st.ps("gram", [P, 2, 512])
        small = [st.ps(f"small{g}", [P, 4, P]) for g in G]
        gram = banks[:, :, 0:2 * P].rearrange("p h (c n) -> p h c n", c=2)
        wide = [st.ps(f"wide{g}", [P, 4, P]) for g in G]
        sums = [st.ps(f"sums{d}", [P, 2, 2, P]) for d in range(2)]
        SMALL = 2 + 2 * LEVELS - 1
        WIDE = 2 + LEVELS + 2

        loaded, ready = st.sems("loaded", "ready")
        gram_in, gram_read = st.sems("gram_in", "gram_read")
        (l_in, r_in, small_in, small_read, wide_in, wide_read, masked, first_x, state_new, y_read, stored) = (
            st.sems(f"{n}0", f"{n}1") for n in (
                "l_in", "r_in", "small_in", "small_read", "wide_in", "wide_read", "masked", "first_x",
                "state_new", "y_read", "stored"))
        v_in = st.sems("v_in0", "v_in1")
        pv_in = [st.sems(f"pv_in{r}0", f"pv_in{r}1") for r in range(2)]
        z_in = [st.sems(f"z_in{r}0", f"z_in{r}1") for r in range(2)]

        HALF = ("t0 -a2 t1 gram0 -b2 -c2 -a3 gram1 -b3 first -c3 av -a4 x0 z -c4 a0 -p r b0 c0 -eq a1 z b1 r c1").split()

        def mixed(early, late):
            return [(name.lstrip("-"), late if name[0] == "-" else early, name[0] == "-") for name in HALF]

        def schedule(eng, stages, z=None, read=None, load=None, store=None):
            def both(ahead, now):
                if ahead and load:
                    load(*ahead)
                for early in G:
                    chunk = {"z": 0, "r": 0}
                    for name, g, is_late in mixed(early, 1 - early):
                        if name in chunk:
                            hook = z if name == "z" else read
                            if now and hook:
                                hook(chunk[name], g, *now)
                            chunk[name] += 1
                            continue
                        step = now if early == 0 and is_late else ahead
                        if step and name in stages:
                            stages[name](g, *step)
                    if now and store:
                        store(early, *now)

            def steps(j, t0, t1, base):
                tiles = (j + t0, (j * -1) + t1)
                return tuple((j * 2 + (base + r), r, j + base // 2, tiles) for r in range(2))

            c, x = (NTX, NTX + NTC - 1, 0), (0, NTX - 1, 2 * NTC)

            def tile(j, phase):
                s0, s1 = steps(j, *phase)
                both(s1, s0)
                both(steps(j + 1, *phase)[0], s1)

            both(steps(0, *c)[0], None)
            loop(eng, NTC - 1, lambda j: tile(j, c))
            s0, s1 = steps(NTC - 1, *c)
            both(s1, s0)
            both(steps(0, *x)[0], s1)
            loop(eng, NTX - 1, lambda j: tile(j, x), peel=False)
            s0, s1 = steps(NTX - 1, *x)
            both(s1, s0)
            both(None, s1)

        def pair(r, g):
            return 2 * r + g

        def half_of(c):
            return slice(c * HD, (c + 1) * HD)

        def small_n(n, m):
            return n * SMALL + m

        def wide_n(n, m):
            return n * WIDE + m

        A_USE = [2 + 2 * k for k in range(LEVELS)]
        C_USE = [2 + k for k in range(LEVELS)]

        with nc.Block() as block:
            @block.sync
            def _(sp):
                sp.dma_start(ident[:], consts[:, C_ID:C_ID + P]).then_inc(loaded, 16)
                for c in range(2):
                    sp.dma_start(stacked[:, c], consts[:, C_SUM:C_SUM + HD]).then_inc(loaded, 16)
                sp.dma_start(gmask[:].rearrange("p a b n -> p (a b n)"), consts[:, C_GRAM:C_GRAM + 4 * CHUNK]).then_inc(loaded, 16)
                sp.dma_start(lmask[:].rearrange("p a n -> p (a n)"), consts[:, C_LEV:C_LEV + (LEVELS + 1) * P]).then_inc(loaded, 16)
                with nc.allow_non_contiguous_dma(reason="one decay per chunk and feature"):
                    for c in range(2):
                        for d in range(2):
                            for h in range(2):
                                sp.dma_start(wend[half_of(1 - c), d, :, h, :],
                                             wcs[d].rearrange("q (h k) c t -> h c k q t", h=2)[h, c]
                                             ).then_inc(loaded, 16)
                for g in G:
                    for c in range(2):
                        for u in range(4):
                            sp.dma_start(RI[g][half_of(c), u, half_of(1 - c)],
                                         consts[0:HD, C_ID:C_ID + HD]).then_inc(loaded, 16)

                def load(n, r, m, tiles):
                    for g in G:
                        sp.wait_ge(masked[g], n * 4)
                        for d in range(2):
                            sp.dma_start(L[g][:, d], streams[d, pair(r, g), :, at(tiles[d])].rearrange("p a n -> p (a n)")
                                         ).then_inc(l_in[g], 16)
                    for g in G:
                        sp.wait_ge(z_in[r][g], m * 2)
                        for d in range(2):
                            for c in range(2):
                                v = vtok[bass.ds(tiles[d] * P + c * CHUNK, CHUNK), pair(r, g) * P:(pair(r, g) + 1) * P]
                                sp.dma_start(PV[r][g][half_of(1 - c), 2 * d:2 * d + 2, c, :],
                                             v.rearrange("t (h v) -> t h v", h=2)).then_inc(pv_in[r][g], 16)
                    for g in G:
                        sp.wait_ge(wide_read[g], n * WIDE)
                        for d in range(2):
                            for c in range(2):
                                sp.dma_start(
                                    RI[g][half_of(c), 2 * d:2 * d + 2, half_of(c)],
                                    streams[d, pair(r, g), :, at(tiles[d]), c * CHUNK:(c + 1) * CHUNK].rearrange(
                                        "(h k) a n -> k h (a n)", h=2)).then_inc(r_in[g], 16)
                schedule(sp, {}, load=load)

            @block.gpsimd
            def _(pool):
                pool.memset(state[:], 0.0).then_inc(ready, 1)
                for g in G:
                    for blocks in (P1, LT, AK):
                        pool.memset(blocks[g][:], 0.0).then_inc(ready, 1)
                pool.wait_ge(loaded, 16 * (5 + 8 + 16))

                def off_diagonals(d):
                    def mask(g, n, r, m, tiles):
                        if d == 0:
                            pool.wait_ge(small_in[g], n * SMALL)
                        pool.wait_ge(gram_read, n * 4 + 2 * g + d + 1)
                        for u in (2 * d, 2 * d + 1):
                            pool.tensor_tensor(off[g][:, u], LT[g][:, u:u + 1, :].to_broadcast([P, LEVELS, P]),
                                               lmask[:, 1:], ALU.mult).then_inc(masked[g], 1)
                    return mask

                def values(g, n, r, m, tiles):
                    pool.wait_ge(small_in[g], n * SMALL)
                    for d in range(2):
                        for c in range(2):
                            pool.dma_start(V[g][half_of(1 - c), d],
                                           vtok[bass.ds(tiles[d] * P + c * CHUNK, CHUNK), pair(r, g) * P:(pair(r, g) + 1) * P]
                                           ).then_inc(v_in[g], 16)
                schedule(pool, {"t0": values, "gram0": off_diagonals(0), "gram1": off_diagonals(1)})

            @block.scalar
            def _(act):
                act.wait_ge(ready, 7)

                def turned(d):
                    def copy(g, n, r, m, tiles):
                        us = slice(2 * d, 2 * d + 2)
                        act.wait_ge(wide_in[g], wide_n(n, d + 1))
                        w = wide[g][:].rearrange("p f (h k) -> p f h k", h=2)
                        act.activation(AV[g][:, us, 0:HD], w[:, 0], ACT.Copy)
                        for c in range(2):
                            last = act.activation(U[r][g][:, us, c, half_of(1 - c)], w[:, 1 + c], ACT.Copy)
                        last.then_inc(wide_read[g], 1)
                    return copy

                def av(g, n, r, m, tiles):
                    act.wait_ge(small_in[g], small_n(n, 1))
                    act.activation(AV[g][:, :, HD:P], small[g][:, :, 0:HD], ACT.Copy).then_inc(small_read[g], 1)

                def first(g, n, r, m, tiles):
                    act.wait_ge(small_in[g], small_n(n, 2))
                    act.activation(X[g][:], small[g][:], ACT.Copy).then_inc(small_read[g], 1)

                def level(k):
                    def copy(g, n, r, m, tiles):
                        act.wait_ge(small_in[g], small_n(n, A_USE[k] + 1))
                        act.activation(Y[g][:], small[g][:], ACT.Copy).then_inc(small_read[g], 1)
                    return copy

                def p(g, n, r, m, tiles):
                    act.wait_ge(wide_in[g], wide_n(n, WIDE - 1))
                    for c in range(2):
                        act.activation(P1[g][half_of(c), :, half_of(c)], wide[g][half_of(c), :, 0:HD], ACT.Copy, scale=-1.0)
                        last = act.activation(PV[r][g][half_of(c), :, c, :], wide[g][half_of(c), :, HD:P], ACT.Copy, scale=-1.0)
                    last.then_inc(wide_read[g], 1)

                def read(x, g, n, r, m, tiles):
                    if x == 0:
                        act.wait_ge(stored[g], n * 32)
                    act.wait_ge(z_in[r][g], m * 2 + x + 1)
                    for d in range(2):
                        c = x ^ d
                        last = act.activation(YO[g][half_of(c), 2 * d:2 * d + 2, :],
                                              sums[d][half_of(c), x, g].rearrange("p (h v) -> p h v", h=2), ACT.Copy)
                    last.then_inc(y_read[g], 1)

                def store(g, n, r, m, tiles):
                    act.wait_ge(y_read[g], n * 2 + 2)
                    for d in range(2):
                        act.dma_start(
                            ydir[d, bass.ds(tiles[d] * P, P), pair(r, g) * P:(pair(r, g) + 1) * P],
                            YO[g][:, 2 * d:2 * d + 2, :].rearrange("p h v -> p (h v)")).then_inc(stored[g], 16)
                stages = {"t0": turned(0), "t1": turned(1), "av": av, "x0": first, "p": p}
                stages.update({f"a{k}": level(k) for k in range(LEVELS)})
                schedule(act, stages, read=read, store=store)
                for g in G:
                    act.wait_ge(stored[g], 2 * NT * 32)

            @block.vector
            def _(dve):
                dve.wait_ge(loaded, 16 * (5 + 8 + 16))

                def masked_gram(d):
                    def mask(g, n, r, m, tiles):
                        if d == 0:
                            dve.wait_ge(masked[g], n * 4)
                            dve.wait_ge(small_in[g], n * SMALL)
                        us = slice(2 * d, 2 * d + 2)
                        dve.wait_ge(gram_in, n * 4 + 2 * g + d + 1)
                        for c in range(2):
                            dve.tensor_tensor(U[r][g][:, us, c, half_of(c)], gram[:, :, c, 0:CHUNK],
                                              gmask[:, d, 0:1, :].to_broadcast([P, 2, CHUNK]), ALU.mult)
                            for blocks, q in ((LT, c), (AK, 1 - c)):
                                last = dve.tensor_tensor(blocks[g][half_of(q), us, half_of(c)], gram[half_of(q), :, c, CHUNK:],
                                                         gmask[half_of(q), d, 1:2, :].to_broadcast([HD, 2, CHUNK]), ALU.mult)
                        last.then_inc(gram_read, 1)
                    return mask

                def first(g, n, r, m, tiles):
                    dve.wait_ge(gram_read, n * 4 + 2 * g + 2)
                    dve.wait_ge(wide_in[g], n * WIDE)
                    dve.tensor_tensor(XT[g][:], LT[g][:], lmask[:, 0:1, :].to_broadcast([P, 4, P]),
                                      ALU.mult).then_inc(first_x[g], 1)
                    dve.wait_ge(first_x[g], n * 2 + 1)
                    dve.tensor_tensor(XT[g][:], ident[:, None, :].to_broadcast([P, 4, P]), XT[g][:],
                                      ALU.subtract).then_inc(first_x[g], 1)

                def x_less(k):
                    def less(g, n, r, m, tiles):
                        dve.wait_ge(small_in[g], small_n(n, A_USE[k] + 2))
                        dve.tensor_tensor(X[g][:], X[g][:], small[g][:], ALU.subtract).then_inc(small_read[g], 1)
                    return less

                def xt_less(k):
                    def less(g, n, r, m, tiles):
                        dve.wait_ge(wide_in[g], wide_n(n, C_USE[k] + 1))
                        for c in range(2):
                            blk = (half_of(c), slice(None), half_of(c))
                            last = dve.tensor_tensor(XT[g][blk], XT[g][blk], wide[g][blk], ALU.subtract)
                        last.then_inc(wide_read[g], 1)
                    return less

                def eq(g, n, r, m, tiles):
                    dve.wait_ge(r_in[g], n * 64 + 64)
                    dve.wait_ge(wide_in[g], wide_n(n, WIDE))
                    dve.tensor_tensor(EQ[r][g][:], wide[g][:], RI[g][:], ALU.add).then_inc(wide_read[g], 1)

                def read(x, g, n, r, m, tiles):
                    dve.wait_ge(z_in[r][g], m * 2 + x + 1)
                    for d in range(2):
                        half = half_of(1 - (x ^ d))
                        last = dve.tensor_tensor(
                            state[half, d, pair(r, g)], sums[d][half, x, g].rearrange("p (h v) -> p h v", h=2),
                            wend[half, d, pair(r, g), :, bass.ds(tiles[d], 1)].to_broadcast([HD, 2, HD]), ALU.mult)
                    last.then_inc(state_new[g], 1)
                stages = {f"gram{d}": masked_gram(d) for d in range(2)}
                stages.update({"first": first, "eq": eq})
                stages.update({f"b{k}": x_less(k) for k in range(LEVELS - 1)})
                stages.update({f"c{k}": xt_less(k) for k in range(LEVELS)})
                schedule(dve, stages, read=read)

            @block.tensor
            def _(pe):
                pe.wait_ge(loaded, 16 * (5 + 8 + 16))
                pe.wait_ge(ready, 7)

                def small_free(g, n, m):
                    pe.wait_ge(small_read[g], small_n(n, m))

                def wide_free(g, n, m):
                    pe.wait_ge(wide_read[g], wide_n(n, m))

                def turned(d):
                    def turn(g, n, r, m, tiles):
                        if d == 0:
                            pe.wait_ge(l_in[g], n * 32 + 32)
                        wide_free(g, n, d)
                        for f in range(3):
                            last = pe.transpose(wide[g][:, f, :], L[g][:, d, (f + 1) * P:(f + 2) * P], ident[:])
                        last.then_inc(wide_in[g], 1)
                    return turn

                def grams(d):
                    def products(g, n, r, m, tiles):
                        pe.wait_ge(gram_read, n * 4 + 2 * g + d)
                        for h in range(2):
                            ra = L[g][half_of(h), d, 0:2 * P].rearrange("p (f n) -> p f n", f=2)
                            for c in range(2):
                                last = pe.matmul(gram[:, h, c, :],
                                                 L[g][half_of(h), d, (2 + c) * P:(3 + c) * P], ra[:, :, half_of(c)],
                                                 start=True, stop=True)
                        last.then_inc(gram_in, 1)
                    return products

                def av(g, n, r, m, tiles):
                    small_free(g, n, 0)
                    pe.wait_ge(v_in[g], n * 64 + 64)
                    pe.wait_ge(gram_read, n * 4 + 2 * g + 2)
                    for u in range(4):
                        last = pe.matmul(small[g][:, u, 0:HD], AK[g][:, u, :],
                                         V[g][:, u // 2, (u % 2) * HD:(u % 2 + 1) * HD], start=True, stop=True)
                    last.then_inc(small_in[g], 1)

                def first(g, n, r, m, tiles):
                    small_free(g, n, 1)
                    pe.wait_ge(first_x[g], n * 2 + 2)
                    for u in range(4):
                        last = pe.matmul(small[g][:, u, :], XT[g][:, u, :], stacked[:].rearrange("p a n -> p (a n)"), start=True, stop=True)
                    last.then_inc(small_in[g], 1)

                def y_of(k):
                    def products(g, n, r, m, tiles):
                        small_free(g, n, A_USE[k])
                        pe.wait_ge(masked[g], n * 4 + 4)
                        for u in range(4):
                            last = pe.matmul(small[g][:, u, :], off[g][:, u, k, :], X[g][:, u, :], start=True, stop=True)
                        last.then_inc(small_in[g], 1)
                    return products

                def xy(k):
                    def products(g, n, r, m, tiles):
                        small_free(g, n, A_USE[k] + 1)
                        wide_free(g, n, C_USE[k])
                        for u in range(4):
                            last = pe.matmul(small[g][:, u, :], XT[g][:, u, :], Y[g][:, u, :], start=True, stop=True)
                        last.then_inc(small_in[g], 1)
                    return products

                def yt_xt(k):
                    def products(g, n, r, m, tiles):
                        small_free(g, n, A_USE[k] + 1)
                        wide_free(g, n, C_USE[k])
                        for u in range(4):
                            last = pe.matmul(wide[g][:, u, :], Y[g][:, u, :], XT[g][:, u, :],
                                             start=True, stop=True)
                        last.then_inc(wide_in[g], 1)
                    return products

                def p(g, n, r, m, tiles):
                    wide_free(g, n, WIDE - 2)
                    for u in range(4):
                        last = pe.matmul(wide[g][:, u, :], XT[g][:, u, :], AV[g][:, u, :], start=True, stop=True)
                    last.then_inc(wide_in[g], 1)

                def eq(g, n, r, m, tiles):
                    wide_free(g, n, WIDE - 1)
                    for u in range(4):
                        for c in range(2):
                            last = pe.matmul(wide[g][half_of(c), u, :], P1[g][:, u, half_of(c)], U[r][g][:, u, c, :],
                                             start=True, stop=True)
                    last.then_inc(wide_in[g], 1)

                def z(x, g, n, r, m, tiles):
                    wide_free(g, n, WIDE)
                    pe.wait_ge(pv_in[r][g], m * 64 + 64)
                    pe.wait_ge(state_new[g], n * 2 + x)
                    pe.wait_ge(y_read[g], n * 2 + x)
                    pe.wait_ge(state_new[1 - g], n * 2 + 2 * g)
                    pe.wait_ge(y_read[1 - g], n * 2 + 2 * g)
                    for u in range(4):
                        d, h = u // 2, u % 2
                        c = x ^ d
                        half = half_of(c)
                        cols = slice(h * HD, (h + 1) * HD)
                        out = sums[d][:, x, g, cols]
                        pe.matmul(out, U[r][g][:, u, c, :], PV[r][g][:, u, c, :], start=True, stop=False)
                        last = pe.matmul(out, EQ[r][g][half, u, :], state[half, d, pair(r, g), h, :], start=False, stop=True)
                    last.then_inc(z_in[r][g], 1)
                stages = {"t0": turned(0), "t1": turned(1), "av": av, "x0": first, "p": p, "eq": eq}
                stages.update({f"gram{d}": grams(d) for d in range(2)})
                stages.update({f"a{k}": y_of(k) for k in range(LEVELS)})
                stages.update({f"b{k}": xy(k) for k in range(LEVELS - 1)})
                stages.update({f"c{k}": yt_xt(k) for k in range(LEVELS)})
                schedule(pe, stages, z=z)


def head_stream(st, tag, loaded, ident, rope, parts, src, nh, gain, qst=None, kst=None, vst=None, pad=0):
    keys = kst is not None
    W = nh * HD
    NG = 1 if keys else nh // R
    gains = st.sb(tag + "gains", [P, HD])
    x = st.sb(tag + "x", [P, 2, W * (2 if keys else 1)])
    cs = st.sb(tag + "cs", [P, 2, 2, 32])
    turns_by = st.sb(tag + "turns_by", [P, 2, 2, HD])
    sq = st.sb(tag + "sq", [P, 2, W])
    ss, ms, rt, r0, t0, t1, rstd = (st.sb(tag + n, [P, 2, nh]) for n in ("ss", "ms", "rt", "r0", "t0", "t1", "rstd"))
    xn = st.sb(tag + "xn", [P, 2, W])
    xc = st.sb(tag + "xc", [P, 2, W])
    xs = st.sb(tag + "xs", [P, 2, W])
    xr = st.sb(tag + "xr", [P, 2, nh, 2, HD])
    NBK = 2 if keys else 4
    bank = [st.ps(f"{tag}bank{b}", [P, 4, P]) for b in range(NBK)]
    hl = [st.sb(f"{tag}hl{b}", [P, 2 if keys else 1, nh if keys else R, P], F32R) for b in range(NBK)]
    vs = st.sb(tag + "vs", [P, 2, nh, 2, HD], F32R) if keys else None
    (x_in, squared, summed, meaned, rooted, inv, nwt, tabled, scaled, cosd, sind, rotated, v_hi, v_lo) = (
        st.sems(f"{tag}{n}0", f"{tag}{n}1") for n in (
            "x_in", "squared", "summed", "meaned", "rooted", "inverted", "newton", "tabled", "scaled", "cosined",
            "sined", "rotated", "v_hi", "v_lo"))
    v_stored, twice = (st.sems(f"{tag}{n}0", f"{tag}{n}1") for n in ("v_stored", "twice"))
    turned, high, low, stored = (
        st.sems(*(f"{tag}{n}{b}" for b in range(NBK))) for n in ("turned", "high", "low", "stored"))

    def uses(i, s, g):
        if NG == NBK:
            return i * 2 + s, g
        return i, s * NG + g

    def pairs_of(t):
        return t.rearrange("p (h a b) -> p h a b", h=nh, b=2)

    def load(sp, i, s, t, k):
        sp.wait_ge(rotated[s], i * 2)
        if keys:
            sp.wait_ge(v_lo[s], i)
        sp.dma_start(x[:, s], rows(src, t)).then_inc(x_in[s], 16)
        sp.dma_start(cs[:, s], rows(rope, t)).then_inc(x_in[s], 16)

    def square(act, i, s, t, k):
        act.wait_ge(x_in[s], i * 32 + 32)
        act.wait_ge(summed[s], i)
        act.activation(sq[:, s], x[:, s, 0:W], ACT.Square).then_inc(squared[s], 1)
        act.wait_ge(meaned[s], i + 1)
        act.wait_ge(inv[s], i)
        act.activation(rt[:, s], ms[:, s], ACT.Sqrt).then_inc(rooted[s], 1)

    def keep_high(act, i, s, t, k):
        for g in range(NG):
            n, b = uses(i, s, g)
            act.wait_ge(turned[b], n + 1)
            act.wait_ge(stored[b], n * 16)
            act.activation(hl[b][:, 0, 0:nh] if keys else hl[b][:, 0], bank[b][:, 0:nh, :] if keys else bank[b][:],
                           ACT.Copy).then_inc(high[b], 1)

    def double(act, i, s, t, k):
        act.wait_ge(rotated[s], i * 2 + 2)
        act.activation(xr[:, s, :, 1, :], xr[:, s, :, 0, :], ACT.Copy).then_inc(twice[s], 1)

    def tables(pool, i, s, t, k):
        pool.wait_ge(x_in[s], i * 32 + 32)
        pool.wait_ge(rotated[s], i * 2)
        pool.tensor_tensor(turns_by[:, s].rearrange("p f (a b) -> p f a b", b=2),
                           cs[:, s, :, :, None].to_broadcast([P, 2, 32, 2]),
                           gains[:].rearrange("p (f a b) -> p f a b", f=1, b=2).to_broadcast([P, 2, 32, 2]),
                           ALU.mult).then_inc(tabled[s], 1)

    def sines(pool, i, s, t, k):
        pool.wait_ge(scaled[s], i + 1)
        pool.wait_ge(tabled[s], i + 1)
        pool.tensor_tensor(xs[:, s].rearrange("p (h d) -> p h d", h=nh), xn[:, s].rearrange("p (h d) -> p h d", h=nh),
                           turns_by[:, s, 1:2, :].to_broadcast([P, nh, HD]), ALU.mult).then_inc(sind[s], 1)

    def store(pool, i, s, t, k):
        col = t * P + (pad if parts[k][0] < NTX else 2 * pad)
        if keys:
            pool.wait_ge(v_lo[s], i + 1)
            pool.dma_start(vst[bass.ds(col, P)], vs[:, s].rearrange("p h a d -> p h (a d)").bitcast(F32)
                         ).then_inc(v_stored[s], 16)
        for g in range(NG):
            n, b = uses(i, s, g)
            pool.wait_ge(low[b], n + 1)
            if keys:
                pool.dma_start(kst[:, :, :, bass.ds(col, P)].rearrange("p a h n -> p (a h) n"),
                               hl[b][:].rearrange("p a h n -> p (a h) n").bitcast(F32)).then_inc(stored[b], 16)
            else:
                pool.dma_start(qst[at(t), g].rearrange("a p n -> (a p) n"),
                             hl[b][:, 0].rearrange("p r n -> p (r n)").bitcast(F32)).then_inc(stored[b], 16)

    def mean_squares(dve, i, s, t, k):
        dve.wait_ge(squared[s], i + 1)
        dve.wait_ge(meaned[s], i)
        dve.tensor_reduce(ss[:, s], sq[:, s].rearrange("p (h d) -> p h d", h=nh), AX, ALU.add).then_inc(summed[s], 1)
        dve.wait_ge(summed[s], i + 1)
        dve.tensor_scalar(ms[:, s], ss[:, s], 1.0 / HD, EPS, ALU.mult, ALU.add).then_inc(meaned[s], 1)
        if keys:
            v = x[:, s, W:2 * W].rearrange("p (h d) -> p h d", h=nh)
            dve.wait_ge(v_stored[s], i * 16)
            dve.tensor_copy(vs[:, s, :, 0], v).then_inc(v_hi[s], 1)
            dve.wait_ge(v_hi[s], i + 1)
            dve.tensor_tensor(vs[:, s, :, 1], v, vs[:, s, :, 0].bitcast(F32), ALU.subtract).then_inc(v_lo[s], 1)

    def keep_low(dve, i, s, t, k):
        for g in range(NG):
            n, b = uses(i, s, g)
            dve.wait_ge(high[b], n + 1)
            if keys:
                dve.tensor_tensor(hl[b][:, 1, 0:nh], bank[b][:, 0:nh, :], hl[b][:, 0, 0:nh].bitcast(F32),
                                  ALU.subtract).then_inc(low[b], 1)
            else:
                dve.tensor_tensor(hl[b][HD:P, 0], bank[b][HD:P], hl[b][HD:P, 0].bitcast(F32),
                                  ALU.subtract).then_inc(low[b], 1)

    def normalise(dve, i, s, t, k):
        dve.wait_ge(rooted[s], i + 1)
        dve.reciprocal(r0[:, s], rt[:, s]).then_inc(inv[s], 1)
        dve.wait_ge(inv[s], i + 1)
        dve.tensor_tensor(t0[:, s], r0[:, s], r0[:, s], ALU.mult).then_inc(nwt[s], 1)
        dve.wait_ge(nwt[s], i * 4 + 1)
        dve.tensor_tensor(t1[:, s], t0[:, s], ms[:, s], ALU.mult).then_inc(nwt[s], 1)
        dve.wait_ge(nwt[s], i * 4 + 2)
        dve.tensor_scalar(t1[:, s], t1[:, s], -0.5, 1.5, ALU.mult, ALU.add).then_inc(nwt[s], 1)
        dve.wait_ge(nwt[s], i * 4 + 3)
        dve.tensor_tensor(rstd[:, s], r0[:, s], t1[:, s], ALU.mult).then_inc(nwt[s], 1)
        dve.wait_ge(nwt[s], i * 4 + 4)
        dve.tensor_tensor(xn[:, s].rearrange("p (h d) -> p h d", h=nh), x[:, s, 0:W].rearrange("p (h d) -> p h d", h=nh),
                          rstd[:, s, :, None].to_broadcast([P, nh, HD]), ALU.mult).then_inc(scaled[s], 1)
        dve.wait_ge(scaled[s], i + 1)
        dve.wait_ge(tabled[s], i + 1)
        dve.tensor_tensor(xc[:, s].rearrange("p (h d) -> p h d", h=nh), xn[:, s].rearrange("p (h d) -> p h d", h=nh),
                          turns_by[:, s, 0:1, :].to_broadcast([P, nh, HD]), ALU.mult).then_inc(cosd[s], 1)

    def rotate(dve, i, s, t, k):
        dve.wait_ge(cosd[s], i + 1)
        dve.wait_ge(sind[s], i + 1)
        dve.wait_ge(turned[NBK - 1 if NG == NBK else s * NG + NG - 1], i * 2 if NG == NBK else i)
        cos0, cos1 = (pairs_of(xc[:, s])[:, :, :, b] for b in range(2))
        sin0, sin1 = (pairs_of(xs[:, s])[:, :, :, b] for b in range(2))
        dve.tensor_tensor(xr[:, s, :, 0, 0::2], cos0, sin1, ALU.subtract).then_inc(rotated[s], 1)
        dve.tensor_tensor(xr[:, s, :, 0, 1::2], sin0, cos1, ALU.add).then_inc(rotated[s], 1)

    def turn(pe, i, s, t, k):
        pe.wait_ge(twice[s], i + 1)
        for g in range(NG):
            n, b = uses(i, s, g)
            pe.wait_ge(low[b], n)
            for r in range(nh if keys else R):
                last = pe.transpose(bank[b][:, r, :], xr[:, s, g * R + r].rearrange("p a d -> p (a d)"), ident[:])
            last.then_inc(turned[b], 1)

    def begin(sp):
        sp.dma_start(gains[:], gain.rearrange("(a n) -> a n", a=1).to_broadcast([P, HD])).then_inc(loaded, 16)

    def end(pool):
        total = sum(n for _, n in parts)
        for b in range(NBK):
            pool.wait_ge(stored[b], total * NG // NBK * 16)
        for s in range(2 if keys else 0):
            pool.wait_ge(v_stored[s], total // 2 * 16)

    def bound(eng, *hooks):
        def bind(hook):
            return lambda i, s, t, k: hook(eng, i, s, t, k) if k < len(parts) else None
        return [bind(hook) if hook else None for hook in hooks]

    return {
        "begin": begin, "end": end,
        "sp": lambda sp: bound(sp, load, None, None, None, None),
        "act": lambda act: bound(act, square, keep_high, None, double, None),
        "pool": lambda pool: bound(pool, tables, None, sines, None, store),
        "dve": lambda dve: bound(dve, mean_squares, None, normalise, rotate, keep_low),
        "pe": lambda pe: bound(pe, None, turn, None, None, None),
    }


def heads(nc, name, rope, consts, queries, keys):
    with Stage(nc, name) as st:
        ident = st.sb("ident", [P, P])
        loaded = st.sem("loaded")
        streams = [head_stream(st, tag, loaded, ident, rope, **job) for tag, job in (("q", queries), ("k", keys))]

        def hooks_of(engine, eng):
            q, k = (stream[engine](eng) for stream in streams)
            return [q[0], None, k[0], q[1], q[2], k[1], k[2], None, q[3], None, k[3], q[4], None, k[4]]

        with nc.Block() as block:
            @block.sync
            def _(sp):
                for stream in streams:
                    stream["begin"](sp)
                sp.dma_start(ident[:], consts[:, C_ID:C_ID + P]).then_inc(loaded, 16)
                skewed(sp, keys["parts"], *hooks_of("sp", sp))

            @block.scalar
            def _(act):
                skewed(act, keys["parts"], *hooks_of("act", act))

            @block.gpsimd
            def _(pool):
                pool.wait_ge(loaded, 48)
                skewed(pool, keys["parts"], *hooks_of("pool", pool))
                for stream in streams:
                    stream["end"](pool)

            @block.vector
            def _(dve):
                dve.wait_ge(loaded, 48)
                skewed(dve, keys["parts"], *hooks_of("dve", dve))

            @block.tensor
            def _(pe):
                pe.wait_ge(loaded, 48)
                skewed(pe, keys["parts"], *hooks_of("pe", pe))


def attention(nc, name, qst, kst, vst, consts, orows, ngroups, tile0, count, spans, mask=None, sink=None):
    window = mask is not None
    nk = 5 * P if window else sum(n for _, n in spans)
    nkt = nk // P
    span = min(nk, 5 * P)
    nspan = nk // span
    piece = span // 2
    ctx_col = 2 * P + SEQ
    UN = 4
    turns = count * ngroups // UN
    NB = 4
    AHEAD = min(3, nkt)
    OUT = R * HD
    with Stage(nc, name) as st:
        ident = st.sb("ident", [P, P])
        summer = st.sb("summer", [P, HD])
        ones = st.sb("ones", [P, P])
        ones_r = st.sb("ones_r", [P, P], F32R)
        nkv = UN if window else ngroups
        K = st.sb("K", [P, nkv, 2, nk], F32R)
        V = st.sb("V", [P, nkv, nkt, P], F32R)
        Q = st.sb("Q", [P, UN, R * P], F32R)
        p = st.sb("p", [P, NB, R * P])
        p_hi = st.sb("p_hi", [P, NB, R * P], F32R)
        p_lo = st.sb("p_lo", [P, NB, R * P], F32R)
        gathered = st.sb("gathered", [P, UN, R * P])
        top = st.sb("top", [P, UN, nspan, R])
        zero = st.sb("zero", [P, 1])
        zeroed = st.sem("zeroed")
        top1 = st.sb("top1", [P, UN, R]) if nspan > 1 else None
        ntop = st.sb("ntop", [P, UN, R], F32R)
        shift = st.sb("shift", [P, UN, R * P], F32R)
        osum = st.sb("osum", [P, R * P])
        rinv = st.sb("rinv", [P, UN, R])
        res = st.sb("res", [P, UN, R, HD])
        if window:
            masks = st.sb("masks", [P, NTX, 5 * P], F32R)
            masks_raw = st.sb("masks_raw", [P, NTX, 5 * P])
            eye = st.sb("eye", [P, P], F32R)
            sinks = st.sb("sinks", [P, ngroups * R])
            sinks_up = st.sb("sinks_up", [P, ngroups * R])
            nsinks_up = st.sb("nsinks_up", [P, ngroups * R])
            sd = st.sb("sd", [P, UN, R])
            se = st.sb("se", [P, UN, R])
            den = st.sb("den", [P, UN, R])
        score = st.ps("score", [P, 2, 512])
        turned = [st.ps(f"turned{b}", [P, R * P]) for b in range(NB)]
        osc = st.ps("osc", [P, R * P])
        outb = st.ps("outb", [P, 512])
        loaded, rounded, sinked, scored, topped, o_read = st.sems("loaded", "rounded", "sinked", "scored", "topped", "o_read")
        q_in, k_in, v_in, negated, ntopped, shifted, sink_d, sink_e, fin, denned, inverted, out_done, stored = (
            st.sems(*(f"{n}{u}" for u in range(UN))) for n in (
                "q_in", "k_in", "v_in", "negated", "ntopped", "shifted", "sink_d", "sink_e", "fin", "denned", "inverted",
                "out_done", "stored"))
        turned_in, expd, low, added, pv_done = (
            st.sems(*(f"{n}{b}" for b in range(NB))) for n in ("turned_in", "expd", "low", "added", "pv_done"))
        NCONST = 5 if window else 3

        def tile_of(i, u):
            return i * (UN // ngroups) + u // ngroups, u % ngroups

        def place(i, u, kt):
            step = u * nkt + kt
            return step % NB, i * (UN * nkt // NB) + step // NB

        def nth_start(i, u, r, x):
            return ((i * UN + u) * R + r) * nspan + x

        def before(eng, sems, i, u):
            if u:
                eng.wait_ge(sems[u - 1], i + 1)
            else:
                eng.wait_ge(sems[UN - 1], i)

        def plus(i, u, n):
            return (i, u + n) if u + n < UN else (i + 1, u + n - UN)

        def nothing(*a):
            pass

        due = [2 * (nkt - AHEAD) + q * 2 * nkt // (R * nspan) for q in range(R * nspan)]

        def schedule(eng, load=nothing, start=nothing, turn=nothing, keys=nothing, split=nothing, meet=nothing, copy=nothing, finish=nothing):
            def body(i, last):
                for u in range(UN):
                    def there(n):
                        return not (last and u + n >= UN)
                    if there(3):
                        load(*plus(i, u, 3))

                    def begin(half):
                        for n, shift_ in ((1, 2 * nkt), (2, 0)):
                            for q in range(R * nspan):
                                if there(n) and due[q] - shift_ == half:
                                    start(*plus(i, u, n), *divmod(q, nspan))

                    for kt in range(nkt):
                        if kt == nkt - AHEAD and there(1):
                            turn(*plus(i, u, 1))
                        begin(2 * kt)
                        if kt == nkt - 1:
                            meet(i, u, kt)
                            copy(i, u)
                        for hook, n in ((split, AHEAD - 1), (keys, AHEAD)):
                            if kt + n < nkt:
                                hook(i, u, kt + n)
                            elif there(1):
                                hook(*plus(i, u, 1), kt + n - nkt)
                        begin(2 * kt + 1)
                        if kt < nkt - 1:
                            meet(i, u, kt)
                    finish(i, u)

            for u in range(3):
                load(0, u)
            for q in range(R * nspan):
                start(0, 0, *divmod(q, nspan))
            turn(0, 0)
            for q in range(R * nspan):
                if due[q] < 2 * nkt:
                    start(0, 1, *divmod(q, nspan))
            for kt in range(AHEAD):
                keys(0, 0, kt)
            for kt in range(AHEAD - 1):
                split(0, 0, kt)
            if turns > 1:
                loop(eng, turns - 1, lambda i: body(i, False))
            body(turns - 1, True)

        with nc.Block() as block:
            @block.sync
            def _(sp):
                sp.dma_start(ident[:], consts[:, C_ID:C_ID + P]).then_inc(loaded, 16)
                sp.dma_start(summer[:], consts[:, C_SUM:C_SUM + HD]).then_inc(loaded, 16)
                sp.dma_start(ones[:], consts[0:1, C_ALL:C_ALL + P].to_broadcast([P, P])).then_inc(loaded, 16)

                def load(i, u):
                    tile, g = tile_of(i, u)
                    sp.wait_ge(out_done[u], i)
                    sp.dma_start(Q[:, u].bitcast(F32), qst[at(tile + tile0), g].rearrange("a p n -> (a p) n")
                                 ).then_inc(q_in[u], 16)
                    if window:
                        for col, n, to in ((bass.ds(tile * P, 3 * P), 3, 0), (slice(ctx_col, ctx_col + CTX), 2, 3)):
                            sp.dma_start(K[:, u, :, to * P:(to + n) * P].bitcast(F32), kst[:, :, g, col]
                                         ).then_inc(k_in[u], 16)
                            sp.dma_start(V[:, u, to:to + n].bitcast(F32), vst[col, g, :].rearrange("(t p) n -> p t n", p=P)
                                         ).then_inc(v_in[u], 16)
                    elif u < ngroups and isinstance(i, int) and i == 0:
                        to = 0
                        for col, n in spans:
                            sp.dma_start(K[:, g, :, to:to + n].bitcast(F32), kst[:, :, g, col:col + n]
                                         ).then_inc(k_in[g], 16)
                            sp.dma_start(V[:, g, to // P:(to + n) // P, :].bitcast(F32),
                                         vst[col:col + n, g, :].rearrange("(t p) n -> p t n", p=P)).then_inc(v_in[g], 16)
                            to += n

                if window:
                    sp.dma_start(masks_raw[:], mask.rearrange("i p n -> p i n")).then_inc(loaded, 16)
                    sp.dma_start(sinks[:], sink.rearrange("(a n) -> a n", a=1).to_broadcast([P, ngroups * R])
                                 ).then_inc(loaded, 16)

                def finish(i, u):
                    tile, g = tile_of(i, u)
                    sp.wait_ge(out_done[u], i + 1)
                    sp.dma_start(rows(orows, tile + tile0)[:, g * R * HD:(g + 1) * R * HD],
                                 res[:, u].rearrange("p r d -> p (r d)")).then_inc(stored[u], 16)
                schedule(sp, load=load, finish=finish)
                for u in range(UN):
                    sp.wait_ge(stored[u], turns * 16)

            @block.gpsimd
            def _(pool):
                pool.wait_ge(loaded, 16 * NCONST)
                pool.tensor_copy(ones_r[:], ones[:]).then_inc(rounded, 1)
                pool.memset(zero[:], 0.0).then_inc(zeroed, 1)
                pool.wait_ge(zeroed, 1)
                if window:
                    pool.tensor_copy(eye[:], ident[:]).then_inc(rounded, 1)
                    pool.tensor_copy(masks[:], masks_raw[:]).then_inc(rounded, 1)

                def keys(i, u, kt):
                    b, n = place(i, u, kt)
                    pool.wait_ge(expd[b], n + 1)
                    if kt == 0:
                        pool.wait_ge(fin[u], i)
                        pool.tensor_tensor(gathered[:, u], p[:, b], zero[:].to_broadcast([P, R * P]), ALU.add
                                           ).then_inc(added[b], 1)
                    else:
                        last, m = place(i, u, kt - 1)
                        pool.wait_ge(added[last], m + 1)
                        pool.tensor_tensor(gathered[:, u], gathered[:, u], p[:, b], ALU.add).then_inc(added[b], 1)
                schedule(pool, keys=keys)

            @block.scalar
            def _(act):
                def turn(i, u):
                    if window:
                        act.wait_ge(sink_d[u], i + 1)
                        act.activation(se[:, u], sd[:, u], ACT.Exp, scale=SCALE).then_inc(sink_e[u], 1)

                def keys(i, u, kt):
                    b, n = place(i, u, kt)
                    act.wait_ge(turned_in[b], n + 1)
                    act.wait_ge(pv_done[b], n)
                    act.activation(p_hi[:, b], turned[b][:], ACT.Exp, scale=SCALE)
                    act.wait_ge(low[b], n)
                    act.wait_ge(added[b], n)
                    act.activation(p[:, b], turned[b][:], ACT.Exp, scale=SCALE).then_inc(expd[b], 1)

                def copy(i, u):
                    b, n = place(i, u, nkt - 1)
                    act.wait_ge(pv_done[b], n + 1)
                    before(act, fin, i, u)
                    act.activation(osum[:], osc[:], ACT.Copy).then_inc(o_read, 1)
                schedule(act, turn=turn, keys=keys, copy=copy)

            @block.vector
            def _(dve):
                dve.wait_ge(loaded, 16 * NCONST)
                if window:
                    dve.tensor_scalar(sinks_up[:], sinks[:], 1.0 / SCALE, None, ALU.mult).then_inc(sinked, 1)
                    dve.tensor_scalar(nsinks_up[:], sinks[:], -1.0 / SCALE, None, ALU.mult).then_inc(sinked, 1)
                    dve.wait_ge(sinked, 2)

                def start(i, u, r, x):
                    dve.wait_ge(scored, nth_start(i, u, r, x) + 1)
                    dve.wait_ge(ntopped[u], i)
                    dve.tensor_reduce(top[:, u, x, r:r + 1], score[:, :, 0:piece], AXS, ALU.max).then_inc(topped, 1)

                def turn(i, u):
                    tile, g = tile_of(i, u)
                    dve.wait_ge(topped, nth_start(i, u, R, 0))
                    dve.wait_ge(out_done[u], i)
                    dve.wait_ge(shifted[u], i)
                    if window:
                        dve.scalar_tensor_tensor(ntop[:, u], top[:, u, 0], -1.0, nsinks_up[:, g * R:g * R + R], ALU.mult, ALU.min
                                                 ).then_inc(ntopped[u], 1)
                    elif nspan == 1:
                        dve.tensor_scalar(ntop[:, u], top[:, u, 0], -1.0, None, ALU.mult).then_inc(ntopped[u], 1)
                    else:
                        dve.tensor_scalar(top1[:, u], top[:, u, 1], -1.0, None, ALU.mult).then_inc(negated[u], 1)
                        dve.wait_ge(negated[u], i + 1)
                        dve.scalar_tensor_tensor(ntop[:, u], top[:, u, 0], -1.0, top1[:, u], ALU.mult, ALU.min).then_inc(ntopped[u], 1)
                    dve.wait_ge(ntopped[u], i + 1)
                    if window:
                        dve.wait_ge(sink_e[u], i)
                        dve.tensor_tensor(sd[:, u], ntop[:, u].bitcast(F32), sinks_up[:, g * R:g * R + R], ALU.add
                                          ).then_inc(sink_d[u], 1)
                    dve.tensor_tensor(shift[:, u].rearrange("p (r n) -> p r n", r=R), ident[:, None, :].to_broadcast([P, R, P]),
                                      ntop[:, u, :, None].bitcast(F32).to_broadcast([P, R, P]), ALU.mult).then_inc(shifted[u], 1)

                def split(i, u, kt):
                    b, n = place(i, u, kt)
                    dve.wait_ge(expd[b], n + 1)
                    dve.wait_ge(pv_done[b], n)
                    dve.tensor_tensor(p_lo[:, b], p[:, b], p_hi[:, b].bitcast(F32), ALU.subtract).then_inc(low[b], 1)

                def finish(i, u):
                    dve.wait_ge(fin[u], i + 1)
                    sums = outb[:, OUT:OUT + R]
                    if window:
                        dve.wait_ge(sink_e[u], i + 1)
                        dve.tensor_tensor(den[:, u], sums, se[:, u], ALU.add).then_inc(denned[u], 1)
                        dve.wait_ge(denned[u], i + 1)
                        sums = den[:, u]
                    dve.reciprocal(rinv[:, u], sums).then_inc(inverted[u], 1)
                    dve.wait_ge(inverted[u], i + 1)
                    dve.wait_ge(stored[u], i * 16)
                    dve.tensor_tensor(res[:, u], outb[:, 0:OUT].rearrange("p (r d) -> p r d", r=R),
                                      rinv[:, u, :, None].to_broadcast([P, R, HD]), ALU.mult).then_inc(out_done[u], 1)
                schedule(dve, start=start, turn=turn, split=split, finish=finish)

            @block.tensor
            def _(pe):
                pe.wait_ge(loaded, 16 * NCONST)
                pe.wait_ge(rounded, 3 if window else 1)

                def start(i, u, r, x):
                    tile, g = tile_of(i, u)
                    kv = u if window else g
                    if r == 0 and x == 0:
                        pe.wait_ge(q_in[u], i * 16 + 16)
                        pe.wait_ge(k_in[kv], i * 32 + 32 if window else 16 * len(spans))
                    pe.wait_ge(topped, nth_start(i, u, r, x))
                    for bk in range(2):
                        off = x * span + bk * piece
                        masked = min(piece, 3 * P - off) if window else 0
                        last = pe.matmul(score[:, bk, 0:piece], Q[:, u, r * P:(r + 1) * P], K[:, kv, 0, off:off + piece],
                                         start=True, stop=not masked)
                        if masked:
                            last = pe.matmul(score[:, bk, 0:masked], eye[:],
                                             masks[:, at(tile), off:off + masked].rearrange("p a n -> p (a n)"),
                                             start=False, stop=True)
                    last.then_inc(scored, 1)

                def keys(i, u, kt):
                    tile, g = tile_of(i, u)
                    kv = u if window else g
                    b, n = place(i, u, kt)
                    if kt == 0:
                        pe.wait_ge(shifted[u], i + 1)
                    pe.wait_ge(expd[b], n)
                    cols = slice(kt * P, (kt + 1) * P)
                    pe.matmul(turned[b][:], K[:, kv, 0, cols], Q[:, u], start=True, stop=False)
                    pe.matmul(turned[b][:], K[:, kv, 1, cols], Q[:, u], start=False, stop=False)
                    if window and kt in (0, 2):
                        pe.matmul(turned[b][:].rearrange("p (r n) -> p r n", r=R), eye[:],
                                  masks[:, at(tile), (3 + kt // 2) * P:(4 + kt // 2) * P].to_broadcast([P, R, P]), start=False, stop=False)
                    pe.matmul(turned[b][:], ones_r[:], shift[:, u], start=False, stop=True).then_inc(turned_in[b], 1)

                def meet(i, u, kt):
                    tile, g = tile_of(i, u)
                    kv = u if window else g
                    b, n = place(i, u, kt)
                    if kt == 0:
                        pe.wait_ge(v_in[kv], i * 32 + 32 if window else 16 * len(spans))
                        pe.wait_ge(o_read, i * UN + u)
                    pe.wait_ge(low[b], n + 1)
                    pe.matmul(osc[:], V[:, kv, kt, :], p_hi[:, b], start=(kt == 0), stop=False)
                    pe.matmul(osc[:], V[:, kv, kt, :], p_lo[:, b], start=False, stop=(kt == nkt - 1)).then_inc(pv_done[b], 1)

                def finish(i, u):
                    pe.wait_ge(o_read, i * UN + u + 1)
                    b, n = place(i, u, nkt - 1)
                    pe.wait_ge(added[b], n + 1)
                    before(pe, out_done, i, u)
                    for r in range(R):
                        pe.matmul(outb[:, r * HD:(r + 1) * HD], osum[:, r * P:(r + 1) * P], summer[:], start=True, stop=True)
                    for r in range(R):
                        last = pe.matmul(outb[:, OUT + r:OUT + r + 1], gathered[:, u, r * P:(r + 1) * P], ones[:, 0:1],
                                         start=True, stop=True)
                    last.then_inc(fin[u], 1)
                schedule(pe, start=start, keys=keys, meet=meet, finish=finish)


def gated(nc, name, orows, gates, parts, consts, hi, lo, rwkv=None):
    nh = 2 * BW // HD
    OW = BW if rwkv else D
    with Stage(nc, name) as st:
        ident = st.sb("ident", [P, P])
        o = st.sb("o", [P, 2, D])
        ga = st.sb("ga", [P, 2, D])
        sg = st.sb("sg", [P, 2, D])
        prod = st.sb("prod", [P, 2, D])
        if rwkv:
            ydir, vtok, bonus, gn_w, gn_b = rwkv
            sel = st.sb("sel", [P, PAIRS, 8])
            gw = st.sb("gw", [P, BW])
            gb = st.sb("gb", [P, BW])
            eps = st.sb("eps", [P, 1])
            y = st.sb("y", [P, 2, 2 * BW])
            v = st.sb("v", [P, 2, BW])
            bo = st.sb("bo", [P, 2, PAIRS, P])
            sq = st.sb("sq", [P, 2, 2 * BW])
            mean, var, rt, rstd = (st.sb(n, [P, 2, nh]) for n in ("mean", "var", "rt", "rstd"))
            bsum = st.sb("bsum", [P, 2, 8])
            bank_b = st.ps("bank_b", [P, 2, 8])
        tr = [[st.ps(f"tr{s}{b}", [P, 4, P]) for b in range(2)] for s in range(2)]
        loaded, ready = st.sems("loaded", "ready")
        (o_in, y_in, sig, silu, multiplied, turned, high, low, bon_in, bon_read, bonused, v_done, centred, squared,
         vared, rooted, steps, weighted) = (
            st.sems(f"{n}0", f"{n}1") for n in (
                "o_in", "y_in", "sig", "silu", "multiplied", "turned", "high", "low", "bon_in", "bon_read", "bonused",
                "v_done", "centred", "squared", "vared", "rooted", "steps", "weighted"))
        NCONST = 4 if rwkv else 1
        STEPS = 6

        def heads_of(t, n):
            return t.rearrange("p (h d) -> p h d", h=n)

        with nc.Block() as block:
            @block.sync
            def _(sp):
                sp.dma_start(ident[:], consts[:, C_ID:C_ID + P]).then_inc(loaded, 16)
                if rwkv:
                    sp.dma_start(sel[:].rearrange("p a b -> p (a b)"), consts[:, C_SEL:C_ALL]).then_inc(loaded, 16)
                    sp.dma_start(gw[:], gn_w.rearrange("(a n) -> a n", a=1).to_broadcast([P, BW])).then_inc(loaded, 16)
                    sp.dma_start(gb[:], gn_b.rearrange("(a n) -> a n", a=1).to_broadcast([P, BW])).then_inc(loaded, 16)

                def load(i, s, t, k):
                    sp.wait_ge(multiplied[s], i)
                    if rwkv:
                        for d in range(2):
                            sp.dma_start(y[:, s, d * BW:(d + 1) * BW], rows(ydir[d], t)).then_inc(y_in[s], 16)
                        sp.dma_start(v[:, s], rows(vtok, t)).then_inc(y_in[s], 16)
                        sp.dma_start(bo[:, s], bonus[:, :, bass.ds(t * P, P)].rearrange("q p n -> p q n")).then_inc(y_in[s], 16)
                    sp.dma_start(ga[:, s], rows(gates, t)).then_inc(o_in[s], 16)
                    sp.dma_start(o[:, s, 0:OW], rows(orows, t)).then_inc(o_in[s], 16)
                skewed(sp, parts, load, None)

            @block.scalar
            def _(act):
                def square(i, s, t, k):
                    act.wait_ge(bon_in[s], i + 1)
                    act.wait_ge(bonused[s], i)
                    act.activation(bsum[:, s], bank_b[:, s], ACT.Copy).then_inc(bon_read[s], 1)
                    act.wait_ge(centred[s], i + 1)
                    act.wait_ge(vared[s], i)
                    act.activation(sq[:, s], y[:, s], ACT.Square).then_inc(squared[s], 1)

                def root(i, s, t, k):
                    if rwkv:
                        act.wait_ge(vared[s], i + 1)
                        act.wait_ge(steps[s], i * STEPS)
                        act.activation(rt[:, s], var[:, s], ACT.Sqrt, scale=1.0 / HD, bias=eps[:]).then_inc(rooted[s], 1)
                    act.wait_ge(o_in[s], i * 32 + 32)
                    act.wait_ge(silu[s], i)
                    act.activation(sg[:, s], ga[:, s], ACT.Sigmoid).then_inc(sig[s], 1)

                def keep_high(i, s, t, k):
                    act.wait_ge(turned[s], i + 1)
                    for b in range(2):
                        last = act.activation(hi[:, 4 * b:4 * b + 4, bass.ds(t * P, P)], tr[s][b][:], ACT.Copy)
                    last.then_inc(high[s], 1)
                if rwkv:
                    act.wait_ge(ready, 2)
                skewed(act, parts, square if rwkv else None, None, root, keep_high)

            @block.gpsimd
            def _(pool):
                if rwkv:
                    pool.memset(eps[:], GN_EPS).then_inc(ready, 1)
                    pool.wait_ge(loaded, 16 * NCONST)
                    pool.tensor_tensor(gb[:], gb[:], gb[:], ALU.add).then_inc(ready, 1)
                    pool.wait_ge(ready, 2)

                def bonus_of(i, s, t, k):
                    pool.wait_ge(y_in[s], i * 64 + 64)
                    pool.wait_ge(bon_read[s], i + 1)
                    pool.tensor_tensor(heads_of(v[:, s], 8), heads_of(v[:, s], 8),
                                       bsum[:, s, :, None].to_broadcast([P, 8, HD]), ALU.mult).then_inc(bonused[s], 1)
                    pool.wait_ge(bonused[s], i + 1)
                    pool.tensor_tensor(v[:, s], v[:, s], gb[:], ALU.add).then_inc(v_done[s], 1)

                def silu_of(i, s, t, k):
                    pool.wait_ge(sig[s], i + 1)
                    pool.wait_ge(turned[s], i)
                    pool.tensor_tensor(prod[:, s], ga[:, s], sg[:, s], ALU.mult).then_inc(silu[s], 1)
                skewed(pool, parts, bonus_of if rwkv else None, None, silu_of, None)

            @block.vector
            def _(dve):
                dve.wait_ge(loaded, 16 * NCONST)

                def chain(i, s, n, ins):
                    ins.then_inc(steps[s], 1)
                    dve.wait_ge(steps[s], i * STEPS + n)

                def centre(i, s, t, k):
                    yh = heads_of(y[:, s], nh)
                    dve.wait_ge(y_in[s], i * 64 + 64)
                    chain(i, s, 1, dve.tensor_reduce(mean[:, s], yh, AX, ALU.add))
                    chain(i, s, 2, dve.tensor_scalar(mean[:, s], mean[:, s], 1.0 / HD, None, ALU.mult))
                    dve.tensor_tensor(yh, yh, mean[:, s, :, None].to_broadcast([P, nh, HD]), ALU.subtract
                                      ).then_inc(centred[s], 1)

                def multiply(i, s, t, k):
                    if rwkv:
                        dve.wait_ge(steps[s], i * STEPS + STEPS)
                    dve.wait_ge(o_in[s], i * 32 + 32)
                    dve.wait_ge(silu[s], i + 1)
                    dve.tensor_tensor(prod[:, s], prod[:, s], o[:, s], ALU.mult).then_inc(multiplied[s], 1)

                def readout(i, s, t, k):
                    yh = heads_of(y[:, s], nh)
                    y0 = y[:, s, 0:BW]
                    dve.wait_ge(squared[s], i + 1)
                    dve.wait_ge(rooted[s], i)
                    dve.tensor_reduce(var[:, s], heads_of(sq[:, s], nh), AX, ALU.add).then_inc(vared[s], 1)
                    dve.wait_ge(rooted[s], i + 1)
                    chain(i, s, 3, dve.reciprocal(rstd[:, s], rt[:, s]))
                    dve.wait_ge(centred[s], i + 1)
                    chain(i, s, 4, dve.tensor_tensor(yh, yh, rstd[:, s, :, None].to_broadcast([P, nh, HD]), ALU.mult))
                    chain(i, s, 5, dve.tensor_tensor(y0, y0, y[:, s, BW:], ALU.add))
                    dve.tensor_tensor(y0, y0, gw[:], ALU.mult).then_inc(weighted[s], 1)
                    dve.wait_ge(weighted[s], i + 1)
                    dve.wait_ge(v_done[s], i + 1)
                    chain(i, s, 6, dve.tensor_tensor(o[:, s, BW:], y0, v[:, s], ALU.add))

                def keep_low(i, s, t, k):
                    dve.wait_ge(high[s], i + 1)
                    for b in range(2):
                        part = (slice(None), slice(4 * b, 4 * b + 4), bass.ds(t * P, P))
                        last = dve.tensor_tensor(lo[part], tr[s][b][:], hi[part].bitcast(F32), ALU.subtract)
                    last.then_inc(low[s], 1)
                skewed(dve, parts, centre if rwkv else None, multiply, readout if rwkv else None, keep_low)

            @block.tensor
            def _(pe):
                pe.wait_ge(loaded, 16 * NCONST)

                def bonus_sums(i, s, t, k):
                    pe.wait_ge(y_in[s], i * 64 + 64)
                    pe.wait_ge(bon_read[1 - s], i + s)
                    for q in range(PAIRS):
                        last = pe.matmul(bank_b[:, s], bo[:, s, q, :], sel[:, q, :], start=(q == 0), stop=(q == PAIRS - 1))
                    last.then_inc(bon_in[s], 1)

                def turn(i, s, t, k):
                    pe.wait_ge(multiplied[s], i + 1)
                    pe.wait_ge(low[s], i)
                    for k in range(KC):
                        last = pe.transpose(tr[s][k // 4][:, k % 4, :], prod[:, s, k * P:(k + 1) * P], ident[:])
                    last.then_inc(turned[s], 1)
                skewed(pe, parts, bonus_sums if rwkv else None, turn)


def residual(nc, name, l, yrows, src_x, src_ctx, g_post, mod, dst_x, dst_ctx):
    with Stage(nc, name) as st:
        gt = st.sb("gt", [P, 2, D])
        gp = st.sb("gp", [P, D])
        eps = st.sb("eps", [P, 1])
        y = st.sb("y", [P, NT, D])
        x = st.sb("x", [P, NT, D])
        sq = st.sb("sq", [P, D])
        ss, rt, rstd = (st.sb(n, [P, 2, 1]) for n in ("ss", "rt", "rstd"))
        loaded, gained, ready = st.sems("loaded", "gained", "ready")
        PARTS = [(0, 2), (2, 2), (4, NTX - 4)] + ([] if dst_ctx is None else [(NTX, NTC)])
        y_in = st.sems(*(f"y_in{k}" for k in range(len(PARTS))))
        squared, rooted, inverted, scaled, added, stored = (
            st.sems(f"{n}0", f"{n}1") for n in (
                "squared", "rooted", "inverted", "scaled", "added", "stored"))

        def side(k):
            return (src_ctx, dst_ctx, NTX, 1) if PARTS[k][0] >= NTX else (src_x, dst_x, 0, 0)

        def tile_of(buffer, t):
            return buffer[:, at(t)].rearrange("p a n -> p (a n)")

        with nc.Block() as block:
            @block.sync
            def _(sp):
                sp.dma_start(gp[:], g_post[l:l + 1, :].to_broadcast([P, D])).then_inc(loaded, 16)
                for r in range(2):
                    sp.dma_start(gt[:, r], mod[l, r:r + 1, 2 * D:3 * D].to_broadcast([P, D])).then_inc(loaded, 16)

                for k, (t0, n) in enumerate(PARTS):
                    src, _, base, _ = side(k)
                    for to, what, at_row in ((y, yrows, t0), (x, src, t0 - base)):
                        sp.dma_start(to[:, t0:t0 + n], what[at_row * P:(at_row + n) * P].rearrange("(t p) n -> p t n", p=P)
                                     ).then_inc(y_in[k], 16)

            @block.scalar
            def _(act):
                act.wait_ge(ready, 1)

                def first(i, s, t, k):
                    act.wait_ge(y_in[k], 32)
                    act.wait_ge(rooted[s], i)
                    act.activation(sq[:], tile_of(y, t), ACT.Square, accum_out=ss[:, s]).then_inc(squared[s], 1)
                    act.wait_ge(squared[s], i + 1)
                    act.wait_ge(inverted[s], i)
                    act.activation(rt[:, s], ss[:, s], ACT.Sqrt, scale=1.0 / D, bias=eps[:]).then_inc(rooted[s], 1)

                def second(i, s, t, k):
                    act.wait_ge(added[s], i + 1)
                    act.dma_start(rows(side(k)[1], t - side(k)[2]), tile_of(y, t)).then_inc(stored[s], 16)
                skewed(act, PARTS, first, second)
                for s in range(2):
                    act.wait_ge(stored[s], sum(n for _, n in PARTS) // 2 * 16)

            @block.gpsimd
            def _(pool):
                pool.memset(eps[:], EPS).then_inc(ready, 1)

            @block.vector
            def _(dve):
                dve.wait_ge(loaded, 48)
                for r in range(2):
                    dve.tensor_tensor(gt[:, r], gt[:, r], gp[:], ALU.mult).then_inc(gained, 1)
                dve.wait_ge(gained, 2)

                def first(i, s, t, k):
                    dve.wait_ge(rooted[s], i + 1)
                    dve.wait_ge(scaled[s], i)
                    dve.reciprocal(rstd[:, s], rt[:, s]).then_inc(inverted[s], 1)
                    dve.wait_ge(inverted[s], i + 1)
                    dve.scalar_tensor_tensor(tile_of(y, t), tile_of(y, t), rstd[:, s], gt[:, side(k)[3]], ALU.mult, ALU.mult
                                             ).then_inc(scaled[s], 1)

                def second(i, s, t, k):
                    dve.wait_ge(scaled[s], i + 1)
                    dve.tensor_tensor(tile_of(y, t), tile_of(y, t), tile_of(x, t), ALU.add).then_inc(added[s], 1)
                skewed(dve, PARTS, first, second)


def hybrid_layers(nc, a, out):
    def scratch(name, *shape):
        return nc.dram_tensor(name, shape, F32).ap()

    mod = scratch("mod", 2, 2, 3 * D)
    QC, QKV, KV1 = AH * HD, (AH + 2 * AKV) * HD, 2 * CKV * HD
    GA = QKV + BPROJ
    qkv0, gates0 = scratch("qkv0", TOK, QKV), scratch("gates0", TOK, D)
    rkvz = scratch("rkvz", NFC, P, TOK)
    streams = scratch("streams", 2, PAIRS, P, NT, 4 * P)
    wcs, vtok = scratch("wcs", 2, PAIRS, P, 2, NT), scratch("vtok", TOK, BW)
    bonus, ydir = scratch("bonus", PAIRS, P, TOK), scratch("ydir", 2, TOK, BW)
    qst0, kst0, vst0 = scratch("qst0", NT, AKV, P, R * P), scratch("kst0", P, 2, AKV, TOK), scratch("vst0", TOK, AKV, P)
    oa, y0 = scratch("oa", TOK, BW), scratch("y0", TOK, D)
    x1, ctx1 = scratch("x1", SEQ, D), scratch("ctx1", CTX, D)
    q1, kv1, gates1 = scratch("q1", SEQ, CH * HD), scratch("kv1", TOK, 2 * CKV * HD), scratch("gates1", SEQ, D)
    PT = TOK + 2 * P
    qst1, kst1, vst1 = scratch("qst1", NTX, CKV, P, R * P), scratch("kst1", P, 2, CKV, PT), scratch("vst1", PT, CKV, P)
    oc, y1 = scratch("oc", SEQ, D), scratch("y1", SEQ, D)
    x, ctx, consts = a["x"][0], a["ctx"][0], a["consts"]
    w0, w1 = a["w_in_even"][0], a["w_in_odd"][0]

    modulation(nc, a["c"], a["c_ctx"], a["w_mod"], a["b_mod"], mod, kst1, vst1)

    def halves():
        return (nc.sbuf_tensor(f"{n}{nc.next_id()}", [P, KC, TOK], F32R) for n in ("hi", "lo"))

    h, lw = halves()
    with h as hi, lw as lo:
        normed_input(nc, 0, x, ctx, a["g_pre"], mod, consts, hi, lo)
        shifted_streams(nc, w0, a["mu_b"][0], hi, lo, rkvz)
        project(nc, "in0", w0, ((GA, D // BLK, NT, gates0), (0, QKV // BLK, NT, qkv0)), hi, lo)
    decayed_streams(nc, rkvz, a["w0_b"][0], a["w2_b"][0], a["a0_b"][0], a["a2_b"][0], a["kk_b"][0], a["ka_b"][0],
                    a["rk_b"][0].rearrange("h d -> (h d)"), consts, streams, wcs, vtok, bonus)
    chunked_scan(nc, streams, wcs, vtok, consts, ydir)
    both = ((0, NTX), (NTX, NTC))
    heads(nc, "heads0", a["rope"], consts,
          dict(parts=both, src=qkv0[:, 0:QC], nh=AH, gain=a["qn_a"][0], qst=qst0),
          dict(parts=both, src=qkv0[:, QC:QKV], nh=AKV, gain=a["kn_a"][0], kst=kst0, vst=vst0))
    attention(nc, "dense", qst0, kst0, vst0, consts, oa, AKV, 0, NTX, ((0, TOK),))
    attention(nc, "context", qst0, kst0, vst0, consts, oa, AKV, NTX, NTC, ((SEQ, CTX),))
    h, lw = halves()
    with h as hi, lw as lo:
        gated(nc, "gate0", oa, gates0, both, consts, hi, lo,
              (ydir, vtok, bonus, a["gn_w_b"][0], a["gn_b_b"][0]))
        project(nc, "out0", a["w_out_even"][0], ((0, D // BLK, NT, y0),), hi, lo)
    residual(nc, "res0", 0, y0, x, ctx, a["g_post"], mod, x1, ctx1)
    h, lw = halves()
    with h as hi, lw as lo:
        normed_input(nc, 1, x1, ctx1, a["g_pre"], mod, consts, hi, lo)
        project(nc, "in1", w1, ((0, D // BLK, NTX, q1), (D + KV1, D // BLK, NTX, gates1), (D, KV1 // BLK, NT, kv1)), hi, lo)
    heads(nc, "heads1", a["rope"], consts,
          dict(parts=((0, NTX),), src=q1, nh=CH, gain=a["qn_c"][0], qst=qst1),
          dict(parts=both, src=kv1, nh=CKV, gain=a["kn_c"][0], kst=kst1, vst=vst1, pad=P))
    attention(nc, "window", qst1, kst1, vst1, consts, oc, CKV, 0, NTX, None, a["win"], a["sink_c"][0])
    h, lw = halves()
    with h as hi, lw as lo:
        gated(nc, "gate1", oc, gates1, ((0, NTX),), consts, hi, lo)
        project(nc, "out1", a["w_out_odd"][0], ((0, D // BLK, NTX, y1),), hi, lo)
    residual(nc, "res1", 1, y1, x1, None, a["g_post"], mod, out[0], None)


INPUTS = ("x", "c", "ctx", "c_ctx", "w_mod", "b_mod", "g_pre", "g_post", "w_in_even", "w_out_even", "qn_a", "kn_a",
          "mu_b", "w0_b", "w2_b", "a0_b", "a2_b", "kk_b", "ka_b", "rk_b", "gn_w_b", "gn_b_b",
          "w_in_odd", "w_out_odd", "qn_c", "kn_c", "sink_c")


def kernel(**inputs):
    import numpy as _np
    import concourse.bacc as _bacc
    from concourse import mybir as _mybir
    from concourse.bass_utils import run_bass_kernel_spmd as _run

    nc = _bacc.Bacc("TRN2", target_bir_lowering=False, num_devices=1)
    arrays = {name: _np.ascontiguousarray(inputs[name]) for name in INPUTS}
    arrays["consts"], arrays["win"], arrays["rope"] = constant_tables()
    feeds, args = {}, {}
    for name, v in arrays.items():
        feeds[f"in_{name}"] = v
        args[name] = nc.dram_tensor(f"in_{name}", v.shape, _mybir.dt.from_np(v.dtype), kind="ExternalInput").ap()
    out = nc.dram_tensor("out", (1, SEQ, D), F32, kind="ExternalOutput").ap()
    hybrid_layers(nc, args, out)
    r = _run(nc, [feeds], core_ids=[0])
    return r.results[0]["out"]
```
